# Optimizing a Trainium2 kernel written in Bass

```python
import math
import jax, jax.numpy as jnp
from jax import lax
import numpy as np
import functools

D_MODEL = 1024
BATCH = 1
SEQ = 256
DEPTH = 2

ATTN_HEADS = 8
ATTN_KV_HEADS = 2
ATTN_HEAD_DIM = D_MODEL // ATTN_HEADS
ATTN_WIDTH = ATTN_HEADS * ATTN_HEAD_DIM
ATTN_KV_WIDTH = ATTN_KV_HEADS * ATTN_HEAD_DIM
ATTN_ROT_DIM = ATTN_HEAD_DIM // 4
IDX_HEADS = 8
IDX_DIM = 64
IDX_ROT_DIM = IDX_DIM // 4
INDEX_TOPK = 256
Q_BLOCK = 128
ROPE_THETA = 500000.0
GDN_HEADS = 8
GDN_DK = 128
GDN_DV = 128
GDN_QK_WIDTH = GDN_HEADS * GDN_DK
GDN_WIDTH = GDN_HEADS * GDN_DV
GDN_QKV_WIDTH = 2 * GDN_QK_WIDTH + GDN_WIDTH
CONV_K = 4
CHUNK = 64
N_BRANCH = 2
NORM_EPS = 1e-6

IN_SPLITS = [
    ATTN_WIDTH,
    ATTN_KV_WIDTH,
    ATTN_KV_WIDTH,
    ATTN_WIDTH,
    IDX_HEADS * IDX_DIM,
    IDX_DIM,
    IDX_HEADS,
    GDN_QKV_WIDTH,
    GDN_WIDTH,
    GDN_HEADS,
    GDN_HEADS,
    N_BRANCH * D_MODEL,
]
IN_COLS = sum(IN_SPLITS)
IN_SPLIT_IDX = [sum(IN_SPLITS[:i + 1]) for i in range(len(IN_SPLITS) - 1)]


def rms_norm(x, gain):
    xf = x.astype(jnp.float32)
    y = xf * lax.rsqrt(jnp.mean(xf * xf, axis=-1, keepdims=True) + NORM_EPS)
    return (y * gain.astype(jnp.float32)).astype(x.dtype)

def l2_normalize(x):
    xf = x.astype(jnp.float32)
    return xf * lax.rsqrt(jnp.sum(xf * xf, axis=-1, keepdims=True) + NORM_EPS)

def rope_tables(positions, rot_dim):
    inv_freq = ROPE_THETA ** (-jnp.arange(0, rot_dim, 2, dtype=jnp.float32) / rot_dim)
    ang = positions.astype(jnp.float32)[..., None] * inv_freq
    return jnp.cos(ang)[:, :, None, :], jnp.sin(ang)[:, :, None, :]

def apply_partial_rope(x, cos, sin):
    half = cos.shape[-1]
    rot = 2 * half
    x1, x2, xp = x[..., :half], x[..., half:rot], x[..., rot:]
    c, s = cos.astype(x.dtype), sin.astype(x.dtype)
    return jnp.concatenate([x1 * c - x2 * s, x2 * c + x1 * s, xp], axis=-1)

def dsa_attention(q, k, v, q_idx, k_idx, w_idx):
    B, S = q.shape[0], q.shape[1]
    topk = min(INDEX_TOPK, S // 4)
    nb = S // Q_BLOCK
    group = ATTN_HEADS // ATTN_KV_HEADS
    scale = ATTN_HEAD_DIM ** -0.5
    key_pos = jnp.arange(S, dtype=jnp.int32)

    def blocks(t):
        return t.reshape(B, nb, Q_BLOCK, *t.shape[2:]).swapaxes(0, 1)

    def one_block(args):
        qb, qib, wb, tb = args
        raw = jnp.einsum('bqhd,bsd->bqhs', qib, k_idx)
        iscore = jnp.einsum('bqhs,bqh->bqs', jax.nn.relu(raw), wb).astype(jnp.float32)
        causal = key_pos[None, :] <= tb[:, None]
        iscore = jnp.where(causal[None], iscore, -jnp.inf)
        _, sel = lax.top_k(iscore, topk)
        valid = sel <= tb[None, :, None]
        k_sel = jax.vmap(lambda kb, ib: kb[ib])(k, sel)
        v_sel = jax.vmap(lambda vb, ib: vb[ib])(v, sel)
        qg = qb.reshape(B, Q_BLOCK, ATTN_KV_HEADS, group, ATTN_HEAD_DIM)
        logits = jnp.einsum('bqhgd,bqkhd->bqhgk', qg, k_sel).astype(jnp.float32) * scale
        logits = jnp.where(valid[:, :, None, None, :], logits, -jnp.inf)
        p = jax.nn.softmax(logits, axis=-1).astype(v.dtype)
        o = jnp.einsum('bqhgk,bqkhd->bqhgd', p, v_sel)
        return o.reshape(B, Q_BLOCK, ATTN_WIDTH)

    out = lax.map(one_block, (blocks(q), blocks(q_idx), blocks(w_idx),
                              key_pos.reshape(nb, Q_BLOCK)))
    return out.swapaxes(0, 1).reshape(B, S, ATTN_WIDTH)

def causal_depthwise_conv(x, w):
    C = x.shape[-1]
    return lax.conv_general_dilated(
        x, w[:, None, :].astype(x.dtype), window_strides=(1,),
        padding=[(CONV_K - 1, 0)], dimension_numbers=('NWC', 'WIO', 'NWC'),
        feature_group_count=C)

def chunked_gated_delta_rule(q, k, v, beta, g):
    B, S, H, dk = q.shape
    dv = v.shape[-1]
    nc = S // CHUNK

    def c4(t):
        return t.reshape(B, nc, CHUNK, H, t.shape[-1]).transpose(0, 3, 1, 2, 4)

    def c3(t):
        return t.reshape(B, nc, CHUNK, H).transpose(0, 3, 1, 2)

    q, k, v = c4(q) * (dk ** -0.5), c4(k), c4(v)
    beta, gc = c3(beta), jnp.cumsum(c3(g), axis=-1)
    incl = jnp.tril(jnp.ones((CHUNK, CHUNK), dtype=bool))
    strict = jnp.tril(jnp.ones((CHUNK, CHUNK), dtype=bool), k=-1)
    decay = jnp.exp(jnp.where(incl, gc[..., :, None] - gc[..., None, :], -jnp.inf))
    kb = k * beta[..., None]
    lower = jnp.where(strict, jnp.einsum('bhnid,bhnjd->bhnij', kb, k) * decay, 0.0)
    tmat = jnp.eye(CHUNK, dtype=jnp.float32) + lower
    u = lax.linalg.triangular_solve(tmat, v * beta[..., None], left_side=True,
                                    lower=True, unit_diagonal=True)
    w = lax.linalg.triangular_solve(tmat, kb * jnp.exp(gc)[..., None], left_side=True,
                                    lower=True, unit_diagonal=True)
    qk = jnp.einsum('bhnid,bhnjd->bhnij', q, k) * decay
    q_dec = q * jnp.exp(gc)[..., None]
    k_dec = k * jnp.exp(gc[..., -1:] - gc)[..., None]
    g_tot = jnp.exp(gc[..., -1])
    xs = (jnp.moveaxis(qk, 2, 0), jnp.moveaxis(q_dec, 2, 0), jnp.moveaxis(k_dec, 2, 0),
          jnp.moveaxis(u, 2, 0), jnp.moveaxis(w, 2, 0), jnp.moveaxis(g_tot, 2, 0))

    def step(state, xc):
        qk_c, qd_c, kd_c, u_c, w_c, gt_c = xc
        v_new = u_c - jnp.einsum('bhcd,bhde->bhce', w_c, state)
        o_c = (jnp.einsum('bhcd,bhde->bhce', qd_c, state)
               + jnp.einsum('bhij,bhje->bhie', qk_c, v_new))
        state = state * gt_c[..., None, None] + jnp.einsum('bhcd,bhce->bhde', kd_c, v_new)
        return state, o_c

    state0 = jnp.zeros((B, H, dk, dv), dtype=jnp.float32)
    _, o = lax.scan(step, state0, xs)
    return o.transpose(1, 0, 3, 2, 4).reshape(B, S, H, dv)

def first_inputs(seed: int = 0) -> dict:
    key = jax.random.key(seed)
    ks = jax.random.split(key, 12)
    x = jax.random.normal(ks[0], (BATCH, SEQ, D_MODEL), jnp.float32)
    positions = jnp.broadcast_to(jnp.arange(SEQ, dtype=jnp.int32), (BATCH, SEQ))
    norm_gain = 1.0 + 0.02 * jax.random.normal(ks[1], (DEPTH, D_MODEL), jnp.float32)
    w_in = jax.random.normal(ks[2], (DEPTH, D_MODEL, IN_COLS), jnp.float32) * D_MODEL ** -0.5
    conv_w = jax.random.normal(ks[3], (DEPTH, CONV_K, GDN_QKV_WIDTH), jnp.float32) * CONV_K ** -0.5
    a_log = jnp.log(jax.random.uniform(ks[4], (DEPTH, GDN_HEADS), jnp.float32, 1.0, 16.0))
    dt = jnp.exp(jax.random.uniform(ks[5], (DEPTH, GDN_HEADS), jnp.float32,
                                    math.log(1e-3), math.log(1e-1)))
    dt_bias = dt + jnp.log(-jnp.expm1(-dt))
    gdn_norm_gain = 1.0 + 0.02 * jax.random.normal(ks[6], (DEPTH, GDN_DV), jnp.float32)
    idx_k_gain = 1.0 + 0.02 * jax.random.normal(ks[7], (DEPTH, IDX_DIM), jnp.float32)
    w_out = jax.random.normal(ks[8], (DEPTH, D_MODEL, D_MODEL), jnp.float32) * D_MODEL ** -0.5
    final_gain = 1.0 + 0.02 * jax.random.normal(ks[9], (D_MODEL,), jnp.float32)
    return {"x": x, "positions": positions, "norm_gain": norm_gain, "w_in": w_in,
            "conv_w": conv_w, "a_log": a_log, "dt_bias": dt_bias,
            "gdn_norm_gain": gdn_norm_gain, "idx_k_gain": idx_k_gain,
            "w_out": w_out, "final_gain": final_gain}

def first_block(x, positions, norm_gain, w_in, conv_w, a_log, dt_bias, gdn_norm_gain,
              idx_k_gain, w_out, final_gain):
    B, S = x.shape[0], x.shape[1]
    cos_a, sin_a = rope_tables(positions, ATTN_ROT_DIM)
    cos_i, sin_i = rope_tables(positions, IDX_ROT_DIM)
    idx_scale = IDX_HEADS ** -0.5 * IDX_DIM ** -0.5
    for layer in range(DEPTH):
        h = rms_norm(x, norm_gain[layer])
        proj = h @ w_in[layer]
        (q_a, k_a, v_a, z_a, q_i, k_i, w_i, qkv_b, z_b, beta_l, a_l, gate_l) = jnp.split(
            proj, IN_SPLIT_IDX, axis=-1)

        q_a = apply_partial_rope(q_a.reshape(B, S, ATTN_HEADS, ATTN_HEAD_DIM), cos_a, sin_a)
        k_a = apply_partial_rope(k_a.reshape(B, S, ATTN_KV_HEADS, ATTN_HEAD_DIM), cos_a, sin_a)
        v_a = v_a.reshape(B, S, ATTN_KV_HEADS, ATTN_HEAD_DIM)
        q_i = apply_partial_rope(q_i.reshape(B, S, IDX_HEADS, IDX_DIM), cos_i, sin_i)
        k_i = apply_partial_rope(rms_norm(k_i, idx_k_gain[layer])[:, :, None, :],
                                 cos_i, sin_i)[:, :, 0, :]
        w_i = w_i * idx_scale
        y_a = dsa_attention(q_a, k_a, v_a, q_i, k_i, w_i) * jax.nn.silu(z_a)

        qkv_b = jax.nn.silu(causal_depthwise_conv(qkv_b, conv_w[layer]))
        q_b, k_b, v_b = jnp.split(qkv_b, [GDN_QK_WIDTH, 2 * GDN_QK_WIDTH], axis=-1)
        q_b = l2_normalize(q_b.reshape(B, S, GDN_HEADS, GDN_DK))
        k_b = l2_normalize(k_b.reshape(B, S, GDN_HEADS, GDN_DK))
        v_b = v_b.reshape(B, S, GDN_HEADS, GDN_DV).astype(jnp.float32)
        beta = jax.nn.sigmoid(beta_l.astype(jnp.float32))
        g = -jnp.exp(a_log[layer].astype(jnp.float32)) * jax.nn.softplus(
            a_l.astype(jnp.float32) + dt_bias[layer].astype(jnp.float32))
        o_b = chunked_gated_delta_rule(q_b, k_b, v_b, beta, g).astype(x.dtype)
        y_b = (rms_norm(o_b, gdn_norm_gain[layer])
               * jax.nn.silu(z_b.reshape(B, S, GDN_HEADS, GDN_DV))).reshape(B, S, GDN_WIDTH)

        gates = jax.nn.sigmoid(gate_l).reshape(B, S, N_BRANCH, D_MODEL)
        mixed = gates[:, :, 0, :] * y_a + gates[:, :, 1, :] * y_b
        x = x + mixed @ w_out[layer]
    return rms_norm(x, final_gain)


MEM_LEN = 256
MAX_GROUPS = 8
N_BRANCHES = 4
BRANCH_WIDTH = 256
MLA_HEADS = 4
MLA_NOPE = 64
MLA_ROPE = 32
MLA_V = 64
MLA_Q_RANK = 384
MLA_KV_RANK = 256
ROPE_THETA_2 = 10000.0
SB_HEADS = 4
SB_HEAD_DIM = 64
FOX_HEADS = 4
FOX_HEAD_DIM = 64
MEM_HEADS = 4
MEM_HEAD_DIM = 64
MERGE_RANK = 128
RMS_EPS = 1e-6
LN_EPS = 1e-5
DEEPNORM_ALPHA = (2 * DEPTH) ** 0.25
DEEPNORM_BETA = (8 * DEPTH) ** -0.25

IN_SPLITS_2 = (
    MLA_Q_RANK,
    MLA_KV_RANK,
    MLA_ROPE,
    3 * SB_HEADS * SB_HEAD_DIM,
    3 * FOX_HEADS * FOX_HEAD_DIM,
    FOX_HEADS,
    MEM_HEADS * MEM_HEAD_DIM,
    N_BRANCHES * BRANCH_WIDTH,
    MERGE_RANK,
)
IN_WIDTH = sum(IN_SPLITS_2)


def _split_last(t, sizes):
    out, start = [], 0
    for n in sizes:
        out.append(t[..., start:start + n])
        start += n
    return out

def _rms_norm(x, g):
    xf = x.astype(jnp.float32)
    y = xf * lax.rsqrt(jnp.mean(xf * xf, axis=-1, keepdims=True) + RMS_EPS)
    return (y * g.astype(jnp.float32)).astype(x.dtype)

def _layer_norm(x, g, b):
    xf = x.astype(jnp.float32)
    mu = jnp.mean(xf, axis=-1, keepdims=True)
    var = jnp.mean(jnp.square(xf - mu), axis=-1, keepdims=True)
    y = (xf - mu) * lax.rsqrt(var + LN_EPS)
    return (y * g.astype(jnp.float32) + b.astype(jnp.float32)).astype(x.dtype)

def _rope(x, cos, sin):
    x1, x2 = jnp.split(x, 2, axis=-1)
    return jnp.concatenate([x1 * cos - x2 * sin, x1 * sin + x2 * cos], axis=-1)

def _causal_sweep(block_fn, s):
    n_blocks = s // Q_BLOCK
    n_groups = min(MAX_GROUPS, n_blocks)
    bounds = [(g * n_blocks) // n_groups for g in range(n_groups + 1)]
    outs = []
    for g in range(n_groups):
        b0, b1 = bounds[g], bounds[g + 1]
        o = lax.map(functools.partial(block_fn, kend=b1 * Q_BLOCK), jnp.arange(b0, b1))
        nb, b, qn, h, dv = o.shape
        outs.append(o.transpose(1, 0, 2, 3, 4).reshape(b, nb * qn, h, dv))
    return jnp.concatenate(outs, axis=1)

def _causal_softmax_attention(q, k, v, log_decay=None):
    b, s, h, d = q.shape
    q = q * (d ** -0.5)
    c_t = None if log_decay is None else log_decay.transpose(0, 2, 1)

    def block(i, kend):
        start = i * Q_BLOCK
        qb = lax.dynamic_slice_in_dim(q, start, Q_BLOCK, axis=1)
        kb, vb = k[:, :kend], v[:, :kend]
        logits = jnp.einsum('bqhd,bkhd->bhqk', qb, kb, preferred_element_type=jnp.float32)
        if c_t is not None:
            cq = lax.dynamic_slice_in_dim(c_t, start, Q_BLOCK, axis=2)
            logits = logits + (cq[..., :, None] - c_t[..., None, :kend])
        causal = jnp.arange(kend)[None, :] <= (start + jnp.arange(Q_BLOCK))[:, None]
        logits = jnp.where(causal, logits, -jnp.inf)
        m = jnp.max(logits, axis=-1, keepdims=True)
        p = jnp.exp(logits - m)
        denom = jnp.sum(p, axis=-1).transpose(0, 2, 1)[..., None]
        o = jnp.einsum('bhqk,bkhd->bqhd', p.astype(v.dtype), vb, preferred_element_type=jnp.float32)
        return (o / denom).astype(v.dtype)

    return _causal_sweep(block, s)

def _stick_breaking_attention(q, k, v):
    b, s, h, d = q.shape
    q = q * (d ** -0.5)
    tri = jnp.tril(jnp.ones((Q_BLOCK, Q_BLOCK), jnp.float32))

    def block(i, kend):
        start = i * Q_BLOCK
        nk = kend // Q_BLOCK
        qb = lax.dynamic_slice_in_dim(q, start, Q_BLOCK, axis=1)
        kb, vb = k[:, :kend], v[:, :kend]
        z = jnp.einsum('bqhd,bkhd->bhqk', qb, kb, preferred_element_type=jnp.float32)
        strict = jnp.arange(kend)[None, :] < (start + jnp.arange(Q_BLOCK))[:, None]
        log_keep = jnp.where(strict, jax.nn.log_sigmoid(-z), 0.0)
        local = jnp.einsum('bhqnc,cr->bhqnr', log_keep.reshape(b, h, Q_BLOCK, nk, Q_BLOCK), tri)
        tot = local[..., 0]
        cross = lax.cumsum(tot, axis=3, reverse=True) - tot
        incl = (local + cross[..., None]).reshape(b, h, Q_BLOCK, kend)
        a = jnp.where(strict, jnp.exp(z + incl), 0.0).astype(v.dtype)
        return jnp.einsum('bhqk,bkhd->bqhd', a, vb)

    return _causal_sweep(block, s)

def _memory_attention(q, k, v):
    logits = jnp.einsum('bshd,bmhd->bhsm', q * (q.shape[-1] ** -0.5), k,
                        preferred_element_type=jnp.float32)
    p = jax.nn.softmax(logits, axis=-1).astype(v.dtype)
    return jnp.einsum('bhsm,bmhd->bshd', p, v)

def _layer(x, mem, cos, sin, w_in, q_norm, w_qb, kv_norm, w_kvb, fox_bias,
           w_mem_kv, w_merge_up, w_branch, w_out, ln_g, ln_b):
    b, s, _ = x.shape
    h = x @ w_in
    (c_q, c_kv, k_rope, sb_qkv, fox_qkv, fox_f, mem_q, gate_z, merge_r) = _split_last(h, IN_SPLITS_2)

    q = (_rms_norm(c_q, q_norm) @ w_qb).reshape(b, s, MLA_HEADS, MLA_NOPE + MLA_ROPE)
    q_nope, q_pe = q[..., :MLA_NOPE], q[..., MLA_NOPE:]
    q_pe = _rope(q_pe, cos[:, :, None, :], sin[:, :, None, :])
    kv = (_rms_norm(c_kv, kv_norm) @ w_kvb).reshape(b, s, MLA_HEADS, MLA_NOPE + MLA_V)
    k_nope, v_mla = kv[..., :MLA_NOPE], kv[..., MLA_NOPE:]
    k_pe = _rope(k_rope[:, :, None, :], cos[:, :, None, :], sin[:, :, None, :])
    k_pe = jnp.broadcast_to(k_pe, (b, s, MLA_HEADS, MLA_ROPE))
    y_mla = _causal_softmax_attention(jnp.concatenate([q_nope, q_pe], -1),
                                      jnp.concatenate([k_nope, k_pe], -1), v_mla)

    sq, sk, sv = [t.reshape(b, s, SB_HEADS, SB_HEAD_DIM) for t in jnp.split(sb_qkv, 3, axis=-1)]
    y_sb = _stick_breaking_attention(sq, sk, sv)

    fq, fk, fv = [t.reshape(b, s, FOX_HEADS, FOX_HEAD_DIM) for t in jnp.split(fox_qkv, 3, axis=-1)]
    log_f = jax.nn.log_sigmoid(fox_f.astype(jnp.float32) + fox_bias.astype(jnp.float32))
    c = jnp.cumsum(log_f, axis=1)
    y_fox = _causal_softmax_attention(fq, fk, fv, log_decay=c)

    mk, mv = jnp.split(mem @ w_mem_kv, 2, axis=-1)
    mk = mk.reshape(b, MEM_LEN, MEM_HEADS, MEM_HEAD_DIM)
    mv = mv.reshape(b, MEM_LEN, MEM_HEADS, MEM_HEAD_DIM)
    y_mem = _memory_attention(mem_q.reshape(b, s, MEM_HEADS, MEM_HEAD_DIM), mk, mv)

    branches = (y_mla, y_sb, y_fox, y_mem)
    gate_z = gate_z.reshape(b, s, N_BRANCHES, BRANCH_WIDTH)
    merge_g = jax.nn.sigmoid(merge_r @ w_merge_up).reshape(b, s, N_BRANCHES, D_MODEL)
    merged = jnp.zeros_like(x)
    for n in range(N_BRANCHES):
        yb = branches[n].reshape(b, s, BRANCH_WIDTH) * jax.nn.silu(gate_z[:, :, n])
        merged = merged + merge_g[:, :, n] * (yb @ w_branch[n])
    out = merged @ w_out

    return _layer_norm(DEEPNORM_ALPHA * x + out, ln_g, ln_b)

def second_inputs(seed: int = 0) -> dict:
    key = jax.random.key(seed)
    ks = jax.random.split(key, 16)
    f32 = jnp.float32

    def nrm(k, shape, scale):
        return jax.random.normal(k, shape, f32) * scale

    x = nrm(ks[0], (BATCH, SEQ, D_MODEL), 1.0)
    mem = nrm(ks[1], (BATCH, MEM_LEN, D_MODEL), 1.0)
    offsets = jax.random.randint(ks[2], (BATCH, 1), 0, 4096, dtype=jnp.int32)
    positions = (jnp.arange(SEQ, dtype=jnp.int32)[None, :] + offsets).astype(jnp.int32)

    w_in = nrm(ks[3], (DEPTH, D_MODEL, IN_WIDTH), D_MODEL ** -0.5)
    mla_q_norm = 1.0 + nrm(ks[4], (DEPTH, MLA_Q_RANK), 0.02)
    mla_w_qb = nrm(ks[5], (DEPTH, MLA_Q_RANK, MLA_HEADS * (MLA_NOPE + MLA_ROPE)), MLA_Q_RANK ** -0.5)
    mla_kv_norm = 1.0 + nrm(ks[6], (DEPTH, MLA_KV_RANK), 0.02)
    mla_w_kvb = nrm(ks[7], (DEPTH, MLA_KV_RANK, MLA_HEADS * (MLA_NOPE + MLA_V)), MLA_KV_RANK ** -0.5)
    fox_forget_bias = jax.random.uniform(ks[8], (DEPTH, FOX_HEADS), f32, 1.0, 4.0)
    w_mem_kv = nrm(ks[9], (DEPTH, D_MODEL, 2 * MEM_HEADS * MEM_HEAD_DIM), D_MODEL ** -0.5)
    w_merge_up = nrm(ks[10], (DEPTH, MERGE_RANK, N_BRANCHES * D_MODEL), MERGE_RANK ** -0.5)
    w_branch = nrm(ks[11], (DEPTH, N_BRANCHES, BRANCH_WIDTH, D_MODEL), BRANCH_WIDTH ** -0.5 * DEEPNORM_BETA)
    w_out = nrm(ks[12], (DEPTH, D_MODEL, D_MODEL), D_MODEL ** -0.5 * DEEPNORM_BETA)
    ln_gain = 1.0 + nrm(ks[13], (DEPTH, D_MODEL), 0.02)
    ln_bias = nrm(ks[14], (DEPTH, D_MODEL), 0.02)
    return {"x": x, "mem": mem, "positions": positions, "w_in": w_in,
            "mla_q_norm": mla_q_norm, "mla_w_qb": mla_w_qb,
            "mla_kv_norm": mla_kv_norm, "mla_w_kvb": mla_w_kvb,
            "fox_forget_bias": fox_forget_bias, "w_mem_kv": w_mem_kv,
            "w_merge_up": w_merge_up, "w_branch": w_branch, "w_out": w_out,
            "ln_gain": ln_gain, "ln_bias": ln_bias}

def second_block(x, mem, positions, w_in, mla_q_norm, mla_w_qb, mla_kv_norm, mla_w_kvb,
              fox_forget_bias, w_mem_kv, w_merge_up, w_branch, w_out, ln_gain, ln_bias):
    inv_freq = ROPE_THETA_2 ** (-jnp.arange(0, MLA_ROPE, 2, dtype=jnp.float32) / MLA_ROPE)
    ang = positions.astype(jnp.float32)[..., None] * inv_freq
    cos = jnp.cos(ang).astype(x.dtype)
    sin = jnp.sin(ang).astype(x.dtype)
    for l in range(DEPTH):
        x = _layer(x, mem, cos, sin, w_in[l], mla_q_norm[l], mla_w_qb[l],
                   mla_kv_norm[l], mla_w_kvb[l], fox_forget_bias[l], w_mem_kv[l],
                   w_merge_up[l], w_branch[l], w_out[l], ln_gain[l], ln_bias[l])
    return x


def setup_inputs(seed=0):
    out = dict(first_inputs(seed))
    for name, value in second_inputs(seed + 1).items():
        if name != "x":
            out[name + "_2"] = value
    return out


def reference(
    x, positions, norm_gain, w_in, conv_w, a_log, dt_bias, gdn_norm_gain, idx_k_gain, w_out,
    final_gain, mem_2, positions_2, w_in_2, mla_q_norm_2, mla_w_qb_2, mla_kv_norm_2,
    mla_w_kvb_2, fox_forget_bias_2, w_mem_kv_2, w_merge_up_2, w_branch_2, w_out_2, ln_gain_2,
    ln_bias_2,
):
    x = first_block(
        x, positions, norm_gain, w_in, conv_w, a_log, dt_bias, gdn_norm_gain, idx_k_gain, w_out,
        final_gain,
    )
    return second_block(
        x, mem_2, positions_2, w_in_2, mla_q_norm_2, mla_w_qb_2, mla_kv_norm_2, mla_w_kvb_2,
        fox_forget_bias_2, w_mem_kv_2, w_merge_up_2, w_branch_2, w_out_2, ln_gain_2, ln_bias_2,
    )


_drawn_inputs = setup_inputs


def setup_inputs(seed=0):
    import zlib

    import numpy as np

    out = dict(_drawn_inputs(seed))
    spreads = {}
    factors = {'norm_gain': 2.796,
     'gdn_norm_gain': 5.653,
     'idx_k_gain': 6.153,
     'final_gain': 2.843,
     'mem_2': 6.915,
     'mla_q_norm_2': 8.0,
     'mla_w_qb_2': 4.566,
     'mla_kv_norm_2': 8.0,
     'mla_w_kvb_2': 3.063,
     'fox_forget_bias_2': 4.296,
     'w_mem_kv_2': 6.401}
    for name, (base, spread) in spreads.items():
        noise = np.random.default_rng([zlib.crc32(name.encode()), seed]).standard_normal(out[name].shape)
        drawn = base * np.exp(spread * noise) if base else spread * noise
        out[name] = __import__('jax').numpy.asarray(drawn.astype(out[name].dtype))
    for name, factor in factors.items():
        out[name] = (out[name] * factor).astype(out[name].dtype)
    return out
```

```python
from contextlib import ExitStack

import numpy as np
import concourse.bass as bass
from concourse import mybir

F32 = mybir.dt.float32
F32R = mybir.dt.float32r
I32 = mybir.dt.int32
ALU = mybir.AluOpType
ACT = mybir.ActivationFunctionType
AX = mybir.AxisListType.X

P = 128
S = 256
R = S // P
D = 1024
KD = D // P
DEPTH = 2
NEG = -1.0e30
TAKEN = -3.0e38
EPS = 1e-6
LN_EPS = 1e-5
TOPK = 64
ALPHA = (2 * DEPTH) ** 0.25

C_QA, C_ZA, C_QI, C_KI, C_GQ, C_ZB, C_BA, C_GATE = 0, 1536, 2560, 3072, 3144, 6216, 7240, 7256
IN_COLS = 9304
IN_WIDTH = 3620
B_CKV, B_KR, B_SB, B_FOX, B_FF, B_MQ, B_GATE, B_MR = 384, 640, 672, 1440, 2208, 2212, 2468, 3492

K_ID, K_TRIU, K_LEVEL, K_PAIR, K_NEG, K_STR, K_NSTR, K_TRIL, K_ONE, K_FREQ = (
    0, 128, 256, 1024, 1152, 1408, 1664, 1920, 2048, 2176)
LEVELS = (2, 4, 8, 16, 32, 64)
K_COLS = K_FREQ + 40


def shape_constants():
    c = np.zeros((P, K_COLS), np.float32)
    p, f = np.arange(P)[:, None], np.arange(P)[None, :]
    c[:, K_ID:K_ID + P] = p == f
    c[:, K_TRIU:K_TRIU + P] = p <= f
    for n, s in enumerate(LEVELS):
        c[:, K_LEVEL + n * P:K_LEVEL + (n + 1) * P] = (
            (p // (2 * s) == f // (2 * s)) & (p // s % 2 == 1) & (f // s % 2 == 0))
    c[:, K_PAIR:K_PAIR + P] = (f % 2 == 1) & (p == f - 1)
    c[:, K_NEG + P:K_NEG + 2 * P] = np.where(f > p, np.float32(NEG), np.float32(0))
    c[:, K_STR:K_STR + P] = p < f
    c[:, K_STR + P:K_STR + 2 * P] = 1
    c[:, K_NSTR:K_NSTR + P] = np.where(p < f, np.float32(0), np.float32(NEG))
    c[:, K_TRIL:K_TRIL + P] = p >= f
    c[:, K_ONE:K_ONE + P] = 1
    at = K_FREQ
    for theta, rot in ((500000.0, 32), (500000.0, 16), (10000.0, 32)):
        half = rot // 2
        c[:, at:at + half] = np.float32(theta) ** (-np.arange(0, rot, 2, dtype=np.float32) / np.float32(rot))
        at += half
    return c


def tile_units(ksizes):
    out, k = [], 0
    for n in ksizes:
        out.append((k, n))
        k += n
    return out


PAIRS = [2, 2, 2, 2]
MEM_TILES = [(f"mkv{l}", dict(src="w_mem_kv", layer=l, col=0, n=512, ks=PAIRS, lhs="big", drain="scalar"))
             for l in range(DEPTH)]


def nat(src, col, n, drain, ks=PAIRS, lhs="big"):
    return dict(src=src, col=col, n=n, ks=ks, lhs=lhs, drain=drain)


def conv_tiles(g):
    return [(f"c{w}{g}", dict(src="w_in", col=C_GQ + w * 1024 + g * 512, n=512, ks=PAIRS, lhs="T", drain="scalar"))
            for w in range(3)]


ONE_TILES = (
    [("ba", nat("w_in", C_BA, 16, "vector", ks=[8]))]
    + conv_tiles(0)
    + [("qi", nat("w_in", C_QI, 512, "scalar")), ("ki", nat("w_in", C_KI, 72, "scalar", ks=[8])),
       ("kv", nat("w_in", 1024, 512, "scalar")), ("qa0", nat("w_in", 0, 512, "scalar")),
       ("qa1", nat("w_in", 512, 512, "scalar"))]
    + conv_tiles(1)
    + [(f"za{c}", nat("w_in", C_ZA + c * 512, 512, "scalar")) for c in range(2)]
    + [(f"zb{c}", nat("w_in", C_ZB + c * 512, 512, "scalar")) for c in range(2)]
    + [(f"g{b}{c}", nat("w_in", C_GATE + b * 1024 + c * 512, 512, "scalar")) for b in range(2) for c in range(2)]
    + [(f"o{c}", nat("w_out", c * 512, 512, "vector")) for c in range(2)])

H2_TILES = [(0, 512), (512, 512), (1024, 512), (1536, 512), (2048, 420)]
TWO_TILES = (
    [(f"h{n}", nat("w_in_2", c, w, "scalar")) for n, (c, w) in enumerate(H2_TILES)]
    + [("qb", nat("mla_w_qb", 0, 384, "scalar", ks=[2, 1], lhs="cq")),
       ("kvb", nat("mla_w_kvb", 0, 512, "scalar", ks=[2], lhs="ckv")),
       ("mr", nat("w_in_2", B_MR, 128, "scalar", ks=[8]))]
    + [(f"gz{c}", nat("w_in_2", B_GATE + c * 512, 512, "scalar")) for c in range(2)]
    + [(f"mu{c}", nat("w_merge_up", c * 512, 512, "scalar", ks=[1], lhs="mr")) for c in range(8)]
    + [(f"br{n}{c}", nat("w_branch", c * 512, 512, "vector", ks=[2], lhs=f"yb{n}"))
       for n in (1, 2, 3, 0) for c in range(2)]
    + [(f"o{c}", nat("w_out_2", c * 512, 512, "vector")) for c in range(2)])

RAW_SLOTS = 5
SPLIT_SLOTS = 3
LOOK = 3
RATE_ONE = 2
RATE_TWO = 2
ARENA = 24600


def units_of(tiles):
    return [(name, t, k0, nk, k0 == 0, k0 + nk == sum(t["ks"])) for name, t in tiles for k0, nk in tile_units(t["ks"])]


UNITS = {"mem": units_of(MEM_TILES), "one": units_of(ONE_TILES), "mid": [], "two": units_of(TWO_TILES)}


DRAIN_STEP = {"scalar": "drain_s", "vector": "drain_v"}


def weave(units, before, chain, rate):
    out, done, chain = list(before), set(), list(chain)
    marks = ("need", "gate", "gate_end")

    def flush(kind, tile):
        if (kind, tile) in chain:
            n = chain.index((kind, tile))
            out.extend(s for s in chain[:n] if s[0] not in marks)
            del chain[:n + 1]

    for u in range(min(LOOK, len(units))):
        out.append(("split", u))
    for u, (name, w, _, _, first, last) in enumerate(units):
        if first:
            flush("gate", name)
        out.append(("mm", u))
        if u + LOOK < len(units):
            out.append(("split", u + LOOK))
        if last:
            flush("gate_end", name)
            if w["lhs"] == "T":
                out += [("tap", int(name[1]), int(name[2])), ("conv", int(name[1]), int(name[2]))]
            else:
                out.append((DRAIN_STEP[w["drain"]], name))
                if w["src"] == "w_in" and w["col"] >= C_GATE:
                    out.append(("gmul", name))
                if name == "mr":
                    out.append(("mrT",))
            done.add(name)
        k = 0
        while chain and k < rate and chain[0][0][:4] != "gate" and (chain[0][0] != "need" or chain[0][1] in done):
            step = chain.pop(0)
            if step[0] != "need":
                out.append(step)
                k += 1
    return out + [step for step in chain if step[0] not in marks]


def gdn_chain(g):
    out = [("need", f"c0{g}"), ("stat", 0, g), ("need", f"c1{g}"), ("stat", 1, g), ("rn", g),
           ("dec", g, 0), ("dec_b", g, 0), ("dec_c", g, 0), ("kk", g, 0), ("dec", g, 1), ("dec_b", g, 1),
           ("dec_c", g, 1), ("kk", g, 1), ("x1", g, 0), ("x1", g, 1), ("kT", g)]
    for n in range(len(LEVELS)):
        for r in range(R):
            out.append(("invY", g, r, n))
        for r in range(R):
            out.append(("invZ", g, r, n))
        if n == 0:
            out += [("need", f"c2{g}"), ("vT", g)]
    out += [("kq", g, 0), ("kq", g, 1), ("u", g, 0), ("st", g), ("ks", g), ("o", g, 0), ("u", g, 1), ("o", g, 1)]
    return out


def attention_chain():
    out = [("need", "ki"), ("kinorm_a",), ("kinorm",), ("rope_i",)]
    out += [("iT", r) for r in range(R)]
    out += [("raw", 0, 0), ("raw", 1, 0), ("raw", 1, 1), ("topk", 0), ("topk", 1), ("need", "qa1"), ("rope_a",)]
    out += [("qT", r) for r in range(R)] + [("kaT",)]
    units = [(kv, qb) for kv in range(2) for qb in range(2)]
    for i, u in enumerate(units + [None]):
        if u is not None:
            out.append(("sc", *u))
        if i > 0:
            out += [("pT", *units[i - 1]), ("pv", *units[i - 1])]
    return out


def block_one():
    chain = [("need", "ba"), ("ba_a",), ("ba_b",), ("ba_c",), ("gc",), ("gc_b",)]
    chain += gdn_chain(0) + [("gate_end", "c01")] + gdn_chain(1)
    chain += [("onorm_a",), ("onorm",), ("onorm_c",)] + attention_chain()
    chain += [("need", "g11"), ("mix", 0), ("mT", 0), ("mix", 1), ("mT", 1), ("gate", "o0")]
    before = [("params",), ("norm_a",), ("norm",), ("norm_c",), ("gain",)] + [("hT", r) for r in range(R)]
    return weave(UNITS["one"], before, chain, RATE_ONE)


FOX, MEM, MLA = 2, 3, 0


def softmax_chain(n):
    out = [("qk2T", n)] + ([("qk2T", n, 1)] if n == MLA else [])
    if n == FOX:
        out += [("fb",)]
    return out + [("sc2", n, 0), ("sc2", n, 1), ("p2T", n, 0), ("pv2", n, 0), ("p2T", n, 1), ("pv2", n, 1)]


def block_two():
    chain = [("need", "h1"), ("lat_a",), ("lat",), ("lat_c",), ("ckT", 0), ("ckT", 1), ("gate", "qb"),
             ("need", "h2"), ("qk2T", 1), ("sbz", 0), ("sbz", 1), ("sbl", 0), ("sbl", 1), ("sbm", 0), ("sbm", 1),
             ("sbi", 0), ("sbi", 1), ("sbe", 0), ("sbe", 1), ("sbo", 0), ("sbo", 1)]
    chain += [("need", "h4"), ("ff_a",), ("ff",), ("ff_c",), ("fc",)] + softmax_chain(FOX) + softmax_chain(MEM)
    chain += [("ln_rows",), ("need", "kvb"), ("rope_2",), ("need", "gz1")]
    for n in (1, 2, 3):
        chain += [("gy", n), ("yT", n)]
    chain += [("gate", "br10")] + softmax_chain(MLA) + [("gy", 0), ("yT", 0), ("gate", "br00")]
    chain += [("gate_end", "br01"), ("need", "br01"), ("gT", 0), ("gT", 1), ("gate", "o0")]
    before = [("params2",), ("xT", 0), ("xT", 1)]
    return weave(UNITS["two"], before, chain, RATE_TWO) + [("ln_a",), ("ln_s",), ("ln",)]


TIMELINE = {
    "mem": weave(UNITS["mem"], [("memT", 0), ("memT", 1)],
                 [("tables_a",), ("tables",), ("tables_c",), ("cwT",)], 1),
    "one": block_one(),
    "mid": [("norm_a",), ("norm",), ("norm_c",)],
    "two": block_two(),
}
TILES = {"mem": MEM_TILES, "one": ONE_TILES, "mid": [], "two": TWO_TILES}
LEFT = {
    "mem": {"mkv0": [("memT", 1)]},
    "one": {"ba": [("hT", 1)], "o0": [("mT", 1)]},
    "two": {"h0": [("xT", 1)], "qb": [("ckT", 1)], "mu0": [("mrT",)],
            "br10": [("yT", 1)], "br20": [("yT", 2)], "br30": [("yT", 3)], "br00": [("yT", 0)],
            "o0": [("gT", 1)]},
}
CONV_BEFORE = {(1, 0): (0, 0), (2, 0): (1, 0), (0, 1): (2, 0), (1, 1): (0, 1), (2, 1): (1, 1)}
ITERATIONS = {"mem": 1, "one": DEPTH, "mid": 1, "two": DEPTH}
SECTIONS = ["mem", "one", "mid", "two"]

DRAINER = {
    "memT": "vector", "cwT": "vector", "hT": "vector", "gc": "vector", "stat": "vector", "dec": "vector",
    "kk": "vector", "x1": "scalar", "kT": "vector", "invY": "vector", "invZ": "vector", "vT": "vector",
    "kq": "vector", "u": "scalar", "st": "scalar", "ks": "vector", "o": "vector", "iT": "scalar",
    "raw": "scalar", "qT": "scalar", "kaT": "scalar", "sc": "vector", "pT": "scalar", "pv": "vector",
    "mT": "vector",
    "xT": "vector", "ckT": "vector", "mrT": "vector", "qk2T": "scalar", "fc": "vector",
    "fb": "vector", "sc2": "vector", "p2T": "scalar", "pv2": "vector", "sbz": "vector", "sbi": "vector",
    "sbo": "vector", "yT": "vector", "gT": "vector",
}


EMPTIED_BY = {"dec": "dec_c"}


class Order:

    def __init__(self, ctx, nc):
        self.ctx, self.nc, self.sems = ctx, nc, {}
        self.ordinal, self.per = {}, {}
        for sec in SECTIONS:
            for step in TIMELINE[sec]:
                n = self.per.get((sec, step[0]), 0)
                self.ordinal[(sec,) + step] = n
                self.per[(sec, step[0])] = n + 1

    def sem(self, name):
        if name not in self.sems:
            self.sems[name] = self.ctx.enter_context(self.nc.semaphore(name))
        return self.sems[name]

    def base(self, sec, step):
        return sum(ITERATIONS[s] * self.per.get((s, step), 0) for s in SECTIONS[:SECTIONS.index(sec)])

    def after(self, engine, sec, l, step, *args):
        n = self.ordinal[(sec, step) + args]
        return self.sem(f"{step}_{engine}"), self.base(sec, step) + l * self.per[(sec, step)] + n + 1

    def before_section(self, engine, sec, l, step):
        return self.sem(f"{step}_{engine}"), self.base(sec, step) + l * self.per.get((sec, step), 0)


STEPS = {"mem": {"vector": 11},
         "one": {"scalar": 6, "vector": 186},
         "mid": {"scalar": 1, "vector": 6},
         "two": {"scalar": 5, "vector": 60}}
COUNTED = None


class Program:

    def __init__(self, order, eng, name):
        self.o, self.eng, self.name = order, eng, name
        self.own = order.sem(f"{name}_step")
        self.n, self.base, self.sec, self.l = 0, 0, None, 0

    def enter(self, sec, l):
        self.sec, self.l, self.n = sec, l, 0
        self.base = sum(ITERATIONS[s] * STEPS[s].get(self.name, 0) for s in SECTIONS[:SECTIONS.index(sec)])

    def leave(self):
        COUNTED.append((self.sec, self.name, self.n)) if COUNTED is not None else None
        if COUNTED is None:
            assert self.n == STEPS[self.sec].get(self.name, 0), (self.sec, self.name, self.n)

    def after(self, engine, step, *args):
        return self.o.after(engine, self.sec, self.l, step, *args)

    def done(self, step):
        return self.o.sem(f"{step}_{self.name}")

    def here(self, step):
        return self.o.after(self.name, self.sec, self.l, step, *self.args)

    def last(self):
        self.n += 1
        return self.own, self.base + self.l * STEPS[self.sec].get(self.name, 0) + self.n


def two_before():
    half, had = {}, {}
    for sec in SECTIONS:
        seen = []
        for step in TIMELINE[sec]:
            if step[0] in DRAINER:
                half[(sec,) + step] = len(seen) % 2
                had[(sec,) + step] = seen[-2] if len(seen) >= 2 else None
                seen.append(step)
    return half, had


def build(nc, t, out, stop_after="two"):
    ctx = ExitStack()
    with ctx:
        o = Order(ctx, nc)
        half_of, had_half = two_before()

        def sb(name, cols, dt=F32, parts=P):
            return ctx.enter_context(nc.sbuf_tensor(name, [parts] + cols, dt))

        cst = sb("cst", [K_COLS])
        xs = sb("xs", [R, D])
        raw = sb("raw", [RAW_SLOTS, 1024])
        w_hi = sb("w_hi", [SPLIT_SLOTS, 1024], F32R)
        w_lo = sb("w_lo", [SPLIT_SLOTS, 1024], F32R)
        hT_hi = sb("hT_hi", [KD, S], F32R)
        hT_lo = sb("hT_lo", [KD, S], F32R)
        sT_hi = sb("sT_hi", [6, S], F32R)
        sT_lo = sb("sT_lo", [6, S], F32R)
        gain = sb("gain", [D])
        gain2 = sb("gain2", [D])
        cw_rows = sb("cw_rows", [DEPTH, P], parts=96)
        par1 = sb("par1", [DEPTH, 304])
        now1 = sb("now1", [304])
        taps, a_log, dt_bias = now1[:, 0:96], now1[:, 96:104], now1[:, 104:112]
        gdn_gain, idx_gain = now1[:, 112:240], now1[:, 240:304]
        par2 = sb("par2", [DEPTH, 644])
        now2 = sb("now2", [644])
        q_gain, kv_gain, fox_bias = now2[:, 0:384], now2[:, 384:640], now2[:, 640:644]
        pos_i = sb("pos_i", [2, R], I32)
        cos_t = sb("cos_t", [R, 40])
        sin_t = sb("sin_t", [R, 40])
        mkv = sb("mkv", [DEPTH, R, 512])
        tiny = sb("tiny", [512])
        arena = sb("arena", [ARENA])

        at = [0]

        def area(*dims, start=None):
            if start is not None:
                at[0] = start
            n = int(np.prod(dims))
            v = arena[:, at[0]:at[0] + n]
            at[0] += n
            assert at[0] <= ARENA, at[0]
            if len(dims) == 2:
                v = v.rearrange("p (a b) -> p a b", a=dims[0])
            if len(dims) == 3:
                v = v.rearrange("p (a b c) -> p a b c", a=dims[0], b=dims[1])
            return v

        pq = area(R, 1536, start=0)
        pi = area(R, 584)
        g0 = area(R, D)
        g1 = area(R, D)
        od = area(R, D)
        shared = at[0]
        cs = area(3, 4, S)
        cv = area(4, S)
        sq = area(4, S)
        vb = area(R, 4, P)
        kd = area(4, P)
        st = area(4, P)
        uu = area(R, 4, P)
        dt_ = area(R, 4, P)
        lt = area(R, 4, P)
        xx = area(R, 4, P)
        xt = area(R, 4, P)
        yy = area(R, 4, P)
        qaT = area(8, S, start=shared)
        kaT = area(2, S)
        qiT = area(4, S)
        kiT = area(S)
        isc = [area(P), area(S)]
        mb = [area(P), area(S)]
        rl = area(D)
        pr = [area(1024), area(1024)]
        pt = [area(1024), area(1024)]
        kk2 = area(R, 2, 64)
        rope_tmp = area(4, R * 160)
        assert at[0] <= ARENA
        h_nat = g0
        mem_raw = area(R, D, start=0)
        ang = area(5, R * 40, start=4096)

        h2 = area(R, IN_WIDTH, start=0)
        mg = area(R, 4096)
        q2 = area(R, 384)
        kv2 = area(R, 512)
        kc = area(R, 384)
        reg_a, reg_b = area(2048), area(1024)
        pr2 = [area(512), area(1024)]
        pt2 = [area(512), area(1024)]
        mkv_now = gain2[:, :].rearrange("p (r n) -> p r n", r=R)
        merged = h2[:, :, 0:D]
        tmp2 = kc[:, :, :].rearrange("p r n -> p (r n)")[:, 0:512].rearrange("p (a n) -> p a n", a=4)

        tn = [0]

        def small(*dims):
            n = int(np.prod(dims))
            v = tiny[:, tn[0]:tn[0] + n]
            tn[0] += n
            assert tn[0] <= 512
            if len(dims) == 2:
                v = v.rearrange("p (a b) -> p a b", a=dims[0])
            if len(dims) == 3:
                v = v.rearrange("p (a b c) -> p a b c", a=dims[0], b=dims[1])
            return v

        nrm = small(4, R)
        ba = small(R, 16)
        ay = small(2, R, 8)
        be = small(R, 8)
        eb = small(R, 8)
        ea = small(8)
        gdec = small(R, 8)
        gc = small(R, 8)
        egc = small(R, 8)
        wl = small(2, 8)
        ss = small(2, R, 4)
        s2 = small(2, R, 4)
        s3 = small(2, R, 4)
        av = small(R, 4)
        bke = small(4)
        wk = small(4)
        so = small(3, R, 8)
        kn = small(4, R)
        wi = small(R, 8)
        mx = [small(4), small(4)]
        rs = [small(4), small(4)]
        top = small(8)
        lat = small(4, 2, R)
        fy = small(3, R, 4)
        cf = small(R, 4)
        mx2 = [small(4), small(4)]
        rs2 = [small(4), small(4)]
        lnm = small(5, R)

        def ps(name):
            return ctx.enter_context(nc.psum_tensor(name, [P, 1024], F32))

        bulk = [ps("bulk0"), ps("bulk1")]
        chain = [ps("chain0"), ps("chain1")]

        ident = cst[:, K_ID:K_ID + P]
        triu = cst[:, K_TRIU:K_TRIU + P]
        ones = cst[:, K_ONE:K_ONE + P]

        Q_OF = {1: B_SB, FOX: B_FOX, MEM: B_MQ}

        def t_parts(n):
            reg = reg_b if n in (1, MEM) else reg_a
            a = 4 if n == MLA else 2
            return (reg[:, 0:a * S].rearrange("p (a n) -> p a n", a=a),
                    reg[:, a * S:2 * a * S].rearrange("p (a n) -> p a n", a=a))

        def head_of(n, q):
            return q if n == MLA else bank_order(q, 4)

        def head_T(n, h, which, cols):
            x = t_parts(n)[which]
            if n == MLA:
                return x[0:96, h, cols]
            return x[64 * (h % 2):64 * (h % 2) + 64, h // 2, cols]

        def values(n, h, k):
            if n == MLA:
                return kv2[:, k, h * P + 64:h * P + P]
            if n == MEM:
                return mkv_now[:, k, S + h * 64:S + (h + 1) * 64]
            c = Q_OF[n] + 512 + h * 64
            return h2[:, k, c:c + 64]

        def branch_y(n, r):
            return q2[:, r, 0:S] if n == MLA else h2[:, r, Q_OF[n]:Q_OF[n] + S]

        def keys_of(n, qb):
            return S if n == MEM else P * (qb + 1)

        def buf_of(n, qb):
            return keys_of(n, qb) // P - 1

        score_users = [[x for x in [(n, qb) for n in (FOX, MEM, MLA) for qb in range(2)] if buf_of(*x) == b]
                       for b in range(2)]

        def user_before(n, qb):
            u = score_users[buf_of(n, qb)]
            i = u.index((n, qb))
            return u[i - 1] if i else None

        def places(x, nk):
            return x.rearrange("p (q n) -> p q n", q=4)[:, :, 0:nk]

        def bank_order(i, per):
            return 2 * (i % (per // 2)) + i // (per // 2)

        def bc(v, n):
            return v.unsqueeze(2).broadcast_to([v.shape[0], v.shape[1], n])

        def over(v, a):
            return v.unsqueeze(1).broadcast_to([v.shape[0], a, v.shape[1]])

        def heads(v, a=4):
            return v.rearrange("p (a n) -> p a n", a=a)

        def layer_of(v, l, starts):
            n = int(np.prod(v.shape[1:]))
            if isinstance(l, int):
                at_l = l * n
            else:
                if n not in starts:
                    starts[n] = nc.sync.snap((l + 1) * n)
                at_l = starts[n] - n
            dims = " ".join(f"d{i}" for i in range(len(v.shape)))
            flat_v = v.rearrange(f"{dims} -> ({dims})")[bass.ds(at_l, n)]
            inner = " ".join(f"d{i}" for i in range(1, len(v.shape)))
            return flat_v.rearrange(f"({inner}) -> {inner}", **{f"d{i}": v.shape[i] for i in range(1, len(v.shape))})

        def dview(name, l, starts):
            v = layer_of(t[name], l, starts)
            if name == "w_branch":
                return v.rearrange("n (k p) c -> p (n k) c", p=P)
            return v.rearrange("(k p) c -> p k c", p=P)

        raw_in = [o.sem(f"raw_in{n}") for n in range(RAW_SLOTS)]
        const_in = o.sem("constants_loaded")
        par_in = o.sem("parameters_loaded")
        gain_in = o.sem("gain_loaded")
        ln_in = o.sem("ln_rows_loaded")
        topk_step = o.sem("topk_step")
        x_in = o.sem("x_loaded")
        mem_in = o.sem("memory_loaded")
        out_sem = o.sem("out_stored")
        N_PARAMS = 9

        def slot_value(sec, l, u):
            s = u % RAW_SLOTS
            uses = lambda sc: (len(UNITS[sc]) - s + RAW_SLOTS - 1) // RAW_SLOTS
            before = sum(ITERATIONS[x] * uses(x) for x in SECTIONS[:SECTIONS.index(sec)])
            return raw_in[s], (before + l * uses(sec) + u // RAW_SLOTS + 1) * 16

        def unit_before(p, engine, step, u, slots):
            if u >= slots:
                return p.after(engine, step, u - slots)
            return o.before_section(engine, p.sec, p.l, step)

        def drained(p, tile):
            name, w = tile
            if w["lhs"] == "T":
                return p.after("vector", "tap", int(name[1]), int(name[2]))
            return p.after(w["drain"], DRAIN_STEP[w["drain"]], name)

        def run(eng, name, handlers):
            p = Program(o, eng, name)
            steps = handlers(p)
            for sec in SECTIONS:
                if sec not in RUN_SECTIONS:
                    continue

                def body(l):
                    p.enter(sec, l)
                    for step in TIMELINE[sec]:
                        if step[0] in steps:
                            p.args = step[1:]
                            steps[step[0]](*step[1:])
                    p.leave()

                if ITERATIONS[sec] == 1:
                    body(0)
                else:
                    with eng.Fori(0, ITERATIONS[sec]) as l:
                        body(l)

        RUN_SECTIONS = SECTIONS[:SECTIONS.index(stop_after) + 1]
        block = ctx.enter_context(nc.Block())

        @block.sync
        def _(sp):
            for dst, src in (
                    (cst[:, :], t["shape_constants"]),
                    (pos_i[:, 0, :], t["positions"].rearrange("a (r p) -> p (a r)", p=P)),
                    (pos_i[:, 1, :], t["positions_2"].rearrange("a (r p) -> p (a r)", p=P))):
                sp.dma_start(dst, src, allow_slow_non_contiguous=True).then_inc(const_in, 16)
            sp.dma_start(mem_raw, t["mem_2"].rearrange("a (r p) d -> p (a r) d", p=P)).then_inc(mem_in, 16)
            loads = [(cw_rows[:, l, :], t["conv_w"][l].rearrange("k (c q) -> (k c) q", q=P)) for l in range(DEPTH)]
            for par, col, name in ((par1, 96, "a_log"), (par1, 104, "dt_bias"), (par1, 112, "gdn_norm_gain"),
                                   (par1, 240, "idx_k_gain"), (par2, 0, "mla_q_norm_2"), (par2, 384, "mla_kv_norm_2"),
                                   (par2, 640, "fox_forget_bias_2")):
                n = t[name].shape[1]
                loads.append((par[:, :, col:col + n], t[name].unsqueeze(0).broadcast_to([P, DEPTH, n])))
            assert len(loads) == N_PARAMS

            def load_gain(row):
                sp.dma_start(gain[:, :], row.broadcast_to([P, D])).then_inc(gain_in, 16)

            def handlers(p):
                starts = {}

                def first(*_):
                    starts.clear()
                    for n in sorted({w["src"] for _, w in TILES[p.sec]}):
                        dview(n, p.l, starts)
                    layer_of(t["ln_rows"].rearrange("(l i) d -> l i d", i=2), p.l, starts)
                    layer_of(t["gains"][1:, :], p.l, starts)

                def load(u):
                    if u == 0:
                        first()
                    name, w, k0, nk, _, _ = UNITS[p.sec][u]
                    if p.sec != "mem" or u >= RAW_SLOTS:
                        sp.wait_ge(*unit_before(p, "gpsimd", "split", u, RAW_SLOTS))
                    src = dview(w["src"], w.get("layer", p.l), starts)
                    if w["src"] == "w_branch":
                        k0 += 2 * int(w["lhs"][2])
                    sem, _ = slot_value(p.sec, p.l, u)
                    sp.dma_start(raw[:, u % RAW_SLOTS, 0:nk * w["n"]].rearrange("p (k n) -> p k n", k=nk),
                                 src[:, k0:k0 + nk, w["col"]:w["col"] + w["n"]]).then_inc(sem, 16)
                    if p.sec == "mem" and u == 3:
                        sp.dma_start(xs[:, :, :], t["x"].rearrange("a (r p) d -> p (a r) d", p=P)).then_inc(x_in, 16)
                        load_gain(t["gains"][0:1, :])
                        for dst, src in loads:
                            sp.dma_start(dst, src).then_inc(par_in, 16)

                def next_gain():
                    first()
                    sp.wait_ge(*p.after("vector", "norm_c"))
                    load_gain(layer_of(t["gains"][1:, :], p.l, starts).unsqueeze(0))

                def ln_rows():
                    sp.wait_ge(*p.after("vector", "pv2", MEM, 1))
                    sp.wait_ge(*p.after("tensor", "pv2", MEM, 1))
                    rows = layer_of(t["ln_rows"].rearrange("(l i) d -> l i d", i=2), p.l, starts)
                    for i, dst in enumerate((gain, gain2)):
                        sp.dma_start(dst[:, :], rows[i:i + 1, :].broadcast_to([P, D])).then_inc(
                            ln_in, 16)

                return {"split": load, "gain": next_gain, "ln_rows": ln_rows}

            run(sp, "sync", handlers)
            sem, v = o.after("vector", "mid", 0, "norm_c") if stop_after == "mid" else o.after(
                "vector", "two", DEPTH - 1, "ln")
            sp.wait_ge(sem, v)
            sp.dma_start(out.rearrange("a (r p) d -> p (a r) d", p=P), xs[:, :, :]).then_inc(out_sem, 16)
            sp.wait_ge(out_sem, 16)

        @block.gpsimd
        def _(pool):
            def handlers(p):
                def split(u):
                    _, w, _, nk, _, _ = UNITS[p.sec][u]
                    n = nk * w["n"]
                    pool.wait_ge(*slot_value(p.sec, p.l, u))
                    pool.wait_ge(*p.after("scalar", "split", u))
                    pool.tensor_tensor(w_lo[:, u % SPLIT_SLOTS, 0:n], raw[:, u % RAW_SLOTS, 0:n],
                                             w_hi[:, u % SPLIT_SLOTS, 0:n].bitcast(F32), ALU.subtract).then_inc(p.done("split"), 1)
                return {"split": split}

            run(pool, "gpsimd", handlers)

        @block.tensor
        def _(pe):
            def handlers(p):
                def lhs(w, kk, r):
                    kind, rr = w["lhs"], slice(r * P, (r + 1) * P)
                    if kind == "big":
                        return hT_hi[:, kk, rr], hT_lo[:, kk, rr]
                    if kind[:2] == "yb":
                        return hT_hi[:, 2 * int(kind[2]) + kk, rr], hT_lo[:, 2 * int(kind[2]) + kk, rr]
                    k = {"cq": 0, "ckv": 3, "mr": 5}[kind] + kk
                    return sT_hi[:, k, rr], sT_lo[:, k, rr]

                def mm(u):
                    name, w, k0, nk, first, last = UNITS[p.sec][u]
                    names = [x for x, _ in TILES[p.sec]]
                    tile, n, slot = names.index(name), w["n"], u % SPLIT_SLOTS
                    pair = bulk[tile % 2]
                    if first and tile >= 2:
                        pe.wait_ge(*drained(p, TILES[p.sec][tile - 2]))
                    if u == 0 or (first and w["lhs"] != "T"):
                        left_ready(w, name)
                    pe.wait_ge(*p.after("gpsimd", "split", u))
                    tot = sum(w["ks"])
                    hi = w_hi[:, slot, 0:nk * n].rearrange("p (k n) -> p k n", k=nk)
                    lo = w_lo[:, slot, 0:nk * n].rearrange("p (k n) -> p k n", k=nk)
                    for k in range(nk):
                        kk = k0 + k
                        if w["lhs"] == "T":
                            for j in range(4):
                                dst = pair[:, j * S:(j + 1) * S]
                                a_hi, a_lo = hi[:, k, j * P:(j + 1) * P], lo[:, k, j * P:(j + 1) * P]
                                for i, (a, b) in enumerate(((a_hi, hT_hi), (a_hi, hT_lo), (a_lo, hT_hi))):
                                    m = pe.matmul(dst, a, b[:, kk, :], start=(kk == 0 and i == 0 and j % 2 == 0),
                                                  stop=(kk == tot - 1 and i == 2 and j % 2 == 1),
                                                  skip_group_check=True)
                        else:
                            for r in range(R):
                                dst = pair[:, r * 512:r * 512 + n]
                                a_hi, a_lo = lhs(w, kk, r)
                                for i, (a, b) in enumerate(((a_hi, hi), (a_hi, lo), (a_lo, hi))):
                                    m = pe.matmul(dst, a, b[:, k, :], start=(kk == 0 and i == 0),
                                                  stop=(kk == tot - 1 and i == 2))
                    m.then_inc(p.done("mm"), 1)

                def left_ready(w, name):
                    if name in LEFT[p.sec]:
                        for step in LEFT[p.sec][name]:
                            pe.wait_ge(*p.after("vector", *step))

                def take(step, *args):
                    key = (p.sec, step) + args
                    had = had_half[key]
                    if had is not None:
                        pe.wait_ge(*p.after(DRAINER[had[0]], EMPTIED_BY.get(had[0], had[0]), *had[1:]))
                    return chain[half_of[key]]

                def transposes(c, srcs, n=P):
                    for i, v in enumerate(srcs):
                        m = pe.transpose(c[0:n, i * P:i * P + v.shape[0]], v, ident[0:v.shape[0], 0:v.shape[0]])
                    return m

                def memT(r):
                    if r == 0:
                        pe.wait_ge(const_in, 16 * 3)
                        pe.wait_ge(mem_in, 16)
                    c = take("memT", r)
                    transposes(c, [mem_raw[:, r, k * P:(k + 1) * P] for k in range(KD)]).then_inc(p.done("memT"), 1)

                def hT(r):
                    c = take("hT", r)
                    pe.wait_ge(*p.after("vector", "norm_c"))
                    transposes(c, [h_nat[:, r, k * P:(k + 1) * P] for k in range(KD)]).then_inc(p.done("hT"), 1)

                def cwT():
                    pe.wait_ge(par_in, 16 * N_PARAMS)
                    c = take("cwT")
                    transposes(c, [cw_rows[:, l, :] for l in range(DEPTH)]).then_inc(p.done("cwT"), 1)

                def gc_():
                    c = take("gc")
                    pe.wait_ge(*p.after("vector", "ba_c"))
                    for r in range(R):
                        pe.matmul(c[:, r * 8:(r + 1) * 8], triu, gdec[:, r, :], start=(r == 0), stop=False,
                                  skip_group_check=True)
                    pe.matmul(c[:, 16:24], ones, gdec[:, 0, :], start=False, stop=True,
                                    skip_group_check=True).then_inc(p.done("gc"), 1)

                def stat(w, g):
                    c = take("stat", w, g)
                    pe.wait_ge(*p.after("scalar", "stat", w, g))
                    for r in range(R):
                        for j in range(4):
                            m = pe.matmul(c[:, r * 4 + j:r * 4 + j + 1], sq[:, j, r * P:(r + 1) * P], ones[:, 0:1],
                                          start=(r == 0 and j == 0), stop=(r == 1 and j == 3), skip_group_check=True)
                    m.then_inc(p.done("stat"), 1)

                def dec(g, r):
                    c = take("dec", g, r)
                    pe.wait_ge(*p.after("vector", "rn", g))
                    for j in range(4):
                        pe.matmul(c[:, j * P:(j + 1) * P], gdec[:, r, 4 * g + j:4 * g + j + 1].broadcast_to([P, P]), triu,
                                  start=(j == 0), stop=(j == 3), skip_group_check=True)
                    for j in range(4):
                        m = pe.matmul(c[:, 512 + j * P:512 + (j + 1) * P], av[:, r, j:j + 1].broadcast_to([P, P]), ident,
                                      start=(j == 0), stop=(j == 3), skip_group_check=True)
                    m.then_inc(p.done("dec"), 1)

                def four(c, pairs):
                    for j, (a, b) in enumerate(pairs):
                        m = pe.matmul(c[:, j * P:(j + 1) * P], a, b, start=(j == 0), stop=(j == 3),
                                      skip_group_check=True)
                    return m

                def cst_t(w, j, r):
                    return cs[:, w, j, r * P:(r + 1) * P]

                def kk(g, r):
                    c = take("kk", g, r)
                    four(c, [(cst_t(1, j, r), cst_t(1, j, r)) for j in range(4)]).then_inc(p.done("kk"), 1)

                def x1(g, r):
                    c = take("x1", g, r)
                    pe.wait_ge(*p.after("vector", "kk", g, r))
                    transposes(c, [xt[:, r, j, :] for j in range(4)]).then_inc(p.done("x1"), 1)

                def kT(g):
                    c = take("kT", g)
                    transposes(c, [cst_t(1, j, 0) for j in range(4)]).then_inc(p.done("kT"), 1)

                def vT(g):
                    c = take("vT", g)
                    pe.wait_ge(*p.after("scalar", "conv", 2, g))
                    transposes(c, [cst_t(2, j, r) for r in range(R) for j in range(4)]).then_inc(p.done("vT"), 1)

                def invY(g, r, n):
                    c = take("invY", g, r, n)
                    if n == 0:
                        pe.wait_ge(*p.after("scalar", "x1", g, r))
                    else:
                        pe.wait_ge(*p.after("vector", "invZ", g, r, n - 1))
                    four(c, [(lt[:, r, j, :], xx[:, r, j, :]) for j in range(4)]).then_inc(p.done("invY"), 1)

                def invZ(g, r, n):
                    c = take("invZ", g, r, n)
                    pe.wait_ge(*p.after("vector", "invY", g, r, n))
                    if n < len(LEVELS) - 1:
                        four(c[:, 0:512], [(xt[:, r, j, :], yy[:, r, j, :]) for j in range(4)])
                    four(c[:, 512:1024], [(yy[:, r, j, :], xt[:, r, j, :]) for j in range(4)]).then_inc(p.done("invZ"), 1)

                def kq(g, r):
                    c = take("kq", g, r)
                    four(c, [(cst_t(1, j, r), cst_t(0, j, r)) for j in range(4)]).then_inc(p.done("kq"), 1)

                def u_(g, r):
                    c = take("u", g, r)
                    pe.wait_ge(*p.after("vector", "invZ", g, r, len(LEVELS) - 1))
                    pe.wait_ge(*p.after("vector", *(("vT", g) if r == 0 else ("ks", g))))
                    four(c, [(xt[:, r, j, :], vb[:, r, j, :]) for j in range(4)]).then_inc(p.done("u"), 1)

                def st_(g):
                    c = take("st", g)
                    pe.wait_ge(*p.after("vector", "kT", g))
                    pe.wait_ge(*p.after("scalar", "u", g, 0))
                    four(c, [(kd[:, j, :], uu[:, 0, j, :]) for j in range(4)]).then_inc(p.done("st"), 1)

                def ks(g):
                    c = take("ks", g)
                    pe.wait_ge(*p.after("scalar", "st", g))
                    four(c, [(cst_t(1, j, 1), st[:, j, :]) for j in range(4)]).then_inc(p.done("ks"), 1)

                def o_(g, r):
                    c = take("o", g, r)
                    pe.wait_ge(*p.after("vector", "kq", g, r))
                    pe.wait_ge(*p.after("scalar", "u", g, r))
                    m = four(c[:, 0:512], [(lt[:, r, j, :], uu[:, r, j, :]) for j in range(4)])
                    if r == 1:
                        m = four(c[:, 512:1024], [(cst_t(0, j, 1), st[:, j, :]) for j in range(4)])
                    m.then_inc(p.done("o"), 1)

                def iT(r):
                    c = take("iT", r)
                    pe.wait_ge(*p.after("vector", "rope_i"))
                    transposes(c, [pi[:, r, n * P:(n + 1) * P] for n in range(4)]
                                     + [kk2[:, r, :, :].rearrange("p a b -> p (a b)")]).then_inc(p.done("iT"), 1)

                def raw_(qb, part):
                    c = take("raw", qb, part)
                    pe.wait_ge(*p.after("scalar", "iT", R - 1))
                    nk = P * (qb + 1)
                    per = 1024 // nk
                    for i in range(per):
                        h = part * per + bank_order(i, per)
                        lo_ = 64 * (h % 2)
                        m = pe.matmul(c[:, i * nk:(i + 1) * nk], qiT[lo_:lo_ + 64, h // 2, qb * P:(qb + 1) * P],
                                      kiT[lo_:lo_ + 64, 0:nk], start=(i * nk % 512 == 0),
                                      stop=((i + 1) * nk % 512 == 0), skip_group_check=True)
                    m.then_inc(p.done("raw"), 1)

                def qT(r):
                    c = take("qT", r)
                    pe.wait_ge(*p.after("vector", "rope_a"))
                    transposes(c, [pq[:, r, h * P:(h + 1) * P] for h in range(8)]).then_inc(p.done("qT"), 1)

                def kaT_():
                    c = take("kaT")
                    transposes(c, [pq[:, r, D + kv * P:D + (kv + 1) * P] for kv in range(2) for r in range(R)]).then_inc(p.done("kaT"), 1)

                def sc(kv, qb):
                    c = take("sc", kv, qb)
                    pe.wait_ge(*p.after("scalar", "qT", 1))
                    pe.wait_ge(*p.after("scalar", "kaT"))
                    nk = P * (qb + 1)
                    for j in range(4):
                        m = pe.matmul(c[:, j * nk:(j + 1) * nk], qaT[:, 4 * kv + j, qb * P:(qb + 1) * P],
                                      kaT[:, kv, 0:nk], start=(j * nk % 512 == 0), stop=((j + 1) * nk % 512 == 0),
                                      skip_group_check=True)
                    m.then_inc(p.done("sc"), 1)

                def pT(kv, qb):
                    c = take("pT", kv, qb)
                    pe.wait_ge(*p.after("scalar", "sc", kv, qb))
                    transposes(c, [pr[qb][:, i * P:(i + 1) * P] for i in range(4 * (qb + 1))]).then_inc(p.done("pT"), 1)

                def pv(kv, qb):
                    c = take("pv", kv, qb)
                    pe.wait_ge(*p.after("scalar", "pT", kv, qb))
                    for j in range(4):
                        for k in range(qb + 1):
                            i = j * (qb + 1) + k
                            m = pe.matmul(c[:, j * P:(j + 1) * P], pt[qb][:, i * P:(i + 1) * P],
                                          pq[:, k, 1280 + kv * P:1280 + (kv + 1) * P],
                                          start=(j == 0 and k == 0), stop=(j == 3 and k == qb), skip_group_check=True)
                    m.then_inc(p.done("pv"), 1)

                def mT(r):
                    c = take("mT", r)
                    pe.wait_ge(*p.after("vector", "mix", r))
                    transposes(c, [g0[:, r, k * P:(k + 1) * P] for k in range(KD)]).then_inc(p.done("mT"), 1)

                def xT(r):
                    c = take("xT", r)
                    if r == 0:
                        pe.wait_ge(*p.after("vector", "params2"))
                    transposes(c, [xs[:, r, k * P:(k + 1) * P] for k in range(KD)]).then_inc(p.done("xT"), 1)

                def ckT(r):
                    c = take("ckT", r)
                    pe.wait_ge(*p.after("vector", "lat_c"))
                    transposes(c, [h2[:, r, k * P:(k + 1) * P] for k in range(5)]).then_inc(p.done("ckT"), 1)

                def mrT():
                    c = take("mrT")
                    pe.wait_ge(*p.after("scalar", "drain_s", "mr"))
                    transposes(c, [h2[:, r, B_MR:B_MR + P] for r in range(R)]).then_inc(p.done("mrT"), 1)

                def qk2T(n, part=0):
                    c = take("qk2T", n) if n != MLA or not part else take("qk2T", n, part)
                    if n == MLA:
                        pe.wait_ge(*p.after("vector", "rope_2"))
                        src = (q2, kc)[part]
                        return transposes(c, [src[:, r, h * 96:(h + 1) * 96] for h in range(4) for r in range(R)],
                                                96).then_inc(p.done("qk2T"), 1)
                    pe.wait_ge(*p.after("scalar", "drain_s", "h2" if n == 1 else "h4"))
                    q0 = Q_OF[n]
                    k_src, k0 = (mkv_now, 0) if n == MEM else (h2, q0 + S)
                    transposes(c, [h2[:, r, q0 + i * P:q0 + (i + 1) * P] for i in range(2) for r in range(R)]
                                     + [k_src[:, r, k0 + i * P:k0 + (i + 1) * P] for i in range(2) for r in range(R)]).then_inc(p.done("qk2T"), 1)

                def sbz(k):
                    c = take("sbz", k)
                    pe.wait_ge(*p.after("scalar", "qk2T", 1))
                    n = S - k * P
                    for q in range(4):
                        h = head_of(1, q)
                        m = pe.matmul(c[:, q * S:q * S + n], head_T(1, h, 1, slice(k * P, (k + 1) * P)),
                                      head_T(1, h, 0, slice(k * P, S)), start=(q % 2 == 0), stop=(q % 2 == 1),
                                      skip_group_check=True)
                    m.then_inc(p.done("sbz"), 1)

                def sbi(k):
                    c = take("sbi", k)
                    tril = cst[:, K_TRIL:K_TRIL + P]
                    pe.wait_ge(*p.after("vector", "sbm", 1))
                    if k == 1:
                        return pe.matmul(c[:, 0:512], tril, pt2[0], start=True, stop=True).then_inc(p.done("sbi"), 1)
                    for b in range(2):
                        pe.matmul(c[:, b * 512:(b + 1) * 512], tril, pt2[1][:, b * 512:(b + 1) * 512], start=True,
                                  stop=False, skip_group_check=True)
                        for q in (2 * b, 2 * b + 1):
                            m = pe.matmul(c[:, q * S + P:(q + 1) * S], ones, pt2[0][:, q * P:(q + 1) * P],
                                          start=False, stop=(q % 2 == 1), skip_group_check=True)
                    m.then_inc(p.done("sbi"), 1)

                def sbo(qb):
                    c = take("sbo", qb)
                    pe.wait_ge(*p.after("scalar", "sbe", 1))
                    for q in range(4):
                        h = head_of(1, q)
                        for k in range(qb + 1):
                            a = (pr2[1][:, q * S + qb * P:q * S + (qb + 1) * P] if k == 0
                                 else pr2[0][:, q * P:(q + 1) * P])
                            m = pe.matmul(c[:, h * 64:(h + 1) * 64], a, values(1, h, k), start=(q == 0 and k == 0),
                                          stop=(q == 3 and k == qb), skip_group_check=True)
                    m.then_inc(p.done("sbo"), 1)

                def fc():
                    c = take("fc")
                    pe.wait_ge(*p.after("vector", "ff_c"))
                    pe.matmul(c[:, 0:4], triu, fy[:, 2, 0, :], start=True, stop=False, skip_group_check=True)
                    pe.matmul(c[:, 4:8], ones, fy[:, 2, 0, :], start=False, stop=False, skip_group_check=True)
                    pe.matmul(c[:, 4:8], triu, fy[:, 2, 1, :], start=False, stop=True, skip_group_check=True).then_inc(p.done("fc"), 1)

                def fb():
                    c = take("fb")
                    for q in range(4):
                        h = head_of(FOX, q)
                        row = [fy[:, 2, r, h:h + 1].broadcast_to([P, P]) for r in range(R)]
                        pe.matmul(c[:, q * S:q * S + P], row[0], triu, start=(q % 2 == 0), stop=False,
                                  skip_group_check=True)
                        pe.matmul(c[:, q * S + P:(q + 1) * S], row[0], ones, start=False, stop=False,
                                  skip_group_check=True)
                        m = pe.matmul(c[:, q * S + P:(q + 1) * S], row[1], triu, start=False, stop=(q % 2 == 1),
                                      skip_group_check=True)
                    m.then_inc(p.done("fb"), 1)

                def sc2(n, qb):
                    c = take("sc2", n, qb)
                    pe.wait_ge(*p.after("scalar", "qk2T", *((n, 1) if n == MLA else (n,))))
                    nk = keys_of(n, qb)
                    for q in range(4):
                        h = head_of(n, q)
                        m = pe.matmul(c[:, q * S:q * S + nk], head_T(n, h, 0, slice(qb * P, (qb + 1) * P)),
                                      head_T(n, h, 1, slice(0, nk)), start=(q % 2 == 0), stop=(q % 2 == 1),
                                      skip_group_check=True)
                    m.then_inc(p.done("sc2"), 1)

                def p2T(n, qb):
                    c = take("p2T", n, qb)
                    pe.wait_ge(*p.after("scalar", "sc2", n, qb))
                    src = pr2[buf_of(n, qb)]
                    transposes(c, [src[:, i * P:(i + 1) * P] for i in range(4 * keys_of(n, qb) // P)]).then_inc(p.done("p2T"), 1)

                def pv2(n, qb):
                    c = take("pv2", n, qb)
                    pe.wait_ge(*p.after("scalar", "p2T", n, qb))
                    nt = keys_of(n, qb) // P
                    for q in range(4):
                        h = head_of(n, q)
                        for k in range(nt):
                            i = q * nt + k
                            m = pe.matmul(c[:, h * 64:(h + 1) * 64], pt2[buf_of(n, qb)][:, i * P:(i + 1) * P],
                                          values(n, h, k), start=(q == 0 and k == 0),
                                          stop=(q == 3 and k == nt - 1), skip_group_check=True)
                    m.then_inc(p.done("pv2"), 1)

                def yT(n):
                    c = take("yT", n)
                    pe.wait_ge(*p.after("vector", "gy", n))
                    g_0 = B_GATE + n * S
                    transposes(c, [h2[:, r, g_0 + k * P:g_0 + (k + 1) * P] for r in range(R) for k in range(2)]).then_inc(p.done("yT"), 1)

                def gT(r):
                    c = take("gT", r)
                    pe.wait_ge(*p.after("vector", "drain_v", "br01"))
                    transposes(c, [merged[:, r, k * P:(k + 1) * P] for k in range(KD)]).then_inc(p.done("gT"), 1)

                return dict(xT=xT, ckT=ckT, mrT=mrT, qk2T=qk2T, sbz=sbz, sbi=sbi, sbo=sbo, fc=fc, fb=fb, sc2=sc2,
                            p2T=p2T, pv2=pv2, yT=yT, gT=gT, mm=mm, memT=memT, hT=hT, cwT=cwT, gc=gc_, stat=stat, dec=dec, kk=kk, x1=x1, kT=kT, vT=vT,
                            invY=invY, invZ=invZ, kq=kq, u=u_, st=st_, ks=ks, o=o_, iT=iT, raw=raw_, qT=qT, kaT=kaT_,
                            sc=sc, pT=pT, pv=pv, mT=mT)

            run(pe, "tensor", handlers)

        @block.scalar
        def _(act):
            A = act.activation

            def handlers(p):
                def split(u):
                    _, w, _, nk, _, _ = UNITS[p.sec][u]
                    n = nk * w["n"]
                    act.wait_ge(*slot_value(p.sec, p.l, u))
                    if p.sec != "mem" or u >= SPLIT_SLOTS:
                        act.wait_ge(*unit_before(p, "tensor", "mm", u, SPLIT_SLOTS))
                    A(w_hi[:, u % SPLIT_SLOTS, 0:n], raw[:, u % RAW_SLOTS, 0:n], ACT.Copy).then_inc(p.done("split"), 1)

                def tile_in(name):
                    names = [x for x, _ in TILES[p.sec]]
                    last = max(u for u, x in enumerate(UNITS[p.sec]) if x[0] == name)
                    act.wait_ge(*p.after("tensor", "mm", last))
                    i = names.index(name)
                    return bulk[i % 2], dict(TILES[p.sec])[name]

                def rows(b, n):
                    return b[:, :].rearrange("p (r n) -> p r n", r=R)[:, :, 0:n]

                def drain(name):
                    b, w = tile_in(name)
                    if name[:3] == "mkv":
                        return A(mkv[:, int(name[3]), :, :], rows(b, 512), ACT.Copy).then_inc(p.done("drain_s"), 1)
                    if name == "qi":
                        return A(pi[:, :, 0:512], rows(b, 512), ACT.Copy).then_inc(p.done("drain_s"), 1)
                    if name == "ki":
                        return A(pi[:, :, 512:584], rows(b, 72), ACT.Copy).then_inc(p.done("drain_s"), 1)
                    if name == "kv":
                        return A(pq[:, :, 1024:1536], rows(b, 512), ACT.Copy).then_inc(p.done("drain_s"), 1)
                    if name[:2] == "qa":
                        c = int(name[2]) * 512
                        return A(pq[:, :, c:c + 512], rows(b, 512), ACT.Copy).then_inc(p.done("drain_s"), 1)
                    if name[:2] in ("za", "zb"):
                        c = int(name[2]) * 512
                        dst = (g0 if name[1] == "a" else g1)[:, :, c:c + 512]
                        return A(dst, rows(b, 512), ACT.Silu).then_inc(p.done("drain_s"), 1)
                    if name[0] == "g" and p.sec == "one":
                        prev = {"g01": "g00", "g10": "g01", "g11": "g10"}.get(name)
                        if prev:
                            act.wait_ge(*p.after("vector", "gmul", prev))
                        return A(gain2[:, :].rearrange("p (r n) -> p r n", r=R), rows(b, 512), ACT.Sigmoid).then_inc(p.done("drain_s"), 1)
                    return drain_two(name, b, w)

                def drain_two(name, b, w):
                    n = w["n"]
                    if name[0] == "h":
                        return A(h2[:, :, w["col"]:w["col"] + n], rows(b, n), ACT.Copy).then_inc(p.done("drain_s"), 1)
                    if name == "mr":
                        return A(h2[:, :, B_MR:B_MR + n], rows(b, n), ACT.Copy).then_inc(p.done("drain_s"), 1)
                    if name == "qb":
                        return A(q2[:, :, :], rows(b, n), ACT.Copy).then_inc(p.done("drain_s"), 1)
                    if name == "kvb":
                        return A(kv2[:, :, :], rows(b, n), ACT.Copy).then_inc(p.done("drain_s"), 1)
                    if name[:2] == "gz":
                        return A(h2[:, :, w["col"]:w["col"] + n], rows(b, n), ACT.Silu).then_inc(p.done("drain_s"), 1)
                    if name[:2] == "mu":
                        return A(mg[:, :, w["col"]:w["col"] + n], rows(b, n), ACT.Sigmoid).then_inc(p.done("drain_s"), 1)
                    raise NotImplementedError(name)

                def conv_silu(w, g):
                    act.wait_ge(*p.after("vector", "tap", w, g))
                    if (w, g) == (0, 1):
                        act.wait_ge(*p.after("tensor", "o", 0, 1))
                    A(cs[:, w, :, :], cv[:, :, :], ACT.Silu).then_inc(p.done("conv"), 1)

                def conv_tap(w, g):
                    b, _ = tile_in(f"c{w}{g}")
                    if (w, g) != (0, 0):
                        act.wait_ge(*p.after("scalar", "conv", *CONV_BEFORE[(w, g)]))
                    for j in range(4):
                        c = 3 * 24 + w * 8 + g * 4 + j
                        ins = A(cv[:, j, :], b[:, j * S:(j + 1) * S], ACT.Copy, scale=taps[:, c:c + 1])
                    ins.then_inc(p.done("tap"), 1)

                def norm():
                    act.wait_ge(*p.after("vector", "norm_a"))
                    rsq(nrm[:, 0, :], nrm[:, 1, :]).then_inc(p.done("norm"), 1)

                def rsq(src, dst):
                    A(dst, src, ACT.Ln).then_inc(p.own, 1)
                    act.wait_ge(*p.last())
                    return A(dst, dst, ACT.Exp, scale=-0.5)

                def ba_b():
                    act.wait_ge(*p.after("vector", "ba_a"))
                    A(be[:, :, :], ba[:, :, 0:8], ACT.Exp, scale=-1.0)
                    A(ea, a_log, ACT.Exp)
                    A(eb[:, :, :], ay[:, 1, :, :], ACT.Exp, scale=-1.0).then_inc(p.own, 1)
                    act.wait_ge(*p.last())
                    A(eb[:, :, :], eb[:, :, :], ACT.Ln, bias=1.0).then_inc(p.done("ba_b"), 1)

                def gc_b():
                    act.wait_ge(*p.after("vector", "gc"))
                    A(egc[:, :, :], gc[:, :, :], ACT.Exp)
                    A(wl[:, 0, :], wl[:, 1, :], ACT.Exp).then_inc(p.done("gc_b"), 1)

                def stat(w, g):
                    act.wait_ge(*p.after("scalar", "conv", w, g))
                    if (w, g) != (0, 0):
                        act.wait_ge(*p.after("tensor", "stat", *((0, g) if w else (1, 0))))
                    A(sq[:, :, :], cs[:, w, :, :], ACT.Square).then_inc(p.done("stat"), 1)

                def rn(g):
                    act.wait_ge(*p.after("vector", "stat", 1, g))
                    rsq(s2[:, :, :, :], ss[:, :, :, :]).then_inc(p.done("rn"), 1)

                def dec_b(g, r):
                    act.wait_ge(*p.after("vector", "dec", g, r))
                    A(dt_[:, r, :, :], dt_[:, r, :, :], ACT.Exp).then_inc(p.done("dec_b"), 1)

                def x1(g, r):
                    act.wait_ge(*p.after("tensor", "x1", g, r))
                    A(xx[:, r, :, :], heads(half("x1", g, r)[:, 0:512]), ACT.Copy).then_inc(p.done("x1"), 1)

                def half(*key):
                    return chain[half_of[(p.sec,) + key]]

                def u_(g, r):
                    act.wait_ge(*p.after("tensor", "u", g, r))
                    A(uu[:, r, :, :], heads(half("u", g, r)[:, 0:512]), ACT.Copy).then_inc(p.done("u"), 1)

                def st_(g):
                    act.wait_ge(*p.after("tensor", "st", g))
                    A(st[:, :, :], heads(half("st", g)[:, 0:512]), ACT.Copy).then_inc(p.done("st"), 1)

                def onorm():
                    act.wait_ge(*p.after("vector", "onorm_a"))
                    rsq(so[:, 0, :, :], so[:, 1, :, :]).then_inc(p.done("onorm"), 1)

                def kinorm():
                    act.wait_ge(*p.after("vector", "kinorm_a"))
                    rsq(kn[:, 0, :], kn[:, 1, :]).then_inc(p.done("kinorm"), 1)

                def iT(r):
                    act.wait_ge(*p.after("tensor", "iT", r))
                    if r == 0:
                        act.wait_ge(*p.after("tensor", "o", 1, 1))
                    c = half("iT", r)
                    A(qiT[:, :, r * P:(r + 1) * P], heads(c[:, 0:512]), ACT.Copy)
                    A(kiT[:, r * P:(r + 1) * P], c[:, 512:640], ACT.Copy).then_inc(p.done("iT"), 1)

                def raw_(qb, part):
                    act.wait_ge(*p.after("tensor", "raw", qb, part))
                    prev = {(1, 0): (0, 0), (1, 1): (1, 0)}.get((qb, part))
                    if prev:
                        act.wait_ge(*p.after("vector", "raw", *prev))
                    A(rl, half("raw", qb, part)[:, :], ACT.Relu).then_inc(p.done("raw"), 1)

                def qT(r):
                    act.wait_ge(*p.after("tensor", "qT", r))
                    A(qaT[:, :, r * P:(r + 1) * P], heads(half("qT", r)[:, :], 8), ACT.Copy).then_inc(p.done("qT"), 1)

                def kaT_():
                    act.wait_ge(*p.after("tensor", "kaT"))
                    A(kaT[:, :, :].rearrange("p a n -> p (a n)"), half("kaT")[:, 0:512], ACT.Copy).then_inc(p.done("kaT"), 1)

                def sc(kv, qb):
                    act.wait_ge(*p.after("vector", "sc", kv, qb))
                    nk = P * (qb + 1)
                    if kv:
                        act.wait_ge(*p.after("vector", "pv", 0, qb))
                    for j in range(4):
                        v = pr[qb][:, j * nk:(j + 1) * nk]
                        ins = A(v, v, ACT.Exp, bias=mx[qb][:, j:j + 1], accum_out=rs[qb][:, j:j + 1])
                    ins.then_inc(p.done("sc"), 1)

                def pT(kv, qb):
                    act.wait_ge(*p.after("tensor", "pT", kv, qb))
                    if kv:
                        act.wait_ge(*p.after("tensor", "pv", 0, qb))
                    n = 512 * (qb + 1)
                    A(pt[qb][:, 0:n], half("pT", kv, qb)[:, 0:n], ACT.Copy).then_inc(p.done("pT"), 1)

                def tables():
                    act.wait_ge(*p.after("vector", "tables_a"))
                    A(sin_t[:, :, :].rearrange("p r n -> p (r n)"), ang[:, 3, :], ACT.Sin)
                    A(ang[:, 4, :], ang[:, 3, :], ACT.Sin, scale=0.5).then_inc(p.done("tables"), 1)

                def lat_():
                    act.wait_ge(*p.after("vector", "lat_a"))
                    rsq(lat[:, 0, :, :], lat[:, 1, :, :]).then_inc(p.done("lat"), 1)

                def qk2T(n, part=0):
                    act.wait_ge(*p.after("tensor", "qk2T", *((n, part) if part else (n,))))
                    c = half("qk2T", *((n, part) if part else (n,)))
                    if n == MEM:
                        act.wait_ge(*p.after("tensor", "sbz", 1))
                    if n == MLA:
                        act.wait_ge(*p.after("tensor", "sc2", FOX, 1))
                        dst = t_parts(n)[part][0:96]
                        return A(dst.rearrange("p a n -> p (a n)"), c[0:96, :], ACT.Copy).then_inc(p.done("qk2T"), 1)
                    reg = reg_a if n == FOX else reg_b
                    A(reg[:, 0:1024], c[:, :], ACT.Copy).then_inc(p.done("qk2T"), 1)

                def sbl(k):
                    act.wait_ge(*p.after("vector", "sbz", k))
                    x = pt2[1 - k]
                    A(x, x, ACT.Exp, scale=-1.0).then_inc(p.own, 1)
                    act.wait_ge(*p.last())
                    A(x, x, ACT.Ln, bias=1.0).then_inc(p.done("sbl"), 1)

                def sbe(k):
                    act.wait_ge(*p.after("vector", "sbi", k))
                    A(pr2[1 - k], pr2[1 - k], ACT.Exp).then_inc(p.done("sbe"), 1)

                def ff():
                    act.wait_ge(*p.after("vector", "ff_a"))
                    A(fy[:, 1, :, :], fy[:, 1, :, :], ACT.Exp, scale=-1.0).then_inc(p.own, 1)
                    act.wait_ge(*p.last())
                    A(fy[:, 1, :, :], fy[:, 1, :, :], ACT.Ln, bias=1.0).then_inc(p.done("ff"), 1)

                def sc2(n, qb):
                    act.wait_ge(*p.after("vector", "sc2", n, qb))
                    nk, b = keys_of(n, qb), buf_of(n, qb)
                    for q in range(4):
                        x, h = pr2[b][:, q * nk:(q + 1) * nk], head_of(n, q)
                        ins = A(x, x, ACT.Exp, bias=mx2[qb][:, q:q + 1], accum_out=rs2[qb][:, h:h + 1])
                    ins.then_inc(p.done("sc2"), 1)

                def p2T(n, qb):
                    act.wait_ge(*p.after("tensor", "p2T", n, qb))
                    prev = user_before(n, qb)
                    if prev:
                        act.wait_ge(*p.after("tensor", "pv2", *prev))
                    k = 4 * keys_of(n, qb)
                    A(pt2[buf_of(n, qb)][:, 0:k], half("p2T", n, qb)[:, 0:k], ACT.Copy).then_inc(p.done("p2T"), 1)

                def ln_s():
                    act.wait_ge(*p.after("vector", "ln_a"))
                    rsq(lnm[:, 2, :], lnm[:, 3, :]).then_inc(p.done("ln_s"), 1)

                return dict(lat=lat_, qk2T=qk2T, sbl=sbl, sbe=sbe, ff=ff, sc2=sc2, p2T=p2T, ln_s=ln_s,
                            split=split, drain_s=drain, tap=conv_tap, conv=conv_silu, norm=norm, ba_b=ba_b, gc_b=gc_b,
                            stat=stat, rn=rn, dec_b=dec_b, x1=x1, u=u_, st=st_, onorm=onorm, kinorm=kinorm, iT=iT,
                            raw=raw_, qT=qT, kaT=kaT_, sc=sc, pT=pT, tables=tables)

            run(act, "scalar", handlers)

        @block.vector
        def _(v):
            TT, TS, STT = v.tensor_tensor, v.tensor_scalar, v.scalar_tensor_tensor

            def handlers(p):
                def half(*key):
                    return chain[half_of[(p.sec,) + key]]

                def flat(x):
                    return x.rearrange("p a n -> p (a n)")

                def newton(y, x, tmp):
                    TT(tmp, y, y, ALU.mult).then_inc(p.own, 1)
                    v.wait_ge(*p.last())
                    TT(tmp, tmp, x, ALU.mult).then_inc(p.own, 1)
                    v.wait_ge(*p.last())
                    TS(tmp, tmp, -0.5, 1.5, ALU.mult, ALU.add).then_inc(p.own, 1)
                    v.wait_ge(*p.last())
                    TT(y, y, tmp, ALU.mult).then_inc(p.own, 1)
                    v.wait_ge(*p.last())

                def split_T(c, step, r, hi, lo, k0, nk, base=0):
                    src = c[:, base:base + nk * P].rearrange("p (k n) -> p k n", k=nk)
                    rr = slice(r * P, (r + 1) * P)
                    v.tensor_copy(hi[:, k0:k0 + nk, rr], src).then_inc(p.own, 1)
                    v.wait_ge(*p.last())
                    return TT(lo[:, k0:k0 + nk, rr], src, hi[:, k0:k0 + nk, rr].bitcast(F32), ALU.subtract)

                def memT(r):
                    v.wait_ge(*p.after("tensor", "memT", r))
                    split_T(half("memT", r), "memT", r, hT_hi, hT_lo, 0, KD).then_inc(p.done("memT"), 1)

                def tables_a():
                    v.wait_ge(const_in, 48)
                    pf = ang[:, 0, 0:4]
                    v.tensor_copy(pf, pos_i[:, :, :].rearrange("p a r -> p (a r)")).then_inc(p.own, 1)
                    v.wait_ge(*p.last())
                    for r in range(R):
                        TS(ang[:, 1, r * 40:r * 40 + 24], cst[:, K_FREQ:K_FREQ + 24], ang[:, 0, r:r + 1], None, ALU.mult)
                        TS(ang[:, 1, r * 40 + 24:r * 40 + 40], cst[:, K_FREQ + 24:K_FREQ + 40],
                                  ang[:, 0, 2 + r:3 + r], None, ALU.mult).then_inc(p.own, 1)
                        v.wait_ge(*p.last())
                    two_pi = 2 * np.pi
                    c1 = 6.28125
                    c2 = float(np.float32(np.round((two_pi - c1) * 2 ** 24) / 2 ** 24))
                    c3 = float(two_pi - c1 - c2)
                    magic = 1.5 * 2 ** 23
                    TS(ang[:, 2, :], ang[:, 1, :], float(1 / two_pi), magic, ALU.mult, ALU.add).then_inc(p.own, 1)
                    v.wait_ge(*p.last())
                    TS(ang[:, 2, :], ang[:, 2, :], -magic, None, ALU.add).then_inc(p.own, 1)
                    v.wait_ge(*p.last())
                    STT(ang[:, 3, :], ang[:, 2, :], -c1, ang[:, 1, :], ALU.mult, ALU.add).then_inc(p.own, 1)
                    v.wait_ge(*p.last())
                    STT(ang[:, 3, :], ang[:, 2, :], -c2, ang[:, 3, :], ALU.mult, ALU.add).then_inc(p.own, 1)
                    v.wait_ge(*p.last())
                    STT(ang[:, 3, :], ang[:, 2, :], -c3, ang[:, 3, :], ALU.mult, ALU.add).then_inc(p.own, 1)
                    v.wait_ge(*p.last())
                    pi_ = 3.1415925
                    TS(ang[:, 3, :], ang[:, 3, :], pi_, -pi_, ALU.min, ALU.max).then_inc(p.done("tables_a"), 1)

                def tables_c():
                    v.wait_ge(*p.after("scalar", "tables"))
                    TT(ang[:, 4, :], ang[:, 4, :], ang[:, 4, :], ALU.mult).then_inc(p.own, 1)
                    v.wait_ge(*p.last())
                    TS(cos_t[:, :, :].rearrange("p r n -> p (r n)"), ang[:, 4, :], -2.0, 1.0,
                                  ALU.mult, ALU.add).then_inc(p.done("tables_c"), 1)
                    v.wait_ge(*p.here("tables_c"))

                def cwT():
                    v.wait_ge(*p.after("tensor", "cwT"))
                    c = half("cwT")
                    v.tensor_copy(par1[:, :, 0:96], c[:, 0:2 * P].rearrange("p (l n) -> p l n", l=DEPTH)[:, :, 0:96]).then_inc(p.done("cwT"), 1)
                    v.wait_ge(*p.here("cwT"))

                def params():
                    ins = v.tensor_copy(now1[:, :], par1[:, bass.ds(p.l, 1), :].rearrange("p a n -> p (a n)"))
                    ins.then_inc(p.done("params"), 1)
                    v.wait_ge(*p.here("params"))

                def norm_a():
                    v.wait_ge(x_in, 16)
                    for r in range(R):
                        ins = v.tensor_tensor_reduce(h_nat[:, r, :], xs[:, r, :], xs[:, r, :], 1.0, 0.0,
                                                     ALU.mult, ALU.add, nrm[:, 2, r:r + 1])
                    ins.then_inc(p.own, 1)
                    v.wait_ge(*p.last())
                    TS(nrm[:, 0, :], nrm[:, 2, :], 1.0 / D, EPS, ALU.mult, ALU.add).then_inc(p.done("norm_a"), 1)

                def norm_c():
                    v.wait_ge(*p.after("scalar", "norm"))
                    newton(nrm[:, 1, :], nrm[:, 0, :], nrm[:, 3, :])
                    v.wait_ge(gain_in, 16 * (p.l + 1) if p.sec == "one" else 16 * (DEPTH + 1))
                    for r in range(R):
                        dst = h_nat if p.sec == "one" else xs
                        ins = STT(dst[:, r, :], xs[:, r, :], nrm[:, 1, r:r + 1], gain[:, :], ALU.mult, ALU.mult)
                        if r == 0:
                            ins.then_inc(p.own, 1)
                            v.wait_ge(*p.last())
                    ins.then_inc(p.done("norm_c"), 1)
                    v.wait_ge(*p.here("norm_c"))

                def hT(r):
                    v.wait_ge(*p.after("tensor", "hT", r))
                    split_T(half("hT", r), "hT", r, hT_hi, hT_lo, 0, KD).then_inc(p.done("hT"), 1)

                def tile_in(name):
                    names = [x for x, _ in TILES[p.sec]]
                    v.wait_ge(*p.after("tensor", "mm", max(u for u, x in enumerate(UNITS[p.sec]) if x[0] == name)))
                    return bulk[names.index(name) % 2]

                def rows(b, n):
                    return b[:, :].rearrange("p (r n) -> p r n", r=R)[:, :, 0:n]

                def drain(name):
                    b = tile_in(name)
                    if name == "ba":
                        v.tensor_copy(ba[:, :, :], rows(b, 16)).then_inc(p.done("drain_v"), 1)
                        v.wait_ge(*p.here("drain_v"))
                        return None
                    if p.sec == "one":
                        xv = xs[:, :, int(name[1]) * 512:int(name[1]) * 512 + 512]
                        TT(xv, xv, rows(b, 512), ALU.add).then_inc(p.done("drain_v"), 1)
                        v.wait_ge(*p.here("drain_v"))
                        return None
                    drain_two(name, b)

                def drain_two(name, b):
                    c = int(name[-1]) * 512
                    if name[0] == "o":
                        xv = xs[:, :, c:c + 512]
                        STT(xv, xv, ALPHA, rows(b, 512), ALU.mult, ALU.add).then_inc(p.done("drain_v"), 1)
                        v.wait_ge(*p.here("drain_v"))
                        return None
                    n = int(name[2])
                    m = mg[:, :, n * D + c:n * D + c + 512]
                    if n == 1:
                        v.wait_ge(*p.after("scalar", "drain_s", "mu7"))
                        TT(merged[:, :, c:c + 512], m, rows(b, 512), ALU.mult).then_inc(p.done("drain_v"), 1)
                        v.wait_ge(*p.here("drain_v"))
                        return None
                    TT(m, m, rows(b, 512), ALU.mult).then_inc(p.own, 1)
                    v.wait_ge(*p.last())
                    TT(merged[:, :, c:c + 512], merged[:, :, c:c + 512], m, ALU.add).then_inc(p.done("drain_v"), 1)
                    v.wait_ge(*p.here("drain_v"))

                def gmul(name):
                    v.wait_ge(*p.after("scalar", "drain_s", name))
                    c = int(name[2]) * 512
                    gv = (g0 if name[1] == "0" else g1)[:, :, c:c + 512]
                    TT(gv, gv, gain2[:, :].rearrange("p (r n) -> p r n", r=R), ALU.mult).then_inc(p.done("gmul"), 1)
                    v.wait_ge(*p.here("gmul"))

                def tap(w, g):
                    v.wait_ge(*p.after("scalar", "tap", w, g))
                    b = tile_in(f"c{w}{g}")
                    for k in range(3):
                        back = 3 - k
                        for j in range(4):
                            c = k * 24 + w * 8 + g * 4 + j
                            ins = STT(cv[:, j, back:S], b[:, j * S:(j + 1) * S - back], taps[:, c:c + 1],
                                      cv[:, j, back:S], ALU.mult, ALU.add)
                            if k < 2 or j < 3:
                                ins.then_inc(p.own, 1)
                                v.wait_ge(*p.last())
                    ins.then_inc(p.done("tap"), 1)

                def ba_a():
                    y = ay[:, 0, :, :]
                    TT(y, ba[:, :, 8:16], over(dt_bias, R), ALU.add).then_inc(p.own, 1)
                    v.wait_ge(*p.last())
                    STT(ay[:, 1, :, :], y, -1.0, y, ALU.mult, ALU.max).then_inc(p.done("ba_a"), 1)

                def ba_c():
                    v.wait_ge(*p.after("scalar", "ba_b"))
                    TS(be[:, :, :], be[:, :, :], 1.0, None, ALU.add).then_inc(p.own, 1)
                    v.wait_ge(*p.last())
                    v.reciprocal(be[:, :, :], be[:, :, :]).then_inc(p.own, 1)
                    v.wait_ge(*p.last())
                    TS(ay[:, 0, :, :], ay[:, 0, :, :], 0.0, None, ALU.max).then_inc(p.own, 1)
                    v.wait_ge(*p.last())
                    TT(ay[:, 0, :, :], ay[:, 0, :, :], eb[:, :, :], ALU.add).then_inc(p.own, 1)
                    v.wait_ge(*p.last())
                    TS(ea, ea, -1.0, None, ALU.mult).then_inc(p.own, 1)
                    v.wait_ge(*p.last())
                    TT(gdec[:, :, :], ay[:, 0, :, :], over(ea, R), ALU.mult).then_inc(p.done("ba_c"), 1)
                    v.wait_ge(*p.here("ba_c"))

                def gc_():
                    v.wait_ge(*p.after("tensor", "gc"))
                    c = half("gc")
                    v.tensor_copy(gc[:, :, :].rearrange("p r n -> p (r n)"), c[:, 0:16]).then_inc(p.own, 1)
                    v.wait_ge(*p.last())
                    TT(wl[:, 1, :], c[:, 16:24], gc[:, 0, :], ALU.subtract).then_inc(p.done("gc"), 1)
                    v.wait_ge(*p.here("gc"))

                def stat(w, g):
                    v.wait_ge(*p.after("tensor", "stat", w, g))
                    TS(s2[:, w, :, :].rearrange("p r n -> p (r n)"), half("stat", w, g)[:, 0:8], EPS, None,
                                  ALU.add).then_inc(p.done("stat"), 1)
                    v.wait_ge(*p.here("stat"))

                def rn(g):
                    v.wait_ge(*p.after("scalar", "rn", g))
                    newton(f3(ss), f3(s2), f3(s3))
                    hs = slice(4 * g, 4 * g + 4)
                    TT(av[:, :, :], be[:, :, hs], ss[:, 1, :, :], ALU.mult).then_inc(p.own, 1)
                    v.wait_ge(*p.last())
                    TS(ss[:, 0, :, :], ss[:, 0, :, :], float(P) ** -0.5, None, ALU.mult).then_inc(p.own, 1)
                    v.wait_ge(*p.last())
                    v.wait_ge(*p.after("scalar", "gc_b"))
                    TT(bke, av[:, 1, :], egc[:, 1, hs], ALU.mult).then_inc(p.own, 1)
                    v.wait_ge(*p.last())
                    TT(wk, ss[:, 1, 0, :], wl[:, 0, hs], ALU.mult).then_inc(p.done("rn"), 1)
                    v.wait_ge(*p.here("rn"))

                def f3(x):
                    return x.rearrange("p a b c -> p (a b c)")

                def dec(g, r):
                    v.wait_ge(*p.after("tensor", "dec", g, r))
                    c = half("dec", g, r)
                    for j in range(4):
                        ins = TS(dt_[:, r, j, :], c[:, j * P:(j + 1) * P], gc[:, r, 4 * g + j:4 * g + j + 1], 0.0,
                                 ALU.subtract, ALU.min)
                    ins.then_inc(p.done("dec"), 1)

                def dec_c(g, r):
                    v.wait_ge(*p.after("scalar", "dec_b", g, r))
                    for j in range(4):
                        ins = STT(dt_[:, r, j, :], dt_[:, r, j, :], ss[:, 1, r, j:j + 1], triu, ALU.mult, ALU.mult)
                    ins.then_inc(p.own, 1)
                    v.wait_ge(*p.last())
                    TT(yy[:, r, :, :], dt_[:, r, :, :], heads(half("dec", g, r)[:, 512:1024]), ALU.mult).then_inc(p.done("dec_c"), 1)
                    v.wait_ge(*p.here("dec_c"))

                def kk(g, r):
                    v.wait_ge(*p.after("tensor", "kk", g, r))
                    TT(lt[:, r, :, :], yy[:, r, :, :], heads(half("kk", g, r)[:, 0:512]), ALU.mult).then_inc(p.own, 1)
                    v.wait_ge(*p.last())
                    TT(xt[:, r, :, :], lt[:, r, :, :], over(cst[:, K_PAIR:K_PAIR + P], 4), ALU.mult).then_inc(p.own, 1)
                    v.wait_ge(*p.last())
                    TT(xt[:, r, :, :], over(ident, 4), xt[:, r, :, :], ALU.subtract).then_inc(p.done("kk"), 1)
                    v.wait_ge(*p.here("kk"))

                def kT(g):
                    v.wait_ge(*p.after("tensor", "kT", g))
                    TT(kd[:, :, :], heads(half("kT", g)[:, 0:512]), bc(wk, P), ALU.mult).then_inc(p.done("kT"), 1)
                    v.wait_ge(*p.here("kT"))

                def vT(g):
                    v.wait_ge(*p.after("tensor", "vT", g))
                    for r in range(R):
                        ins = TT(vb[:, r, :, :], heads(half("vT", g)[:, r * 512:(r + 1) * 512]),
                                 bc(be[:, r, 4 * g:4 * g + 4], P), ALU.mult)
                    ins.then_inc(p.done("vT"), 1)
                    v.wait_ge(*p.here("vT"))

                def invY(g, r, n):
                    v.wait_ge(*p.after("tensor", "invY", g, r, n))
                    m = cst[:, K_LEVEL + n * P:K_LEVEL + (n + 1) * P]
                    TT(yy[:, r, :, :], heads(half("invY", g, r, n)[:, 0:512]), over(m, 4), ALU.mult).then_inc(p.done("invY"), 1)
                    v.wait_ge(*p.here("invY"))

                def invZ(g, r, n):
                    v.wait_ge(*p.after("tensor", "invZ", g, r, n))
                    c = half("invZ", g, r, n)
                    if n < len(LEVELS) - 1:
                        TT(xx[:, r, :, :], xx[:, r, :, :], heads(c[:, 0:512]), ALU.subtract).then_inc(p.own, 1)
                        v.wait_ge(*p.last())
                    TT(xt[:, r, :, :], xt[:, r, :, :], heads(c[:, 512:1024]), ALU.subtract).then_inc(p.done("invZ"), 1)
                    v.wait_ge(*p.here("invZ"))

                def kq(g, r):
                    v.wait_ge(*p.after("tensor", "kq", g, r))
                    TT(lt[:, r, :, :], dt_[:, r, :, :], heads(half("kq", g, r)[:, 0:512]), ALU.mult).then_inc(p.done("kq"), 1)
                    v.wait_ge(*p.here("kq"))

                def ks(g):
                    v.wait_ge(*p.after("tensor", "ks", g))
                    TT(yy[:, 0, :, :], heads(half("ks", g)[:, 0:512]), bc(bke, P), ALU.mult).then_inc(p.own, 1)
                    v.wait_ge(*p.last())
                    TT(vb[:, 1, :, :], vb[:, 1, :, :], yy[:, 0, :, :], ALU.subtract).then_inc(p.done("ks"), 1)
                    v.wait_ge(*p.here("ks"))

                def o_(g, r):
                    v.wait_ge(*p.after("tensor", "o", g, r))
                    c = half("o", g, r)
                    dst = heads(od[:, r, g * 512:(g + 1) * 512])
                    hs = slice(4 * g, 4 * g + 4)
                    if r == 0:
                        TT(dst, heads(c[:, 0:512]), bc(ss[:, 0, 0, :], P), ALU.mult).then_inc(p.done("o"), 1)
                        v.wait_ge(*p.here("o"))
                        return None
                    TT(dst, heads(c[:, 512:1024]), bc(egc[:, 1, hs], P), ALU.mult).then_inc(p.own, 1)
                    v.wait_ge(*p.last())
                    TT(dst, dst, heads(c[:, 0:512]), ALU.add).then_inc(p.own, 1)
                    v.wait_ge(*p.last())
                    TT(dst, dst, bc(ss[:, 0, 1, :], P), ALU.mult).then_inc(p.done("o"), 1)
                    v.wait_ge(*p.here("o"))

                def onorm_a():
                    for r in range(R):
                        t1 = cs[:, r, :, :].rearrange("p a n -> p (a n)")
                        TT(t1, od[:, r, :], od[:, r, :], ALU.mult).then_inc(p.own, 1)
                        v.wait_ge(*p.last())
                        v.tensor_reduce(so[:, 2, r, :], heads(t1, 8), AX, ALU.add).then_inc(p.own, 1)
                        v.wait_ge(*p.last())
                    TS(so[:, 0, :, :], so[:, 2, :, :], 1.0 / P, EPS, ALU.mult, ALU.add).then_inc(p.done("onorm_a"), 1)
                    v.wait_ge(*p.here("onorm_a"))

                def onorm():
                    v.wait_ge(*p.after("scalar", "onorm"))
                    newton(so[:, 1, :, :], so[:, 0, :, :], so[:, 2, :, :])
                    for r in range(R):
                        o8 = heads(od[:, r, :], 8)
                        TT(o8, o8, bc(so[:, 1, r, :], P), ALU.mult).then_inc(p.own, 1)
                        v.wait_ge(*p.last())
                        ins = TT(o8, o8, over(gdn_gain, 8), ALU.mult)
                        if r == 0:
                            ins.then_inc(p.own, 1)
                            v.wait_ge(*p.last())
                    ins.then_inc(p.done("onorm_c"), 1)
                    v.wait_ge(*p.here("onorm_c"))

                def kinorm_a():
                    v.wait_ge(*p.after("scalar", "drain_s", "ki"))
                    for r in range(R):
                        ins = v.tensor_tensor_reduce(kk2[:, r, 0, :], pi[:, r, 512:576], pi[:, r, 512:576], 1.0, 0.0,
                                                     ALU.mult, ALU.add, kn[:, 2, r:r + 1])
                    ins.then_inc(p.own, 1)
                    v.wait_ge(*p.last())
                    TS(kn[:, 0, :], kn[:, 2, :], 1.0 / 64, EPS, ALU.mult, ALU.add).then_inc(p.done("kinorm_a"), 1)

                def rope(x, cos, sin, into=rope_tmp):
                    _, nr, nh, two = x.shape
                    hf = two // 2
                    a, b = x[:, :, :, 0:hf], x[:, :, :, hf:two]

                    def tmp(i):
                        return into[:, i, 0:nr * nh * hf].rearrange("p (r h n) -> p r h n", r=nr, h=nh)

                    def tab(x_):
                        return x_.unsqueeze(2).broadcast_to([P, nr, nh, hf])
                    for i, (m, n) in enumerate(((a, cos), (b, sin), (b, cos), (a, sin))):
                        ins = TT(tmp(i), m, tab(n), ALU.mult)
                    ins.then_inc(p.own, 1)
                    v.wait_ge(*p.last())
                    TT(a, tmp(0), tmp(1), ALU.subtract)
                    return TT(b, tmp(2), tmp(3), ALU.add)

                def rope_i():
                    v.wait_ge(*p.after("scalar", "kinorm"))
                    newton(kn[:, 1, :], kn[:, 0, :], kn[:, 3, :])
                    for r in range(R):
                        ins = STT(pi[:, r, 512:576], pi[:, r, 512:576], kn[:, 1, r:r + 1], idx_gain, ALU.mult, ALU.mult)
                    ins.then_inc(p.own, 1)
                    v.wait_ge(*p.last())
                    v.wait_ge(*p.after("tensor", "o", 1, 1))
                    x = pi[:, :, 0:576].rearrange("p r (h n) -> p r h n", h=9)[:, :, :, 0:16]
                    rope(x, cos_t[:, :, 16:24], sin_t[:, :, 16:24]).then_inc(p.own, 1)
                    v.wait_ge(*p.last())
                    TS(wi[:, :, :], pi[:, :, 576:584], 8 ** -0.5 * 64 ** -0.5, None, ALU.mult)
                    v.sem_clear(topk_step)
                    for c in range(2):
                        ins = v.tensor_copy(kk2[:, :, c, :], pi[:, :, 512:576])
                    ins.then_inc(p.done("rope_i"), 1)
                    v.wait_ge(*p.here("rope_i"))

                def raw_(qb, part):
                    v.wait_ge(*p.after("scalar", "raw", qb, part))
                    nk = P * (qb + 1)
                    per = 1024 // nk
                    for i in range(per):
                        h = part * per + bank_order(i, per)
                        x = rl[:, i * nk:(i + 1) * nk]
                        if h == 0:
                            ins = TS(isc[qb], x, wi[:, qb, 0:1], None, ALU.mult)
                        else:
                            ins = STT(isc[qb], x, wi[:, qb, h:h + 1], isc[qb], ALU.mult, ALU.add)
                        if i < per - 1:
                            ins.then_inc(p.own, 1)
                            v.wait_ge(*p.last())
                    ins.then_inc(p.done("raw"), 1)
                    v.wait_ge(*p.here("raw"))

                def topk(qb):
                    nk = P * (qb + 1)
                    neg = cst[:, K_NEG + P - P * qb:K_NEG + 2 * P]
                    n = qb * (1 + TOPK // 4)
                    TT(isc[qb], isc[qb], neg, ALU.add).then_inc(topk_step, 1)
                    for _ in range(TOPK // 8):
                        v.wait_ge(topk_step, n + 1)
                        v.max(top, isc[qb]).then_inc(topk_step, 1)
                        v.wait_ge(topk_step, n + 2)
                        v.match_replace(isc[qb], top, isc[qb], TAKEN).then_inc(topk_step, 1)
                        n += 2
                    v.wait_ge(topk_step, n + 1)
                    TS(mb[qb], isc[qb], TAKEN, NEG, ALU.not_equal, ALU.mult).then_inc(p.own, 1)
                    v.wait_ge(*p.last())
                    TT(mb[qb], mb[qb], neg, ALU.add).then_inc(p.done("topk"), 1)
                    v.wait_ge(*p.here("topk"))

                def rope_a():
                    for name in ("kv", "qa0", "qa1"):
                        v.wait_ge(*p.after("scalar", "drain_s", name))
                    x = pq[:, :, 0:1280].rearrange("p r (h n) -> p r h n", h=10)[:, :, :, 0:32]
                    rope(x, cos_t[:, :, 0:16], sin_t[:, :, 0:16]).then_inc(p.done("rope_a"), 1)
                    v.wait_ge(*p.here("rope_a"))

                def sc(kv, qb):
                    v.wait_ge(*p.after("tensor", "sc", kv, qb))
                    if kv:
                        v.wait_ge(*p.after("tensor", "pT", 0, qb))
                    nk = P * (qb + 1)
                    x = heads(pr[qb][:, 0:4 * nk])
                    STT(x, heads(half("sc", kv, qb)[:, 0:4 * nk]), float(P) ** -0.5, over(mb[qb], 4),
                               ALU.mult, ALU.add).then_inc(p.own, 1)
                    v.wait_ge(*p.last())
                    v.tensor_reduce(mx[qb], x, AX, ALU.max).then_inc(p.own, 1)
                    v.wait_ge(*p.last())
                    TS(mx[qb], mx[qb], -1.0, None, ALU.mult).then_inc(p.done("sc"), 1)
                    v.wait_ge(*p.here("sc"))

                def pv(kv, qb):
                    v.wait_ge(*p.after("tensor", "pv", kv, qb))
                    v.wait_ge(*p.after("scalar", "sc", kv, qb))
                    v.reciprocal(rs[qb], rs[qb]).then_inc(p.own, 1)
                    v.wait_ge(*p.last())
                    dst = heads(pq[:, qb, kv * 512:(kv + 1) * 512])
                    TT(dst, heads(half("pv", kv, qb)[:, 0:512]), bc(rs[qb], P), ALU.mult).then_inc(p.done("pv"), 1)
                    v.wait_ge(*p.here("pv"))

                def mix(r):
                    TT(g0[:, r, :], g0[:, r, :], pq[:, r, 0:D], ALU.mult).then_inc(p.own, 1)
                    v.wait_ge(*p.last())
                    TT(g1[:, r, :], g1[:, r, :], od[:, r, :], ALU.mult).then_inc(p.own, 1)
                    v.wait_ge(*p.last())
                    TT(g0[:, r, :], g0[:, r, :], g1[:, r, :], ALU.add).then_inc(p.done("mix"), 1)
                    v.wait_ge(*p.here("mix"))

                def mT(r):
                    v.wait_ge(*p.after("tensor", "mm", max(u for u, x in enumerate(UNITS["one"]) if x[0] == "g11")))
                    v.wait_ge(*p.after("tensor", "mT", r))
                    split_T(half("mT", r), "mT", r, hT_hi, hT_lo, 0, KD).then_inc(p.done("mT"), 1)

                def params2():
                    v.tensor_copy(now2[:, :], par2[:, bass.ds(p.l, 1), :].rearrange("p a n -> p (a n)")).then_inc(p.own, 1)
                    v.wait_ge(*p.last())
                    v.tensor_copy(gain2[:, :], mkv[:, bass.ds(p.l, 1), :, :].rearrange("p a r n -> p (a r n)")).then_inc(p.done("params2"), 1)
                    v.wait_ge(*p.here("params2"))

                def xT(r):
                    v.wait_ge(*p.after("tensor", "xT", r))
                    split_T(half("xT", r), "xT", r, hT_hi, hT_lo, 0, KD).then_inc(p.done("xT"), 1)

                def lat_a():
                    v.wait_ge(*p.after("scalar", "drain_s", "h1"))
                    for i, (c, n) in enumerate(((0, 384), (384, 256))):
                        for r in range(R):
                            ins = v.tensor_tensor_reduce(reg_a[:, (2 * i + r) * 512:(2 * i + r) * 512 + n],
                                                         h2[:, r, c:c + n], h2[:, r, c:c + n],
                                                         1.0, 0.0, ALU.mult, ALU.add, lat[:, 2, i, r:r + 1])
                    ins.then_inc(p.own, 1)
                    v.wait_ge(*p.last())
                    TS(lat[:, 0, 0, :], lat[:, 2, 0, :], 1.0 / 384, EPS, ALU.mult, ALU.add)
                    TS(lat[:, 0, 1, :], lat[:, 2, 1, :], 1.0 / 256, EPS, ALU.mult, ALU.add).then_inc(p.done("lat_a"), 1)

                def lat_c():
                    v.wait_ge(*p.after("scalar", "lat"))
                    newton(lat[:, 1, :, :], lat[:, 0, :, :], lat[:, 3, :, :])
                    for i, (c, n, gn) in enumerate(((0, 384, q_gain), (384, 256, kv_gain))):
                        for r in range(R):
                            ins = STT(h2[:, r, c:c + n], h2[:, r, c:c + n], lat[:, 1, i, r:r + 1], gn, ALU.mult, ALU.mult)
                    ins.then_inc(p.done("lat_c"), 1)
                    v.wait_ge(*p.here("lat_c"))

                def ckT(r):
                    v.wait_ge(*p.after("tensor", "ckT", r))
                    split_T(half("ckT", r), "ckT", r, sT_hi, sT_lo, 0, 5).then_inc(p.done("ckT"), 1)

                def mrT():
                    v.wait_ge(*p.after("tensor", "mrT"))
                    v.tensor_copy(sT_hi[:, 5, :], half("mrT")[:, 0:S]).then_inc(p.own, 1)
                    v.wait_ge(*p.last())
                    TT(sT_lo[:, 5, :], half("mrT")[:, 0:S], sT_hi[:, 5, :].bitcast(F32), ALU.subtract).then_inc(p.done("mrT"), 1)

                def sbz(k):
                    v.wait_ge(*p.after("tensor", "sbz", k))
                    n = S - k * P
                    z, a = heads(pr2[1 - k]), heads(pt2[1 - k])
                    STT(z, places(half("sbz", k)[:, :], n), 64 ** -0.5, over(cst[:, K_NSTR:K_NSTR + n], 4),
                               ALU.mult, ALU.add).then_inc(p.own, 1)
                    v.wait_ge(*p.last())
                    STT(a, z, -1.0, z, ALU.mult, ALU.max).then_inc(p.done("sbz"), 1)

                def sbm(k):
                    v.wait_ge(*p.after("scalar", "sbl", k))
                    STT(pt2[1 - k], pr2[1 - k], 0.0, pt2[1 - k], ALU.max, ALU.add).then_inc(p.done("sbm"), 1)
                    v.wait_ge(*p.here("sbm"))

                def sbi(k):
                    v.wait_ge(*p.after("tensor", "sbi", k))
                    n = 4 * (S - k * P)
                    TT(pr2[1 - k], pr2[1 - k], half("sbi", k)[:, 0:n], ALU.subtract).then_inc(p.done("sbi"), 1)
                    v.wait_ge(*p.here("sbi"))

                def sbo(qb):
                    v.wait_ge(*p.after("tensor", "sbo", qb))
                    v.tensor_copy(branch_y(1, qb), half("sbo", qb)[:, 0:S]).then_inc(p.done("sbo"), 1)
                    v.wait_ge(*p.here("sbo"))

                def ff_a():
                    v.wait_ge(*p.after("scalar", "drain_s", "h4"))
                    y = fy[:, 0, :, :]
                    TT(y, h2[:, :, B_FF:B_FF + 4], over(fox_bias, R), ALU.add).then_inc(p.own, 1)
                    v.wait_ge(*p.last())
                    STT(fy[:, 1, :, :], y, -1.0, y, ALU.mult, ALU.max).then_inc(p.done("ff_a"), 1)

                def ff_c():
                    v.wait_ge(*p.after("scalar", "ff"))
                    TS(fy[:, 0, :, :], fy[:, 0, :, :], 0.0, None, ALU.min).then_inc(p.own, 1)
                    v.wait_ge(*p.last())
                    TT(fy[:, 2, :, :], fy[:, 0, :, :], fy[:, 1, :, :], ALU.subtract).then_inc(p.done("ff_c"), 1)
                    v.wait_ge(*p.here("ff_c"))

                def fc():
                    v.wait_ge(*p.after("tensor", "fc"))
                    v.tensor_copy(cf[:, :, :].rearrange("p r n -> p (r n)"), half("fc")[:, 0:8]).then_inc(p.done("fc"), 1)
                    v.wait_ge(*p.here("fc"))

                def fb():
                    v.wait_ge(*p.after("tensor", "fb"))
                    v.wait_ge(*p.after("tensor", "sbi", 1))
                    c = half("fb")
                    for qb in range(2):
                        nk = P * (qb + 1)
                        for q in range(4):
                            h = head_of(FOX, q)
                            ins = STT(pt2[qb][:, q * nk:(q + 1) * nk], c[:, q * S:q * S + nk], cf[:, qb, h:h + 1],
                                      cst[:, K_NEG + P - P * qb:K_NEG + 2 * P], ALU.subtract, ALU.subtract)
                    ins.then_inc(p.done("fb"), 1)
                    v.wait_ge(*p.here("fb"))

                def sc2(n, qb):
                    v.wait_ge(*p.after("tensor", "sc2", n, qb))
                    nk, b = keys_of(n, qb), buf_of(n, qb)
                    prev = user_before(n, qb)
                    if prev:
                        v.wait_ge(*p.after("tensor", "p2T", *prev))
                    x, src = heads(pr2[b][:, 0:4 * nk]), places(half("sc2", n, qb)[:, :], nk)
                    scale = (96 if n == MLA else 64) ** -0.5
                    if n == MLA:
                        neg = cst[:, K_NEG + P - P * qb:K_NEG + 2 * P]
                        ins = STT(x, src, scale, over(neg, 4), ALU.mult, ALU.add)
                    elif n == FOX:
                        ins = STT(x, src, scale, heads(pt2[b][:, 0:4 * nk]), ALU.mult, ALU.subtract)
                    else:
                        ins = TS(x, src, scale, None, ALU.mult)
                    ins.then_inc(p.own, 1)
                    v.wait_ge(*p.last())
                    v.tensor_reduce(mx2[qb], x, AX, ALU.max).then_inc(p.own, 1)
                    v.wait_ge(*p.last())
                    TS(mx2[qb], mx2[qb], -1.0, None, ALU.mult).then_inc(p.done("sc2"), 1)
                    v.wait_ge(*p.here("sc2"))

                def pv2(n, qb):
                    v.wait_ge(*p.after("tensor", "pv2", n, qb))
                    b = buf_of(n, qb)
                    v.reciprocal(rs2[qb], rs2[qb]).then_inc(p.own, 1)
                    v.wait_ge(*p.last())
                    TT(heads(branch_y(n, qb)), heads(half("pv2", n, qb)[:, 0:S]), bc(rs2[qb], 64), ALU.mult).then_inc(p.done("pv2"), 1)
                    v.wait_ge(*p.here("pv2"))

                def rope_2():
                    v.wait_ge(*p.after("scalar", "drain_s", "kvb"))
                    def parts(x, nh, w, c):
                        return x.rearrange("p r (h n) -> p r h n", h=nh)[:, :, :, c:c + 32]
                    cos, sin = cos_t[:, :, 24:40], sin_t[:, :, 24:40]
                    rope(parts(q2[:, :, :], 4, 96, 64), cos, sin, tmp2).then_inc(p.own, 1)
                    v.wait_ge(*p.last())
                    rope(parts(h2[:, :, B_KR:B_KR + 32], 1, 32, 0), cos, sin, tmp2).then_inc(p.own, 1)
                    v.wait_ge(*p.last())
                    kh = kc[:, :, :].rearrange("p r (h n) -> p r h n", h=4)
                    v.tensor_copy(kh[:, :, :, 0:64], kv2[:, :, :].rearrange("p r (h n) -> p r h n", h=4)[:, :, :, 0:64])
                    v.tensor_copy(kh[:, :, :, 64:96],
                                             h2[:, :, B_KR:B_KR + 32].unsqueeze(2).broadcast_to([P, R, 4, 32])).then_inc(p.done("rope_2"), 1)
                    v.wait_ge(*p.here("rope_2"))

                def gy(n):
                    v.wait_ge(*p.after("scalar", "drain_s", "gz1"))
                    gz = h2[:, :, B_GATE + n * S:B_GATE + (n + 1) * S]
                    y = q2[:, :, 0:S] if n == MLA else h2[:, :, Q_OF[n]:Q_OF[n] + S]
                    TT(gz, gz, y, ALU.mult).then_inc(p.done("gy"), 1)
                    v.wait_ge(*p.here("gy"))

                def yT(n):
                    v.wait_ge(*p.after("tensor", "mm", max(u for u, x in enumerate(UNITS["two"]) if x[0] == "gz1")))
                    v.wait_ge(*p.after("tensor", "yT", n))
                    src = half("yT", n)[:, 0:512].rearrange("p (r k n) -> p k r n", r=R, k=2)
                    hi = hT_hi[:, 2 * n:2 * n + 2, :].rearrange("p k (r n) -> p k r n", r=R)
                    lo = hT_lo[:, 2 * n:2 * n + 2, :].rearrange("p k (r n) -> p k r n", r=R)
                    v.tensor_copy(hi, src).then_inc(p.own, 1)
                    v.wait_ge(*p.last())
                    TT(lo, src, hi.bitcast(F32), ALU.subtract).then_inc(p.done("yT"), 1)

                def gT(r):
                    v.wait_ge(*p.after("tensor", "mm", max(u for u, x in enumerate(UNITS["two"]) if x[0] == "br01")))
                    v.wait_ge(*p.after("tensor", "gT", r))
                    split_T(half("gT", r), "gT", r, hT_hi, hT_lo, 0, KD).then_inc(p.done("gT"), 1)

                def ln_a():
                    v.tensor_reduce(lnm[:, 0, :], xs[:, :, :], AX, ALU.add).then_inc(p.own, 1)
                    v.wait_ge(*p.last())
                    TS(lnm[:, 0, :], lnm[:, 0, :], -1.0 / D, None, ALU.mult).then_inc(p.own, 1)
                    v.wait_ge(*p.last())
                    for r in range(R):
                        ins = TS(xs[:, r, :], xs[:, r, :], lnm[:, 0, r:r + 1], None, ALU.add)
                    ins.then_inc(p.own, 1)
                    v.wait_ge(*p.last())
                    for r in range(R):
                        ins = v.tensor_tensor_reduce(h2[:, r, 0:D], xs[:, r, :], xs[:, r, :], 1.0, 0.0,
                                                     ALU.mult, ALU.add, lnm[:, 1, r:r + 1])
                    ins.then_inc(p.own, 1)
                    v.wait_ge(*p.last())
                    TS(lnm[:, 2, :], lnm[:, 1, :], 1.0 / D, LN_EPS, ALU.mult, ALU.add).then_inc(p.done("ln_a"), 1)

                def ln():
                    v.wait_ge(*p.after("scalar", "ln_s"))
                    newton(lnm[:, 3, :], lnm[:, 2, :], lnm[:, 4, :])
                    v.wait_ge(ln_in, 32 * (p.l + 1))
                    for r in range(R):
                        STT(xs[:, r, :], xs[:, r, :], lnm[:, 3, r:r + 1], gain[:, :], ALU.mult, ALU.mult).then_inc(p.own, 1)
                        v.wait_ge(*p.last())
                        ins = TT(xs[:, r, :], xs[:, r, :], gain2[:, :], ALU.add)
                        if r == 0:
                            ins.then_inc(p.own, 1)
                            v.wait_ge(*p.last())
                    ins.then_inc(p.done("ln"), 1)
                    v.wait_ge(*p.here("ln"))

                return dict(params2=params2, xT=xT, lat_a=lat_a, lat_c=lat_c, ckT=ckT, mrT=mrT, sbz=sbz, sbm=sbm,
                            sbi=sbi, sbo=sbo, ff_a=ff_a, ff_c=ff_c, fc=fc, fb=fb, sc2=sc2, pv2=pv2, rope_2=rope_2,
                            gy=gy, yT=yT, gT=gT, ln_a=ln_a, ln=ln,
                            memT=memT, tables_a=tables_a, tables_c=tables_c, cwT=cwT, params=params, norm_a=norm_a,
                            norm_c=norm_c, hT=hT, drain_v=drain, gmul=gmul, tap=tap, ba_a=ba_a, ba_c=ba_c, gc=gc_, stat=stat, rn=rn,
                            dec=dec, dec_c=dec_c, kk=kk, kT=kT, vT=vT, invY=invY, invZ=invZ, kq=kq, ks=ks, o=o_,
                            onorm_a=onorm_a, onorm_c=onorm, kinorm_a=kinorm_a, rope_i=rope_i, raw=raw_, topk=topk,
                            rope_a=rope_a, sc=sc, pv=pv, mix=mix, mT=mT)

            run(v, "vector", handlers)


WEIGHTS = {"w_in": "w_in", "w_out": "w_out", "w_in_2": "w_in_2", "mla_w_qb_2": "mla_w_qb", "mla_w_kvb_2": "mla_w_kvb",
           "w_mem_kv_2": "w_mem_kv", "w_merge_up_2": "w_merge_up", "w_branch_2": "w_branch", "w_out_2": "w_out_2"}
PLAIN = ["x", "positions", "conv_w", "a_log", "dt_bias", "gdn_norm_gain", "idx_k_gain", "mem_2", "positions_2",
         "mla_q_norm_2", "mla_kv_norm_2", "fox_forget_bias_2"]


def kernel(**inputs):
    import concourse.bacc as bacc
    from concourse.bass_utils import run_bass_kernel_spmd

    arrays = laid_out(inputs)
    nc = bacc.Bacc("TRN2", target_bir_lowering=False, num_devices=1, dynamic_dma_scratch_size=8192)
    t = {name: nc.dram_tensor(f"in_{name}_dram", a.shape, mybir.dt.from_np(a.dtype), kind="ExternalInput").ap()
         for name, a in arrays.items()}
    out = nc.dram_tensor("out_0_dram", (1, S, D), F32, kind="ExternalOutput").ap()
    build(nc, t, out)
    r = run_bass_kernel_spmd(nc, [{f"in_{k}_dram": a for k, a in arrays.items()}], core_ids=[0])
    return r.results[0]["out_0_dram"]


def laid_out(inputs):
    arrays = {name: np.ascontiguousarray(inputs[name]) for name in PLAIN}
    for name, short in WEIGHTS.items():
        arrays[short] = np.ascontiguousarray(inputs[name])
    arrays["gains"] = np.concatenate([np.asarray(inputs["norm_gain"]), np.asarray(inputs["final_gain"])[None]])
    arrays["ln_rows"] = np.concatenate([np.stack([np.asarray(inputs["ln_gain_2"])[l], np.asarray(inputs["ln_bias_2"])[l]])
                                        for l in range(DEPTH)])
    arrays["shape_constants"] = shape_constants()
    return arrays
```

```python
from contextlib import ExitStack

import numpy as np
import concourse.bass as bass
from concourse import mybir

F32 = mybir.dt.float32
F32R = mybir.dt.float32r
I32 = mybir.dt.int32
ALU = mybir.AluOpType
ACT = mybir.ActivationFunctionType
AX = mybir.AxisListType.X

P = 128
S = 256
R = S // P
D = 1024
KD = D // P
DEPTH = 2
NEG = -1.0e30
TAKEN = -3.0e38
EPS = 1e-6
LN_EPS = 1e-5
TOPK = 64
ALPHA = (2 * DEPTH) ** 0.25

C_QA, C_ZA, C_QI, C_KI, C_GQ, C_ZB, C_BA, C_GATE = 0, 1536, 2560, 3072, 3144, 6216, 7240, 7256
IN_COLS = 9304
IN_WIDTH = 3620
B_CKV, B_KR, B_SB, B_FOX, B_FF, B_MQ, B_GATE, B_MR = 384, 640, 672, 1440, 2208, 2212, 2468, 3492

K_ID, K_TRIU, K_LEVEL, K_PAIR, K_NEG, K_STR, K_NSTR, K_TRIL, K_ONE, K_FREQ = (
    0, 128, 256, 1024, 1152, 1408, 1664, 1920, 2048, 2176)
LEVELS = (2, 4, 8, 16, 32, 64)
K_COLS = K_FREQ + 40


def shape_constants():
    c = np.zeros((P, K_COLS), np.float32)
    p, f = np.arange(P)[:, None], np.arange(P)[None, :]
    c[:, K_ID:K_ID + P] = p == f
    c[:, K_TRIU:K_TRIU + P] = p <= f
    for n, s in enumerate(LEVELS):
        c[:, K_LEVEL + n * P:K_LEVEL + (n + 1) * P] = (
            (p // (2 * s) == f // (2 * s)) & (p // s % 2 == 1) & (f // s % 2 == 0))
    c[:, K_PAIR:K_PAIR + P] = (f % 2 == 1) & (p == f - 1)
    c[:, K_NEG + P:K_NEG + 2 * P] = np.where(f > p, np.float32(NEG), np.float32(0))
    c[:, K_STR:K_STR + P] = p < f
    c[:, K_STR + P:K_STR + 2 * P] = 1
    c[:, K_NSTR:K_NSTR + P] = np.where(p < f, np.float32(0), np.float32(NEG))
    c[:, K_TRIL:K_TRIL + P] = p >= f
    c[:, K_ONE:K_ONE + P] = 1
    at = K_FREQ
    for theta, rot in ((500000.0, 32), (500000.0, 16), (10000.0, 32)):
        half = rot // 2
        c[:, at:at + half] = np.float32(theta) ** (-np.arange(0, rot, 2, dtype=np.float32) / np.float32(rot))
        at += half
    return c


def tile_units(ksizes):
    out, k = [], 0
    for n in ksizes:
        out.append((k, n))
        k += n
    return out


PAIRS = [2, 2, 2, 2]
MEM_TILES = [(f"mkv{l}", dict(src="w_mem_kv", layer=l, col=0, n=512, ks=PAIRS, lhs="big", drain="scalar"))
             for l in range(DEPTH)]


def nat(src, col, n, drain, ks=PAIRS, lhs="big"):
    return dict(src=src, col=col, n=n, ks=ks, lhs=lhs, drain=drain)


def conv_tiles(g):
    return [(f"c{w}{g}", dict(src="w_in", col=C_GQ + w * 1024 + g * 512, n=512, ks=PAIRS, lhs="T", drain="scalar"))
            for w in range(3)]


NARROW = 72

ONE_TILES = (
    [("ba", nat("w_in", C_BA + 16 - NARROW, NARROW, "vector", ks=[8], lhs="narrow"))]
    + conv_tiles(0)
    + [("qi", nat("w_in", C_QI, 512, "scalar")), ("ki", nat("w_in", C_KI, NARROW, "vector", ks=[8], lhs="narrow")),
       ("kv", nat("w_in", 1024, 512, "scalar")), ("qa0", nat("w_in", 0, 512, "scalar")),
       ("qa1", nat("w_in", 512, 512, "scalar"))]
    + conv_tiles(1)
    + [(f"za{c}", nat("w_in", C_ZA + c * 512, 512, "scalar")) for c in range(2)]
    + [(f"zb{c}", nat("w_in", C_ZB + c * 512, 512, "scalar")) for c in range(2)]
    + [(f"g{b}{c}", nat("w_in", C_GATE + b * 1024 + c * 512, 512, "scalar")) for b in range(2) for c in range(2)]
    + [(f"o{c}", nat("w_out", c * 512, 512, "vector")) for c in range(2)])

H2_TILES = [(0, 512), (512, 512), (1024, 512), (1536, 512), (2048, 420)]
def up_tile(c):
    return (f"mu{c}", nat("w_merge_up", c * 512, 512, "scalar", ks=[1], lhs="mr"))


def branch_tile(n, c):
    return (f"br{n}{c}", nat("w_branch", c * 512, 512, "vector", ks=[2], lhs=f"yb{n}"))


def gate_tile(c):
    return (f"gz{c}", nat("w_in_2", B_GATE + c * 512, 512, "scalar"))


TWO_TILES = (
    [(f"h{n}", nat("w_in_2", c, w, "scalar")) for n, (c, w) in enumerate(H2_TILES)]
    + [("qb", nat("mla_w_qb", 0, 384, "scalar", ks=[2, 1], lhs="cq")),
       ("kvb", nat("mla_w_kvb", 0, 512, "scalar", ks=[2], lhs="ckv")),
       ("mr", nat("w_in_2", B_MR, 128, "vector", ks=[8], lhs="narrow"))]
    + [gate_tile(0), up_tile(2), up_tile(3), gate_tile(1), up_tile(4)]
    + [branch_tile(1, 0), up_tile(5), branch_tile(1, 1), up_tile(6), branch_tile(2, 0), up_tile(7), branch_tile(2, 1),
       up_tile(0), branch_tile(3, 0), up_tile(1), branch_tile(3, 1), branch_tile(0, 0), branch_tile(0, 1)]
    + [(f"o{c}", nat("w_out_2", c * 512, 512, "vector")) for c in range(2)])

RAW_SLOTS = 5
SPLIT_SLOTS = 3
LOOK = 3
CONV_LATE = 2
AHEAD_MEM = [1] * 4
AHEAD_ONE = [
    1, 0, 0, 0, 3, 0, 10, 9, 0, 1, 0, 0, 1, 1, 0, 0, 1, 0, 1, 1, 0, 0, 0, 0, 1, 0, 1, 0, 0, 0, 0, 0, 0, 0, 0, 0,
    0, 0, 0, 0, 0, 0, 0, 0, 0, 0, 0, 0, 0, 0, 0, 0, 0, 0, 0, 0, 0, 0, 12, 8, 0, 2, 0, 0, 0, 2, 0, 0, 0, 2, 1, 0,
    2, 0, 0, 0, 3, 0, 0, 0, 0, 0, 0, 0, 0, 0, 0, 0, 0, 0, 0, 0, 0, 0, 0, 0, 0, 0, 0, 0, 0, 0, 0, 0, 1, 0, 1, 1, 1,
    0, 1, 0, 1, 0, 0, 0, 3, 0, 0, 0, 0, 1, 5, 0, 1, 4, 0, 3, 0, 1, 5, 0, 0, 0, 1, 5]
AHEAD_TWO = [
    6, 2, 0, 3, 0, 2, 0, 0, 0, 0, 0, 0, 3, 1, 0, 0, 4, 1, 1, 0, 0, 6, 0, 0, 1, 1, 0, 3, 0, 1, 1, 0, 2, 1, 5, 3, 2,
    2, 2, 0, 1, 3, 2, 0, 0, 0, 4, 0, 6, 2, 10, 6, 0, 0, 1, 3]
ARENA = 24600


def units_of(tiles):
    return [(name, t, k0, nk, k0 == 0, k0 + nk == sum(t["ks"])) for name, t in tiles for k0, nk in tile_units(t["ks"])]


UNITS = {"mem": units_of(MEM_TILES), "one": units_of(ONE_TILES), "mid": [], "two": units_of(TWO_TILES)}


DRAIN_STEP = {"scalar": "drain_s", "vector": "drain_v"}


def weave(units, before, chain, ahead):
    marks = ("need", "gate", "gate_end", "gate_conv")
    steps = [s for s in chain if s[0] not in marks]
    out, u, taken = [("split", n) for n in range(min(LOOK, len(units)))] + list(before), 0, 0
    last_of = {name: n for n, (name, *_) in enumerate(units)}
    first_of = {name: n for n, (name, *_) in reversed(list(enumerate(units)))}
    limit, low, i = [], [], 0
    for s in chain:
        if s[0] == "need":
            n = last_of[s[1]]
            low.append((i, n + 1 + (CONV_LATE if units[n][1]["lhs"] == "T" else 0)))
        elif s[0] == "gate":
            limit.append((i, first_of[s[1]]))
        elif s[0] == "gate_end":
            limit.append((i, last_of[s[1]]))
        elif s[0] == "gate_conv":
            limit.append((i, last_of[s[1]] + CONV_LATE))
        else:
            i += 1

    def issue(n):
        name, w, _, _, _, last = units[n]
        out.append(("mm", n))
        if n + LOOK < len(units):
            out.append(("split", n + LOOK))
        if last:
            if w["lhs"] == "T":
                out.append(("tap", int(name[1]), int(name[2])))
            else:
                out.append((DRAIN_STEP[w["drain"]], name))
                if w["src"] == "w_in" and w["col"] >= C_GATE:
                    out.append(("gmul", name))

        back = n - CONV_LATE
        if back >= 0 and units[back][1]["lhs"] == "T" and units[back][5]:
            out.append(("conv", int(units[back][0][1]), int(units[back][0][2])))

    for i, step in enumerate(steps):
        taken += ahead[i] if i < len(ahead) else 0
        least = max([n for at, n in low if at <= i], default=0)
        most = min([n for at, n in limit if at > i], default=len(units))
        assert least <= most, step
        while u < min(max(taken, least), most):
            issue(u)
            u += 1
        out.append(step)
    while u < len(units):
        issue(u)
        u += 1
    return out


def gdn_chain(g):
    out = [("need", f"c0{g}"), ("stat", 0, g), ("need", f"c1{g}"), ("stat", 1, g), ("rn", g),
           ("dec", g, 0), ("dec_b", g, 0), ("dec_c", g, 0), ("kk", g, 0), ("dec", g, 1), ("dec_b", g, 1),
           ("dec_c", g, 1), ("kk", g, 1), ("x1", g, 0), ("x1", g, 1), ("kT", g)]
    for n in range(len(LEVELS)):
        for r in range(R):
            out.append(("invY", g, r, n))
        for r in range(R):
            out.append(("invZ", g, r, n))
        if n == 0:
            out += [("need", f"c2{g}"), ("vT", g)]
    out += [("kq", g, 0), ("kq", g, 1), ("u", g, 0), ("st", g), ("ks", g), ("o", g, 0), ("u", g, 1), ("o", g, 1)]
    return out


def attention_chain():
    out = [("iT", r) for r in range(R)]
    out += [("raw", 0, 0), ("raw", 1, 0), ("raw", 1, 1)] + [("qT", r) for r in range(R)] + [("kaT",)]
    out += [("topk", 0), ("sc", 0, 0), ("topk", 1), ("pT", 0, 0), ("pv", 0, 0), ("sc", 0, 1), ("onorm_a",), ("onorm",),
            ("pT", 0, 1), ("pv", 0, 1), ("sc", 1, 0), ("onorm_c",), ("pT", 1, 0), ("pv", 1, 0), ("sc", 1, 1),
            ("need", "g11"), ("mix_b", 0), ("mix", 0), ("mT", 0), ("mix_b", 1), ("pT", 1, 1), ("pv", 1, 1)]
    return out + [("mix", 1), ("mT", 1), ("gate", "o0")]


def block_one():
    chain = [("need", "ba"), ("baT",), ("ba_a",), ("ba_b",), ("ba_c",), ("gc",), ("gc_b",)]
    chain += gdn_chain(0) + [("need", "ki"), ("kxT",), ("kinorm_a",), ("kinorm",), ("rope_i",), ("need", "qa1"), ("rope_a",),
                             ("gate_conv", "c01")]
    chain += gdn_chain(1) + attention_chain()
    before = [("params",), ("norm_a",), ("norm",), ("norm_c",), ("gain",)] + [("hT", r) for r in range(R)]
    return weave(UNITS["one"], before, chain, AHEAD_ONE)


FOX, MEM, MLA = 2, 3, 0


def softmax_chain(n):
    out = [("qk2T", n)] + ([("qk2T", n, 1)] if n == MLA else [])
    if n == FOX:
        out += [("fb",)]
    return out + [("sc2", n, 0), ("sc2", n, 1), ("p2T", n, 0), ("pv2", n, 0), ("p2T", n, 1), ("pv2", n, 1)]


def block_two():
    chain = [("need", "h1"), ("lat_a",), ("lat",), ("lat_c",), ("ckT", 0), ("ckT", 1), ("gate", "qb"),
             ("need", "h2"), ("qk2T", 1), ("sbz", 0), ("sbz", 1), ("sbl", 0), ("sbl", 1), ("sbm", 0), ("sbm", 1),
             ("sbi", 0), ("sbi", 1), ("sbe", 0), ("sbe", 1), ("sbo", 0), ("sbo", 1)]
    chain += [("need", "h4"), ("ff_a",), ("ff",), ("ff_c",), ("fc",)] + softmax_chain(FOX) + softmax_chain(MEM)
    chain += [("ln_rows",), ("need", "kvb"), ("rope_2",), ("need", "gz1"), ("gy", 1), ("yT", 1), ("gate", "br10")]
    mla = softmax_chain(MLA)
    chain += mla[:4] + [("gy", 2), ("yT", 2), ("gate", "br20")] + mla[4:6]
    chain += [("gy", 3), ("yT", 3), ("gate", "br30")] + mla[6:] + [("gy", 0), ("yT", 0), ("gate", "br00")]
    chain += [("gate_end", "br01"), ("need", "br01"), ("gT", 0), ("gT", 1), ("gate", "o0")]
    before = [("params2",), ("xT", 0), ("xT", 1)]
    return weave(UNITS["two"], before, chain, AHEAD_TWO) + [("ln_a",), ("ln_s",), ("ln",)]


TIMELINE = {
    "mem": weave(UNITS["mem"], [("memT", 0), ("memT", 1)],
                 [("tables_a",), ("tables",), ("tables_c",), ("cwT",)], AHEAD_MEM),
    "one": block_one(),
    "mid": [("norm_a",), ("norm",), ("norm_c",)],
    "two": block_two(),
}
TILES = {"mem": MEM_TILES, "one": ONE_TILES, "mid": [], "two": TWO_TILES}
LEFT = {
    "mem": {"mkv0": [("memT", 1)]},
    "one": {"ba": [("hT", 1)], "o0": [("mT", 1)]},
    "two": {"h0": [("xT", 1)], "qb": [("ckT", 1)], "mu2": [("drain_v", "mr")],
            "br10": [("yT", 1)], "br20": [("yT", 2)], "br30": [("yT", 3)], "br00": [("yT", 0)],
            "o0": [("gT", 1)]},
}
CONV_BEFORE = {(1, 0): (0, 0), (2, 0): (1, 0), (0, 1): (2, 0), (1, 1): (0, 1), (2, 1): (1, 1)}
ITERATIONS = {"mem": 1, "one": DEPTH, "mid": 1, "two": DEPTH}
SECTIONS = ["mem", "one", "mid", "two"]

DRAINER = {
    "baT": "vector", "kxT": "vector", "memT": "vector", "cwT": "vector", "hT": "vector", "gc": "vector", "stat": "vector", "dec": "vector",
    "kk": "vector", "x1": "scalar", "kT": "vector", "invY": "vector", "invZ": "vector", "vT": "vector",
    "kq": "vector", "u": "scalar", "st": "scalar", "ks": "vector", "o": "vector", "iT": "scalar",
    "raw": "scalar", "qT": "scalar", "kaT": "scalar", "sc": "vector", "pT": "scalar", "pv": "vector",
    "mT": "vector",
    "xT": "vector", "ckT": "vector", "qk2T": "scalar", "fc": "vector",
    "fb": "vector", "sc2": "vector", "p2T": "scalar", "pv2": "vector", "sbz": "vector", "sbi": "vector",
    "sbo": "vector", "yT": "vector", "gT": "vector",
}


EMPTIED_BY = {"dec": "dec_c"}


class Order:

    def __init__(self, ctx, nc):
        self.ctx, self.nc, self.sems = ctx, nc, {}
        self.ordinal, self.per = {}, {}
        for sec in SECTIONS:
            for step in TIMELINE[sec]:
                n = self.per.get((sec, step[0]), 0)
                self.ordinal[(sec,) + step] = n
                self.per[(sec, step[0])] = n + 1

    def sem(self, name):
        if name not in self.sems:
            self.sems[name] = self.ctx.enter_context(self.nc.semaphore(name))
        return self.sems[name]

    def base(self, sec, step):
        return sum(ITERATIONS[s] * self.per.get((s, step), 0) for s in SECTIONS[:SECTIONS.index(sec)])

    def after(self, engine, sec, l, step, *args):
        n = self.ordinal[(sec, step) + args]
        return self.sem(f"{step}_{engine}"), self.base(sec, step) + l * self.per[(sec, step)] + n + 1

    def before_section(self, engine, sec, l, step):
        return self.sem(f"{step}_{engine}"), self.base(sec, step) + l * self.per.get((sec, step), 0)


STEPS = {"mem": {"vector": 11},
         "one": {"scalar": 6, "vector": 180},
         "mid": {"scalar": 1, "vector": 6},
         "two": {"scalar": 8, "vector": 56}}


class Program:

    def __init__(self, order, eng, name):
        self.o, self.eng, self.name = order, eng, name
        self.own = order.sem(f"{name}_step")
        self.n, self.base, self.sec, self.l = 0, 0, None, 0
        self.step, self.args = None, ()

    def enter(self, sec, l):
        self.sec, self.l, self.n = sec, l, 0
        self.base = sum(ITERATIONS[s] * STEPS[s].get(self.name, 0) for s in SECTIONS[:SECTIONS.index(sec)])

    def leave(self):
        assert self.n == STEPS[self.sec].get(self.name, 0), (self.sec, self.name, self.n)

    def after(self, engine, step, *args):
        return self.o.after(engine, self.sec, self.l, step, *args)

    def done(self, step):
        return self.o.sem(f"{step}_{self.name}")

    def here(self, step):
        return self.o.after(self.name, self.sec, self.l, step, *self.args)

    def last(self):
        self.n += 1
        return self.own, self.base + self.l * STEPS[self.sec].get(self.name, 0) + self.n


def two_before():
    half, had = {}, {}
    for sec in SECTIONS:
        seen = []
        for step in TIMELINE[sec]:
            if step[0] in DRAINER:
                half[(sec,) + step] = len(seen) % 2
                had[(sec,) + step] = seen[-2] if len(seen) >= 2 else None
                seen.append(step)
    return half, had


def build(nc, t, out):
    ctx = ExitStack()
    with ctx:
        o = Order(ctx, nc)
        half_of, had_half = two_before()

        def sb(name, cols, dt=F32, parts=P):
            return ctx.enter_context(nc.sbuf_tensor(name, [parts] + cols, dt))

        cst = sb("cst", [K_COLS])
        xs = sb("xs", [R, D])
        raw = sb("raw", [RAW_SLOTS, 1024])
        w_hi = sb("w_hi", [SPLIT_SLOTS, 1024], F32R)
        w_lo = sb("w_lo", [SPLIT_SLOTS, 1024], F32R)
        hT_hi = sb("hT_hi", [KD, S], F32R)
        hT_lo = sb("hT_lo", [KD, S], F32R)
        sT_hi = sb("sT_hi", [6, S], F32R)
        sT_lo = sb("sT_lo", [6, S], F32R)
        gain = sb("gain", [D])
        gain2 = sb("gain2", [D])
        cw_rows = sb("cw_rows", [DEPTH, P], parts=96)
        par1 = sb("par1", [DEPTH, 304])
        now1 = sb("now1", [304])
        taps, a_log, dt_bias = now1[:, 0:96], now1[:, 96:104], now1[:, 104:112]
        gdn_gain, idx_gain = now1[:, 112:240], now1[:, 240:304]
        par2 = sb("par2", [DEPTH, 644])
        now2 = sb("now2", [644])
        q_gain, kv_gain, fox_bias = now2[:, 0:384], now2[:, 384:640], now2[:, 640:644]
        pos_i = sb("pos_i", [2, R], I32)
        cos_t = sb("cos_t", [R, 40])
        sin_t = sb("sin_t", [R, 40])
        mkv = sb("mkv", [DEPTH, R, 512])
        tiny = sb("tiny", [512])
        arena = sb("arena", [ARENA])

        at = [0]

        def area(*dims, start=None):
            if start is not None:
                at[0] = start
            n = int(np.prod(dims))
            v = arena[:, at[0]:at[0] + n]
            at[0] += n
            assert at[0] <= ARENA, at[0]
            if len(dims) == 2:
                v = v.rearrange("p (a b) -> p a b", a=dims[0])
            if len(dims) == 3:
                v = v.rearrange("p (a b c) -> p a b c", a=dims[0], b=dims[1])
            return v

        pq = area(R, 1536, start=0)
        pi = area(R, 584)
        g0 = area(R, D)
        g1 = area(R, D)
        od = area(R, D)
        shared = at[0]
        cs = area(3, 4, S)
        cv = area(4, S)
        sq = area(4, S)
        vb = area(R, 4, P)
        kd = area(4, P)
        st = area(4, P)
        uu = area(R, 4, P)
        dt_ = area(R, 4, P)
        lt = area(R, 4, P)
        xx = area(R, 4, P)
        xt = area(R, 4, P)
        yy = area(R, 4, P)
        assert at[0] <= ARENA - R * 2 * 64
        qaT = area(8, S, start=shared)
        kaT = area(2, S)
        qiT = area(4, S)
        kiT = area(S)
        isc = [area(P), area(S)]
        mb = [area(P), area(S)]
        rl = area(D)
        pr = [area(1024), area(1024)]
        pt = [area(1024), area(1024)]
        od_sq = area(D)
        assert at[0] <= ARENA - R * 2 * 64
        kk2 = area(R, 2, 64, start=ARENA - R * 2 * 64)
        h_nat = g0
        narrow = kk2[:, :, :, :].rearrange("p r c n -> p (r c n)")
        rope_tmp = g0[:, :, :].rearrange("p r n -> p (r n)")[:, 0:4 * R * 160].rearrange("p (a n) -> p a n", a=4)
        mem_raw = area(R, D, start=0)
        ang = area(5, R * 40, start=4096)

        h2 = area(R, IN_WIDTH, start=0)
        mg = area(R, 4096)
        q2 = area(R, 384)
        kv2 = area(R, 512)
        kc = area(R, 384)
        reg_a, reg_b = area(2048), area(1024)
        pr2 = [area(512), area(1024)]
        pt2 = [area(512), area(1024)]
        mkv_now = gain2[:, :].rearrange("p (r n) -> p r n", r=R)
        merged = h2[:, :, 0:D]
        tmp2 = kc[:, :, :].rearrange("p r n -> p (r n)")[:, 0:512].rearrange("p (a n) -> p a n", a=4)

        tn = [0]

        def small(*dims):
            n = int(np.prod(dims))
            v = tiny[:, tn[0]:tn[0] + n]
            tn[0] += n
            assert tn[0] <= 512
            if len(dims) == 2:
                v = v.rearrange("p (a b) -> p a b", a=dims[0])
            if len(dims) == 3:
                v = v.rearrange("p (a b c) -> p a b c", a=dims[0], b=dims[1])
            return v

        nrm = small(4, R)
        ba = small(R, 16)
        ay = small(2, R, 8)
        be = small(R, 8)
        eb = small(R, 8)
        ea = small(8)
        gdec = small(R, 8)
        gc = small(R, 8)
        egc = small(R, 8)
        wl = small(2, 8)
        ss = small(2, R, 4)
        s2 = small(2, R, 4)
        s3 = small(2, R, 4)
        av = small(R, 4)
        bke = small(4)
        wk = small(4)
        so = small(3, R, 8)
        kn = small(4, R)
        wi = small(R, 8)
        mx = [small(4), small(4)]
        rs = [small(4), small(4)]
        top = small(8)
        lat = small(4, 2, R)
        fy = small(3, R, 4)
        cf = small(R, 4)
        mx2 = [small(4), small(4)]
        rs2 = [small(4), small(4)]
        lnm = small(5, R)

        def ps(name):
            return ctx.enter_context(nc.psum_tensor(name, [P, 1024], F32))

        bulk = [ps("bulk0"), ps("bulk1")]
        chain = [ps("chain0"), ps("chain1")]

        ident = cst[:, K_ID:K_ID + P]
        triu = cst[:, K_TRIU:K_TRIU + P]
        ones = cst[:, K_ONE:K_ONE + P]

        Q_OF = {1: B_SB, FOX: B_FOX, MEM: B_MQ}

        def t_parts(n):
            reg = reg_b if n in (1, MEM) else reg_a
            a = 4 if n == MLA else 2
            return (reg[:, 0:a * S].rearrange("p (a n) -> p a n", a=a),
                    reg[:, a * S:2 * a * S].rearrange("p (a n) -> p a n", a=a))

        def head_of(n, q):
            return q if n == MLA else bank_order(q, 4)

        def head_T(n, h, which, cols):
            x = t_parts(n)[which]
            if n == MLA:
                return x[0:96, h, cols]
            return x[64 * (h % 2):64 * (h % 2) + 64, h // 2, cols]

        def values(n, h, k):
            if n == MLA:
                return kv2[:, k, h * P + 64:h * P + P]
            if n == MEM:
                return mkv_now[:, k, S + h * 64:S + (h + 1) * 64]
            c = Q_OF[n] + 512 + h * 64
            return h2[:, k, c:c + 64]

        def branch_y(n, r):
            return q2[:, r, 0:S] if n == MLA else h2[:, r, Q_OF[n]:Q_OF[n] + S]

        def keys_of(n, qb):
            return S if n == MEM else P * (qb + 1)

        def buf_of(n, qb):
            return keys_of(n, qb) // P - 1

        score_users = [[x for x in [(n, qb) for n in (FOX, MEM, MLA) for qb in range(2)] if buf_of(*x) == b]
                       for b in range(2)]

        def user_before(n, qb):
            u = score_users[buf_of(n, qb)]
            i = u.index((n, qb))
            return u[i - 1] if i else None

        def places(x, nk):
            return x.rearrange("p (q n) -> p q n", q=4)[:, :, 0:nk]

        def bank_order(i, per):
            return 2 * (i % (per // 2)) + i // (per // 2)

        def bc(v, n):
            return v.unsqueeze(2).broadcast_to([v.shape[0], v.shape[1], n])

        def over(v, a):
            return v.unsqueeze(1).broadcast_to([v.shape[0], a, v.shape[1]])

        def heads(v, a=4):
            return v.rearrange("p (a n) -> p a n", a=a)

        def layer_of(v, l, starts):
            n = int(np.prod(v.shape[1:]))
            if isinstance(l, int):
                at_l = l * n
            else:
                if n not in starts:
                    starts[n] = nc.sync.snap((l + 1) * n)
                at_l = starts[n] - n
            dims = " ".join(f"d{i}" for i in range(len(v.shape)))
            flat_v = v.rearrange(f"{dims} -> ({dims})")[bass.ds(at_l, n)]
            inner = " ".join(f"d{i}" for i in range(1, len(v.shape)))
            return flat_v.rearrange(f"({inner}) -> {inner}", **{f"d{i}": v.shape[i] for i in range(1, len(v.shape))})

        def dview(name, l, starts):
            v = layer_of(t[name], l, starts)
            if name == "w_branch":
                return v.rearrange("n (k p) c -> p (n k) c", p=P)
            return v.rearrange("(k p) c -> p k c", p=P)

        raw_in = [o.sem(f"raw_in{n}") for n in range(RAW_SLOTS)]
        const_in = o.sem("constants_loaded")
        par_in = o.sem("parameters_loaded")
        gain_in = o.sem("gain_loaded")
        ln_in = o.sem("ln_rows_loaded")
        topk_step = o.sem("topk_step")
        x_in = o.sem("x_loaded")
        mem_in = o.sem("memory_loaded")
        out_sem = o.sem("out_stored")
        N_PARAMS = 9

        def slot_value(sec, l, u):
            s = u % RAW_SLOTS
            uses = lambda sc: (len(UNITS[sc]) - s + RAW_SLOTS - 1) // RAW_SLOTS
            before = sum(ITERATIONS[x] * uses(x) for x in SECTIONS[:SECTIONS.index(sec)])
            return raw_in[s], (before + l * uses(sec) + u // RAW_SLOTS + 1) * 16

        def unit_before(p, engine, step, u, slots):
            if u >= slots:
                return p.after(engine, step, u - slots)
            return o.before_section(engine, p.sec, p.l, step)

        def drained(p, tile):
            name, w = tile
            if w["lhs"] == "T":
                return p.after("vector", "tap", int(name[1]), int(name[2]))
            return p.after(w["drain"], DRAIN_STEP[w["drain"]], name)

        def run(eng, name, handlers):
            p = Program(o, eng, name)
            steps = handlers(p)
            for sec in SECTIONS:
                def body(l):
                    p.enter(sec, l)
                    for step in TIMELINE[sec]:
                        if step[0] in steps:
                            p.step, p.args = step, step[1:]
                            steps[step[0]](*step[1:])
                    p.leave()

                if ITERATIONS[sec] == 1:
                    body(0)
                else:
                    with eng.Fori(0, ITERATIONS[sec]) as l:
                        body(l)

        block = ctx.enter_context(nc.Block())

        @block.sync
        def _(sp):
            for dst, src in (
                    (cst[:, :], t["shape_constants"]),
                    (pos_i[:, 0, :], t["positions"].rearrange("a (r p) -> p (a r)", p=P)),
                    (pos_i[:, 1, :], t["positions_2"].rearrange("a (r p) -> p (a r)", p=P))):
                sp.dma_start(dst, src, allow_slow_non_contiguous=True).then_inc(const_in, 16)
            sp.dma_start(mem_raw, t["mem_2"].rearrange("a (r p) d -> p (a r) d", p=P)).then_inc(mem_in, 16)
            loads = [(cw_rows[:, l, :], t["conv_w"][l].rearrange("k (c q) -> (k c) q", q=P)) for l in range(DEPTH)]
            for par, col, name in ((par1, 96, "a_log"), (par1, 104, "dt_bias"), (par1, 112, "gdn_norm_gain"),
                                   (par1, 240, "idx_k_gain"), (par2, 0, "mla_q_norm_2"), (par2, 384, "mla_kv_norm_2"),
                                   (par2, 640, "fox_forget_bias_2")):
                n = t[name].shape[1]
                loads.append((par[:, :, col:col + n], t[name].unsqueeze(0).broadcast_to([P, DEPTH, n])))
            assert len(loads) == N_PARAMS

            def load_gain(row):
                sp.dma_start(gain[:, :], row.broadcast_to([P, D])).then_inc(gain_in, 16)

            def handlers(p):
                starts = {}

                def first(*_):
                    starts.clear()
                    for n in sorted({w["src"] for _, w in TILES[p.sec]}):
                        dview(n, p.l, starts)
                    layer_of(t["ln_rows"].rearrange("(l i) d -> l i d", i=2), p.l, starts)
                    layer_of(t["gains"][1:, :], p.l, starts)

                def load(u):
                    if u == 0:
                        first()
                    name, w, k0, nk, _, _ = UNITS[p.sec][u]
                    if p.sec != "mem" or u >= RAW_SLOTS:
                        sp.wait_ge(*unit_before(p, "gpsimd", "split", u, RAW_SLOTS))
                    src = dview(w["src"], w.get("layer", p.l), starts)
                    if w["src"] == "w_branch":
                        k0 += 2 * int(w["lhs"][2])
                    sem, _ = slot_value(p.sec, p.l, u)
                    sp.dma_start(raw[:, u % RAW_SLOTS, 0:nk * w["n"]].rearrange("p (k n) -> p k n", k=nk),
                                 src[:, k0:k0 + nk, w["col"]:w["col"] + w["n"]]).then_inc(sem, 16)
                    if p.sec == "mem" and u == 3:
                        sp.dma_start(xs[:, :, :], t["x"].rearrange("a (r p) d -> p (a r) d", p=P)).then_inc(x_in, 16)
                        load_gain(t["gains"][0:1, :])
                        for dst, src in loads:
                            sp.dma_start(dst, src).then_inc(par_in, 16)

                def next_gain():
                    first()
                    sp.wait_ge(*p.after("vector", "norm_c"))
                    load_gain(layer_of(t["gains"][1:, :], p.l, starts).unsqueeze(0))

                def ln_rows():
                    sp.wait_ge(*p.after("vector", "pv2", MEM, 1))
                    sp.wait_ge(*p.after("tensor", "pv2", MEM, 1))
                    rows = layer_of(t["ln_rows"].rearrange("(l i) d -> l i d", i=2), p.l, starts)
                    for i, dst in enumerate((gain, gain2)):
                        sp.dma_start(dst[:, :], rows[i:i + 1, :].broadcast_to([P, D])).then_inc(
                            ln_in, 16)

                return {"split": load, "gain": next_gain, "ln_rows": ln_rows}

            run(sp, "sync", handlers)
            sp.wait_ge(*o.after("vector", "two", DEPTH - 1, "ln"))
            sp.dma_start(out.rearrange("a (r p) d -> p (a r) d", p=P), xs[:, :, :]).then_inc(out_sem, 16)
            sp.wait_ge(out_sem, 16)

        @block.gpsimd
        def _(pool):
            def handlers(p):
                def split(u):
                    _, w, _, nk, _, _ = UNITS[p.sec][u]
                    n = nk * w["n"]
                    pool.wait_ge(*slot_value(p.sec, p.l, u))
                    pool.wait_ge(*p.after("scalar", "split", u))
                    pool.tensor_tensor(w_lo[:, u % SPLIT_SLOTS, 0:n], raw[:, u % RAW_SLOTS, 0:n],
                                             w_hi[:, u % SPLIT_SLOTS, 0:n].bitcast(F32), ALU.subtract).then_inc(
                                                     p.done("split"), 1)
                return {"split": split}

            run(pool, "gpsimd", handlers)

        @block.tensor
        def _(pe):
            def handlers(p):
                def lhs(w, kk, r):
                    kind, rr = w["lhs"], slice(r * P, (r + 1) * P)
                    if kind == "big":
                        return hT_hi[:, kk, rr], hT_lo[:, kk, rr]
                    if kind[:2] == "yb":
                        return hT_hi[:, 2 * int(kind[2]) + kk, rr], hT_lo[:, 2 * int(kind[2]) + kk, rr]
                    k = {"cq": 0, "ckv": 3, "mr": 5}[kind] + kk
                    return sT_hi[:, k, rr], sT_lo[:, k, rr]

                def mm(u):
                    name, w, k0, nk, first, last = UNITS[p.sec][u]
                    names = [x for x, _ in TILES[p.sec]]
                    tile, n, slot = names.index(name), w["n"], u % SPLIT_SLOTS
                    pair = bulk[tile % 2]
                    if first and tile >= 2:
                        pe.wait_ge(*drained(p, TILES[p.sec][tile - 2]))
                    if first:
                        left_ready(w, name)
                    pe.wait_ge(*p.after("gpsimd", "split", u))
                    tot = sum(w["ks"])
                    hi = w_hi[:, slot, 0:nk * n].rearrange("p (k n) -> p k n", k=nk)
                    lo = w_lo[:, slot, 0:nk * n].rearrange("p (k n) -> p k n", k=nk)
                    for k in range(nk):
                        kk = k0 + k
                        if w["lhs"] == "T":
                            for j in range(4):
                                dst = pair[:, j * S:(j + 1) * S]
                                a_hi, a_lo = hi[:, k, j * P:(j + 1) * P], lo[:, k, j * P:(j + 1) * P]
                                for i, (a, b) in enumerate(((a_hi, hT_hi), (a_hi, hT_lo), (a_lo, hT_hi))):
                                    m = pe.matmul(dst, a, b[:, kk, :], start=(kk == 0 and i == 0 and j % 2 == 0),
                                                  stop=(kk == tot - 1 and i == 2 and j % 2 == 1),
                                                  skip_group_check=True)
                        elif w["lhs"] == "narrow":
                            for i, (a, b) in enumerate(((hi, hT_hi), (hi, hT_lo), (lo, hT_hi))):
                                m = pe.matmul(pair[0:n, 0:S], a[:, k, :], b[:, kk, :], start=(kk == 0 and i == 0),
                                              stop=(kk == tot - 1 and i == 2))
                        else:
                            for r in range(R):
                                dst = pair[:, r * 512:r * 512 + n]
                                a_hi, a_lo = lhs(w, kk, r)
                                for i, (a, b) in enumerate(((a_hi, hi), (a_hi, lo), (a_lo, hi))):
                                    m = pe.matmul(dst, a, b[:, k, :], start=(kk == 0 and i == 0),
                                                  stop=(kk == tot - 1 and i == 2))
                    m.then_inc(p.done("mm"), 1)

                def left_ready(w, name):
                    if name in LEFT[p.sec]:
                        for step in LEFT[p.sec][name]:
                            pe.wait_ge(*p.after("vector", *step))

                def take(step, *args):
                    key = (p.sec, step) + args
                    had = had_half[key]
                    if had is not None:
                        pe.wait_ge(*p.after(DRAINER[had[0]], EMPTIED_BY.get(had[0], had[0]), *had[1:]))
                    return chain[half_of[key]]

                def transposes(c, srcs, n=P):
                    for i, v in enumerate(srcs):
                        m = pe.transpose(c[0:n, i * P:i * P + v.shape[0]], v, ident[0:v.shape[0], 0:v.shape[0]])
                    return m

                def memT(r):
                    if r == 0:
                        pe.wait_ge(const_in, 16 * 3)
                        pe.wait_ge(mem_in, 16)
                    c = take("memT", r)
                    transposes(c, [mem_raw[:, r, k * P:(k + 1) * P] for k in range(KD)]).then_inc(p.done("memT"), 1)

                def hT(r):
                    c = take("hT", r)
                    pe.wait_ge(*p.after("vector", "norm_c"))
                    transposes(c, [h_nat[:, r, k * P:(k + 1) * P] for k in range(KD)]).then_inc(p.done("hT"), 1)

                def cwT():
                    pe.wait_ge(par_in, 16 * N_PARAMS)
                    c = take("cwT")
                    transposes(c, [cw_rows[:, l, :] for l in range(DEPTH)]).then_inc(p.done("cwT"), 1)

                def gc_():
                    c = take("gc")
                    pe.wait_ge(*p.after("vector", "ba_c"))
                    for r in range(R):
                        pe.matmul(c[:, r * 8:(r + 1) * 8], triu, gdec[:, r, :], start=(r == 0), stop=False,
                                  skip_group_check=True)
                    pe.matmul(c[:, 16:24], ones, gdec[:, 0, :], start=False, stop=True,
                                    skip_group_check=True).then_inc(p.done("gc"), 1)

                def stat(w, g):
                    c = take("stat", w, g)
                    pe.wait_ge(*p.after("scalar", "stat", w, g))
                    for r in range(R):
                        for j in range(4):
                            m = pe.matmul(c[:, r * 4 + j:r * 4 + j + 1], sq[:, j, r * P:(r + 1) * P], ones[:, 0:1],
                                          start=(r == 0 and j == 0), stop=(r == 1 and j == 3), skip_group_check=True)
                    m.then_inc(p.done("stat"), 1)

                def dec(g, r):
                    c = take("dec", g, r)
                    pe.wait_ge(*p.after("vector", "rn", g))
                    for j in range(4):
                        pe.matmul(c[:, j * P:(j + 1) * P], gdec[:, r, 4 * g + j:4 * g + j + 1].broadcast_to([P, P]), triu,
                                  start=(j == 0), stop=(j == 3), skip_group_check=True)
                    for j in range(4):
                        m = pe.matmul(c[:, 512 + j * P:512 + (j + 1) * P], av[:, r, j:j + 1].broadcast_to([P, P]), ident,
                                      start=(j == 0), stop=(j == 3), skip_group_check=True)
                    m.then_inc(p.done("dec"), 1)

                def four(c, pairs):
                    for j, (a, b) in enumerate(pairs):
                        m = pe.matmul(c[:, j * P:(j + 1) * P], a, b, start=(j == 0), stop=(j == 3),
                                      skip_group_check=True)
                    return m

                def cst_t(w, j, r):
                    return cs[:, w, j, r * P:(r + 1) * P]

                def kk(g, r):
                    c = take("kk", g, r)
                    four(c, [(cst_t(1, j, r), cst_t(1, j, r)) for j in range(4)]).then_inc(p.done("kk"), 1)

                def x1(g, r):
                    c = take("x1", g, r)
                    pe.wait_ge(*p.after("vector", "kk", g, r))
                    transposes(c, [xt[:, r, j, :] for j in range(4)]).then_inc(p.done("x1"), 1)

                def kT(g):
                    c = take("kT", g)
                    transposes(c, [cst_t(1, j, 0) for j in range(4)]).then_inc(p.done("kT"), 1)

                def vT(g):
                    c = take("vT", g)
                    pe.wait_ge(*p.after("scalar", "conv", 2, g))
                    transposes(c, [cst_t(2, j, r) for r in range(R) for j in range(4)]).then_inc(p.done("vT"), 1)

                def invY(g, r, n):
                    c = take("invY", g, r, n)
                    if n == 0:
                        pe.wait_ge(*p.after("scalar", "x1", g, r))
                    else:
                        pe.wait_ge(*p.after("vector", "invZ", g, r, n - 1))
                    four(c, [(lt[:, r, j, :], xx[:, r, j, :]) for j in range(4)]).then_inc(p.done("invY"), 1)

                def invZ(g, r, n):
                    c = take("invZ", g, r, n)
                    pe.wait_ge(*p.after("vector", "invY", g, r, n))
                    if n < len(LEVELS) - 1:
                        four(c[:, 0:512], [(xt[:, r, j, :], yy[:, r, j, :]) for j in range(4)])
                    four(c[:, 512:1024], [(yy[:, r, j, :], xt[:, r, j, :]) for j in range(4)]).then_inc(
                            p.done("invZ"), 1)

                def kq(g, r):
                    c = take("kq", g, r)
                    four(c, [(cst_t(1, j, r), cst_t(0, j, r)) for j in range(4)]).then_inc(p.done("kq"), 1)

                def u_(g, r):
                    c = take("u", g, r)
                    pe.wait_ge(*p.after("vector", "invZ", g, r, len(LEVELS) - 1))
                    pe.wait_ge(*p.after("vector", *(("vT", g) if r == 0 else ("ks", g))))
                    four(c, [(xt[:, r, j, :], vb[:, r, j, :]) for j in range(4)]).then_inc(p.done("u"), 1)

                def st_(g):
                    c = take("st", g)
                    pe.wait_ge(*p.after("vector", "kT", g))
                    pe.wait_ge(*p.after("scalar", "u", g, 0))
                    four(c, [(kd[:, j, :], uu[:, 0, j, :]) for j in range(4)]).then_inc(p.done("st"), 1)

                def ks(g):
                    c = take("ks", g)
                    pe.wait_ge(*p.after("scalar", "st", g))
                    four(c, [(cst_t(1, j, 1), st[:, j, :]) for j in range(4)]).then_inc(p.done("ks"), 1)

                def o_(g, r):
                    c = take("o", g, r)
                    pe.wait_ge(*p.after("vector", "kq", g, r))
                    pe.wait_ge(*p.after("scalar", "u", g, r))
                    m = four(c[:, 0:512], [(lt[:, r, j, :], uu[:, r, j, :]) for j in range(4)])
                    if r == 1:
                        m = four(c[:, 512:1024], [(cst_t(0, j, 1), st[:, j, :]) for j in range(4)])
                    m.then_inc(p.done("o"), 1)

                def iT(r):
                    c = take("iT", r)
                    pe.wait_ge(*p.after("vector", "rope_i"))
                    transposes(c, [pi[:, r, n * P:(n + 1) * P] for n in range(4)]
                                     + [kk2[:, r, :, :].rearrange("p a b -> p (a b)")]).then_inc(p.done("iT"), 1)

                def raw_(qb, part):
                    c = take("raw", qb, part)
                    pe.wait_ge(*p.after("scalar", "iT", R - 1))
                    nk = P * (qb + 1)
                    per = 1024 // nk
                    for i in range(per):
                        h = part * per + bank_order(i, per)
                        lo_ = 64 * (h % 2)
                        m = pe.matmul(c[:, i * nk:(i + 1) * nk], qiT[lo_:lo_ + 64, h // 2, qb * P:(qb + 1) * P],
                                      kiT[lo_:lo_ + 64, 0:nk], start=(i * nk % 512 == 0),
                                      stop=((i + 1) * nk % 512 == 0), skip_group_check=True)
                    m.then_inc(p.done("raw"), 1)

                def qT(r):
                    c = take("qT", r)
                    pe.wait_ge(*p.after("vector", "rope_a"))
                    transposes(c, [pq[:, r, h * P:(h + 1) * P] for h in range(8)]).then_inc(p.done("qT"), 1)

                def kaT_():
                    c = take("kaT")
                    transposes(c, [pq[:, r, D + kv * P:D + (kv + 1) * P] for kv in range(2) for r in range(R)]).then_inc(
                            p.done("kaT"), 1)

                def sc(kv, qb):
                    c = take("sc", kv, qb)
                    pe.wait_ge(*p.after("scalar", "qT", 1))
                    pe.wait_ge(*p.after("scalar", "kaT"))
                    nk = P * (qb + 1)
                    for j in range(4):
                        m = pe.matmul(c[:, j * nk:(j + 1) * nk], qaT[:, 4 * kv + j, qb * P:(qb + 1) * P],
                                      kaT[:, kv, 0:nk], start=(j * nk % 512 == 0), stop=((j + 1) * nk % 512 == 0),
                                      skip_group_check=True)
                    m.then_inc(p.done("sc"), 1)

                def pT(kv, qb):
                    c = take("pT", kv, qb)
                    pe.wait_ge(*p.after("scalar", "sc", kv, qb))
                    transposes(c, [pr[qb][:, i * P:(i + 1) * P] for i in range(4 * (qb + 1))]).then_inc(p.done("pT"), 1)

                def pv(kv, qb):
                    c = take("pv", kv, qb)
                    pe.wait_ge(*p.after("scalar", "pT", kv, qb))
                    for j in range(4):
                        for k in range(qb + 1):
                            i = j * (qb + 1) + k
                            m = pe.matmul(c[:, j * P:(j + 1) * P], pt[qb][:, i * P:(i + 1) * P],
                                          pq[:, k, 1280 + kv * P:1280 + (kv + 1) * P],
                                          start=(j == 0 and k == 0), stop=(j == 3 and k == qb), skip_group_check=True)
                    m.then_inc(p.done("pv"), 1)

                def mT(r):
                    c = take("mT", r)
                    pe.wait_ge(*p.after("vector", "mix", r))
                    transposes(c, [g0[:, r, k * P:(k + 1) * P] for k in range(KD)]).then_inc(p.done("mT"), 1)

                def xT(r):
                    c = take("xT", r)
                    if r == 0:
                        pe.wait_ge(*p.after("vector", "params2"))
                    transposes(c, [xs[:, r, k * P:(k + 1) * P] for k in range(KD)]).then_inc(p.done("xT"), 1)

                def ckT(r):
                    c = take("ckT", r)
                    pe.wait_ge(*p.after("vector", "lat_c"))
                    transposes(c, [h2[:, r, k * P:(k + 1) * P] for k in range(5)]).then_inc(p.done("ckT"), 1)

                def narrow_T(step):
                    c = take(step)
                    pe.wait_ge(*p.after("vector", "drain_v", "ba" if step == "baT" else "ki"))
                    transposes(c, [narrow[0:NARROW, r * P:(r + 1) * P] for r in range(R)]).then_inc(p.done(step), 1)

                def baT():
                    narrow_T("baT")

                def kxT():
                    narrow_T("kxT")

                def qk2T(n, part=0):
                    c = take("qk2T", n) if n != MLA or not part else take("qk2T", n, part)
                    if n == MLA:
                        pe.wait_ge(*p.after("vector", "rope_2"))
                        src = (q2, kc)[part]
                        return transposes(c, [src[:, r, h * 96:(h + 1) * 96] for h in range(4) for r in range(R)],
                                                96).then_inc(p.done("qk2T"), 1)
                    pe.wait_ge(*p.after("scalar", "drain_s", "h2" if n == 1 else "h4"))
                    q0 = Q_OF[n]
                    k_src, k0 = (mkv_now, 0) if n == MEM else (h2, q0 + S)
                    transposes(c, [h2[:, r, q0 + i * P:q0 + (i + 1) * P] for i in range(2) for r in range(R)]
                                     + [k_src[:, r, k0 + i * P:k0 + (i + 1) * P] for i in range(2) for r in range(R)]).then_inc(
                                             p.done("qk2T"), 1)

                def sbz(k):
                    c = take("sbz", k)
                    pe.wait_ge(*p.after("scalar", "qk2T", 1))
                    n = S - k * P
                    for q in range(4):
                        h = head_of(1, q)
                        m = pe.matmul(c[:, q * S:q * S + n], head_T(1, h, 1, slice(k * P, (k + 1) * P)),
                                      head_T(1, h, 0, slice(k * P, S)), start=(q % 2 == 0), stop=(q % 2 == 1),
                                      skip_group_check=True)
                    m.then_inc(p.done("sbz"), 1)

                def sbi(k):
                    c = take("sbi", k)
                    tril = cst[:, K_TRIL:K_TRIL + P]
                    pe.wait_ge(*p.after("vector", "sbm", 1))
                    if k == 1:
                        return pe.matmul(c[:, 0:512], tril, pt2[0], start=True, stop=True).then_inc(p.done("sbi"), 1)
                    for b in range(2):
                        pe.matmul(c[:, b * 512:(b + 1) * 512], tril, pt2[1][:, b * 512:(b + 1) * 512], start=True,
                                  stop=False, skip_group_check=True)
                        for q in (2 * b, 2 * b + 1):
                            m = pe.matmul(c[:, q * S + P:(q + 1) * S], ones, pt2[0][:, q * P:(q + 1) * P],
                                          start=False, stop=(q % 2 == 1), skip_group_check=True)
                    m.then_inc(p.done("sbi"), 1)

                def sbo(qb):
                    c = take("sbo", qb)
                    pe.wait_ge(*p.after("scalar", "sbe", 1))
                    for q in range(4):
                        h = head_of(1, q)
                        for k in range(qb + 1):
                            a = (pr2[1][:, q * S + qb * P:q * S + (qb + 1) * P] if k == 0
                                 else pr2[0][:, q * P:(q + 1) * P])
                            m = pe.matmul(c[:, h * 64:(h + 1) * 64], a, values(1, h, k), start=(q == 0 and k == 0),
                                          stop=(q == 3 and k == qb), skip_group_check=True)
                    m.then_inc(p.done("sbo"), 1)

                def fc():
                    c = take("fc")
                    pe.wait_ge(*p.after("vector", "ff_c"))
                    pe.matmul(c[:, 0:4], triu, fy[:, 2, 0, :], start=True, stop=False, skip_group_check=True)
                    pe.matmul(c[:, 4:8], ones, fy[:, 2, 0, :], start=False, stop=False, skip_group_check=True)
                    pe.matmul(c[:, 4:8], triu, fy[:, 2, 1, :], start=False, stop=True, skip_group_check=True).then_inc(
                            p.done("fc"), 1)

                def fb():
                    c = take("fb")
                    for q in range(4):
                        h = head_of(FOX, q)
                        row = [fy[:, 2, r, h:h + 1].broadcast_to([P, P]) for r in range(R)]
                        pe.matmul(c[:, q * S:q * S + P], row[0], triu, start=(q % 2 == 0), stop=False,
                                  skip_group_check=True)
                        pe.matmul(c[:, q * S + P:(q + 1) * S], row[0], ones, start=False, stop=False,
                                  skip_group_check=True)
                        m = pe.matmul(c[:, q * S + P:(q + 1) * S], row[1], triu, start=False, stop=(q % 2 == 1),
                                      skip_group_check=True)
                    m.then_inc(p.done("fb"), 1)

                def sc2(n, qb):
                    c = take("sc2", n, qb)
                    pe.wait_ge(*p.after("scalar", "qk2T", *((n, 1) if n == MLA else (n,))))
                    nk = keys_of(n, qb)
                    for q in range(4):
                        h = head_of(n, q)
                        m = pe.matmul(c[:, q * S:q * S + nk], head_T(n, h, 0, slice(qb * P, (qb + 1) * P)),
                                      head_T(n, h, 1, slice(0, nk)), start=(q % 2 == 0), stop=(q % 2 == 1),
                                      skip_group_check=True)
                    m.then_inc(p.done("sc2"), 1)

                def p2T(n, qb):
                    c = take("p2T", n, qb)
                    pe.wait_ge(*p.after("scalar", "sc2", n, qb))
                    src = pr2[buf_of(n, qb)]
                    transposes(c, [src[:, i * P:(i + 1) * P] for i in range(4 * keys_of(n, qb) // P)]).then_inc(
                            p.done("p2T"), 1)

                def pv2(n, qb):
                    c = take("pv2", n, qb)
                    pe.wait_ge(*p.after("scalar", "p2T", n, qb))
                    nt = keys_of(n, qb) // P
                    for q in range(4):
                        h = head_of(n, q)
                        for k in range(nt):
                            i = q * nt + k
                            m = pe.matmul(c[:, h * 64:(h + 1) * 64], pt2[buf_of(n, qb)][:, i * P:(i + 1) * P],
                                          values(n, h, k), start=(q == 0 and k == 0),
                                          stop=(q == 3 and k == nt - 1), skip_group_check=True)
                    m.then_inc(p.done("pv2"), 1)

                def yT(n):
                    c = take("yT", n)
                    pe.wait_ge(*p.after("vector", "gy", n))
                    g_0 = B_GATE + n * S
                    transposes(c, [h2[:, r, g_0 + k * P:g_0 + (k + 1) * P] for r in range(R) for k in range(2)]).then_inc(
                            p.done("yT"), 1)

                def gT(r):
                    c = take("gT", r)
                    pe.wait_ge(*p.after("vector", "drain_v", "br01"))
                    transposes(c, [merged[:, r, k * P:(k + 1) * P] for k in range(KD)]).then_inc(p.done("gT"), 1)

                return dict(baT=baT, kxT=kxT, xT=xT, ckT=ckT, qk2T=qk2T, sbz=sbz, sbi=sbi, sbo=sbo, fc=fc, fb=fb, sc2=sc2,
                            p2T=p2T, pv2=pv2, yT=yT, gT=gT, mm=mm, memT=memT, hT=hT, cwT=cwT, gc=gc_, stat=stat, dec=dec, kk=kk, x1=x1, kT=kT, vT=vT,
                            invY=invY, invZ=invZ, kq=kq, u=u_, st=st_, ks=ks, o=o_, iT=iT, raw=raw_, qT=qT, kaT=kaT_,
                            sc=sc, pT=pT, pv=pv, mT=mT)

            run(pe, "tensor", handlers)

        @block.scalar
        def _(act):
            A = act.activation

            def handlers(p):
                def split(u):
                    _, w, _, nk, _, _ = UNITS[p.sec][u]
                    n = nk * w["n"]
                    act.wait_ge(*slot_value(p.sec, p.l, u))
                    if p.sec != "mem" or u >= SPLIT_SLOTS:
                        act.wait_ge(*unit_before(p, "tensor", "mm", u, SPLIT_SLOTS))
                    A(w_hi[:, u % SPLIT_SLOTS, 0:n], raw[:, u % RAW_SLOTS, 0:n], ACT.Copy).then_inc(p.done("split"), 1)

                def tile_in(name):
                    names = [x for x, _ in TILES[p.sec]]
                    last = max(u for u, x in enumerate(UNITS[p.sec]) if x[0] == name)
                    act.wait_ge(*p.after("tensor", "mm", last))
                    i = names.index(name)
                    return bulk[i % 2], dict(TILES[p.sec])[name]

                def rows(b, n):
                    return b[:, :].rearrange("p (r n) -> p r n", r=R)[:, :, 0:n]

                def drain(name):
                    b, w = tile_in(name)
                    if name[:3] == "mkv":
                        return A(mkv[:, int(name[3]), :, :], rows(b, 512), ACT.Copy).then_inc(p.done("drain_s"), 1)
                    if name == "qi":
                        return A(pi[:, :, 0:512], rows(b, 512), ACT.Copy).then_inc(p.done("drain_s"), 1)
                    if name == "kv":
                        return A(pq[:, :, 1024:1536], rows(b, 512), ACT.Copy).then_inc(p.done("drain_s"), 1)
                    if name[:2] == "qa":
                        c = int(name[2]) * 512
                        return A(pq[:, :, c:c + 512], rows(b, 512), ACT.Copy).then_inc(p.done("drain_s"), 1)
                    if name[:2] in ("za", "zb"):
                        c = int(name[2]) * 512
                        dst = (g0 if name[1] == "a" else g1)[:, :, c:c + 512]
                        if name == "za0":
                            act.wait_ge(*p.after("vector", "rope_a"))
                        return A(dst, rows(b, 512), ACT.Silu).then_inc(p.done("drain_s"), 1)
                    if name[0] == "g" and p.sec == "one":
                        prev = {"g01": "g00", "g10": "g01", "g11": "g10"}.get(name)
                        if prev:
                            act.wait_ge(*p.after("vector", "gmul", prev))
                        return A(gain2[:, :].rearrange("p (r n) -> p r n", r=R), rows(b, 512), ACT.Sigmoid).then_inc(
                                p.done("drain_s"), 1)
                    return drain_two(name, b, w)

                def drain_two(name, b, w):
                    n = w["n"]
                    if name[0] == "h":
                        return A(h2[:, :, w["col"]:w["col"] + n], rows(b, n), ACT.Copy).then_inc(p.done("drain_s"), 1)
                    if name == "qb":
                        return A(q2[:, :, :], rows(b, n), ACT.Copy).then_inc(p.done("drain_s"), 1)
                    if name == "kvb":
                        return A(kv2[:, :, :], rows(b, n), ACT.Copy).then_inc(p.done("drain_s"), 1)
                    if name[:2] == "gz":
                        return A(h2[:, :, w["col"]:w["col"] + n], rows(b, n), ACT.Silu).then_inc(p.done("drain_s"), 1)
                    if name[:2] == "mu":
                        return A(mg[:, :, w["col"]:w["col"] + n], rows(b, n), ACT.Sigmoid).then_inc(
                                p.done("drain_s"), 1)
                    raise NotImplementedError(name)

                def conv_silu(w, g):
                    act.wait_ge(*p.after("vector", "tap", w, g))
                    if (w, g) == (0, 1):
                        act.wait_ge(*p.after("tensor", "o", 0, 1))
                    A(cs[:, w, :, :], cv[:, :, :], ACT.Silu).then_inc(p.done("conv"), 1)

                def conv_tap(w, g):
                    b, _ = tile_in(f"c{w}{g}")
                    if (w, g) != (0, 0):
                        act.wait_ge(*p.after("scalar", "conv", *CONV_BEFORE[(w, g)]))
                    for j in range(4):
                        c = 3 * 24 + w * 8 + g * 4 + j
                        ins = A(cv[:, j, :], b[:, j * S:(j + 1) * S], ACT.Copy, scale=taps[:, c:c + 1])
                    ins.then_inc(p.done("tap"), 1)

                def high_T(step, r):
                    src = half(step, r)[:, :].rearrange("p (k n) -> p k n", k=KD)
                    return A(hT_hi[:, :, r * P:(r + 1) * P], src, ACT.Copy)

                def hT(r):
                    act.wait_ge(*p.after("tensor", "hT", r))
                    high_T("hT", r).then_inc(p.done("hT"), 1)

                def xT(r):
                    act.wait_ge(*p.after("tensor", "xT", r))
                    high_T("xT", r).then_inc(p.done("xT"), 1)

                def mT(r):
                    act.wait_ge(*p.after("tensor", "mm", max(u for u, x in enumerate(UNITS["one"]) if x[0] == "g11")))
                    act.wait_ge(*p.after("tensor", "mT", r))
                    high_T("mT", r).then_inc(p.done("mT"), 1)

                def gT(r):
                    act.wait_ge(*p.after("tensor", "mm", max(u for u, x in enumerate(UNITS["two"]) if x[0] == "br01")))
                    act.wait_ge(*p.after("tensor", "gT", r))
                    high_T("gT", r).then_inc(p.done("gT"), 1)

                def norm_a():
                    if p.sec == "one":
                        act.wait_ge(x_in, 16)
                        act.wait_ge(*p.after("vector", "params"))
                        A(h_nat[:, 1, :], xs[:, 1, :], ACT.Square, accum_out=nrm[:, 2, 1:2]).then_inc(
                                p.done("norm_a"), 1)

                def ln_a():
                    act.wait_ge(*p.after("vector", "drain_v", "o1"))
                    x, m = xs[:, 1, :], lnm[:, 0, 1:2]
                    A(h2[:, 1, 0:D], x, ACT.Copy, accum_out=m).then_inc(p.own, 1)
                    act.wait_ge(*p.last())
                    A(m, m, ACT.Copy, scale=-1.0 / D).then_inc(p.own, 1)
                    act.wait_ge(*p.last())
                    A(x, x, ACT.Identity, bias=m).then_inc(p.own, 1)
                    act.wait_ge(*p.last())
                    A(h2[:, 1, 0:D], x, ACT.Square, accum_out=lnm[:, 1, 1:2]).then_inc(p.done("ln_a"), 1)

                def norm():
                    act.wait_ge(*p.after("vector", "norm_a"))
                    rsq(nrm[:, 0, :], nrm[:, 1, :]).then_inc(p.done("norm"), 1)

                def rsq(src, dst):
                    A(dst, src, ACT.Ln).then_inc(p.own, 1)
                    act.wait_ge(*p.last())
                    return A(dst, dst, ACT.Exp, scale=-0.5)

                def ba_b():
                    act.wait_ge(*p.after("vector", "ba_a"))
                    A(be[:, :, :], ba[:, :, 0:8], ACT.Exp, scale=-1.0)
                    A(ea, a_log, ACT.Exp)
                    A(eb[:, :, :], ay[:, 1, :, :], ACT.Exp, scale=-1.0).then_inc(p.own, 1)
                    act.wait_ge(*p.last())
                    A(eb[:, :, :], eb[:, :, :], ACT.Ln, bias=1.0).then_inc(p.done("ba_b"), 1)

                def gc_b():
                    act.wait_ge(*p.after("vector", "gc"))
                    A(egc[:, :, :], gc[:, :, :], ACT.Exp)
                    A(wl[:, 0, :], wl[:, 1, :], ACT.Exp).then_inc(p.done("gc_b"), 1)

                def stat(w, g):
                    act.wait_ge(*p.after("scalar", "conv", w, g))
                    if (w, g) != (0, 0):
                        act.wait_ge(*p.after("tensor", "stat", *((0, g) if w else (1, 0))))
                    A(sq[:, :, :], cs[:, w, :, :], ACT.Square).then_inc(p.done("stat"), 1)

                def rn(g):
                    act.wait_ge(*p.after("vector", "stat", 1, g))
                    rsq(s2[:, :, :, :], ss[:, :, :, :]).then_inc(p.done("rn"), 1)

                def dec_b(g, r):
                    act.wait_ge(*p.after("vector", "dec", g, r))
                    A(dt_[:, r, :, :], dt_[:, r, :, :], ACT.Exp).then_inc(p.done("dec_b"), 1)

                def x1(g, r):
                    act.wait_ge(*p.after("tensor", "x1", g, r))
                    A(xx[:, r, :, :], heads(half("x1", g, r)[:, 0:512]), ACT.Copy).then_inc(p.done("x1"), 1)

                def half(*key):
                    return chain[half_of[(p.sec,) + key]]

                def u_(g, r):
                    act.wait_ge(*p.after("tensor", "u", g, r))
                    A(uu[:, r, :, :], heads(half("u", g, r)[:, 0:512]), ACT.Copy).then_inc(p.done("u"), 1)

                def st_(g):
                    act.wait_ge(*p.after("tensor", "st", g))
                    A(st[:, :, :], heads(half("st", g)[:, 0:512]), ACT.Copy).then_inc(p.done("st"), 1)

                def onorm():
                    act.wait_ge(*p.after("vector", "onorm_a"))
                    rsq(so[:, 0, :, :], so[:, 1, :, :]).then_inc(p.done("onorm"), 1)

                def kinorm():
                    act.wait_ge(*p.after("vector", "kinorm_a"))
                    rsq(kn[:, 0, :], kn[:, 1, :]).then_inc(p.done("kinorm"), 1)

                def iT(r):
                    act.wait_ge(*p.after("tensor", "iT", r))
                    if r == 0:
                        act.wait_ge(*p.after("tensor", "o", 1, 1))
                    c = half("iT", r)
                    A(qiT[:, :, r * P:(r + 1) * P], heads(c[:, 0:512]), ACT.Copy)
                    A(kiT[:, r * P:(r + 1) * P], c[:, 512:640], ACT.Copy).then_inc(p.done("iT"), 1)

                def raw_(qb, part):
                    act.wait_ge(*p.after("tensor", "raw", qb, part))
                    prev = {(1, 0): (0, 0), (1, 1): (1, 0)}.get((qb, part))
                    if prev:
                        act.wait_ge(*p.after("vector", "raw", *prev))
                    A(rl, half("raw", qb, part)[:, :], ACT.Relu).then_inc(p.done("raw"), 1)

                def qT(r):
                    act.wait_ge(*p.after("tensor", "qT", r))
                    A(qaT[:, :, r * P:(r + 1) * P], heads(half("qT", r)[:, :], 8), ACT.Copy).then_inc(p.done("qT"), 1)

                def kaT_():
                    act.wait_ge(*p.after("tensor", "kaT"))
                    A(kaT[:, :, :].rearrange("p a n -> p (a n)"), half("kaT")[:, 0:512], ACT.Copy).then_inc(
                            p.done("kaT"), 1)

                def sc(kv, qb):
                    act.wait_ge(*p.after("vector", "sc", kv, qb))
                    nk = P * (qb + 1)
                    if kv:
                        act.wait_ge(*p.after("vector", "pv", 0, qb))
                    for j in range(4):
                        v = pr[qb][:, j * nk:(j + 1) * nk]
                        ins = A(v, v, ACT.Exp, bias=mx[qb][:, j:j + 1], accum_out=rs[qb][:, j:j + 1])
                    ins.then_inc(p.done("sc"), 1)

                def pT(kv, qb):
                    act.wait_ge(*p.after("tensor", "pT", kv, qb))
                    if kv:
                        act.wait_ge(*p.after("tensor", "pv", 0, qb))
                    n = 512 * (qb + 1)
                    A(pt[qb][:, 0:n], half("pT", kv, qb)[:, 0:n], ACT.Copy).then_inc(p.done("pT"), 1)

                def tables():
                    act.wait_ge(*p.after("vector", "tables_a"))
                    A(sin_t[:, :, :].rearrange("p r n -> p (r n)"), ang[:, 3, :], ACT.Sin)
                    A(ang[:, 4, :], ang[:, 3, :], ACT.Sin, scale=0.5).then_inc(p.done("tables"), 1)

                def lat_():
                    act.wait_ge(*p.after("vector", "lat_a"))
                    rsq(lat[:, 0, :, :], lat[:, 1, :, :]).then_inc(p.done("lat"), 1)

                def qk2T(n, part=0):
                    act.wait_ge(*p.after("tensor", "qk2T", *((n, part) if part else (n,))))
                    c = half("qk2T", *((n, part) if part else (n,)))
                    if n == MEM:
                        act.wait_ge(*p.after("tensor", "sbz", 1))
                    if n == MLA:
                        act.wait_ge(*p.after("tensor", "sc2", FOX, 1))
                        dst = t_parts(n)[part][0:96]
                        return A(dst.rearrange("p a n -> p (a n)"), c[0:96, :], ACT.Copy).then_inc(p.done("qk2T"), 1)
                    reg = reg_a if n == FOX else reg_b
                    A(reg[:, 0:1024], c[:, :], ACT.Copy).then_inc(p.done("qk2T"), 1)

                def sbl(k):
                    act.wait_ge(*p.after("vector", "sbz", k))
                    x = pt2[1 - k]
                    A(x, x, ACT.Exp, scale=-1.0).then_inc(p.own, 1)
                    act.wait_ge(*p.last())
                    A(x, x, ACT.Ln, bias=1.0).then_inc(p.done("sbl"), 1)

                def sbe(k):
                    act.wait_ge(*p.after("vector", "sbi", k))
                    A(pr2[1 - k], pr2[1 - k], ACT.Exp).then_inc(p.done("sbe"), 1)

                def ff():
                    act.wait_ge(*p.after("vector", "ff_a"))
                    A(fy[:, 1, :, :], fy[:, 1, :, :], ACT.Exp, scale=-1.0).then_inc(p.own, 1)
                    act.wait_ge(*p.last())
                    A(fy[:, 1, :, :], fy[:, 1, :, :], ACT.Ln, bias=1.0).then_inc(p.done("ff"), 1)

                def sc2(n, qb):
                    act.wait_ge(*p.after("vector", "sc2", n, qb))
                    nk, b = keys_of(n, qb), buf_of(n, qb)
                    for q in range(4):
                        x, h = pr2[b][:, q * nk:(q + 1) * nk], head_of(n, q)
                        ins = A(x, x, ACT.Exp, bias=mx2[qb][:, q:q + 1], accum_out=rs2[qb][:, h:h + 1])
                    ins.then_inc(p.done("sc2"), 1)

                def p2T(n, qb):
                    act.wait_ge(*p.after("tensor", "p2T", n, qb))
                    prev = user_before(n, qb)
                    if prev:
                        act.wait_ge(*p.after("tensor", "pv2", *prev))
                    k = 4 * keys_of(n, qb)
                    A(pt2[buf_of(n, qb)][:, 0:k], half("p2T", n, qb)[:, 0:k], ACT.Copy).then_inc(p.done("p2T"), 1)

                def ln_s():
                    act.wait_ge(*p.after("vector", "ln_a"))
                    rsq(lnm[:, 2, :], lnm[:, 3, :]).then_inc(p.done("ln_s"), 1)

                return dict(hT=hT, xT=xT, mT=mT, gT=gT, norm_a=norm_a, ln_a=ln_a, lat=lat_, qk2T=qk2T, sbl=sbl, sbe=sbe, ff=ff, sc2=sc2, p2T=p2T, ln_s=ln_s,
                            split=split, drain_s=drain, tap=conv_tap, conv=conv_silu, norm=norm, ba_b=ba_b, gc_b=gc_b,
                            stat=stat, rn=rn, dec_b=dec_b, x1=x1, u=u_, st=st_, onorm=onorm, kinorm=kinorm, iT=iT,
                            raw=raw_, qT=qT, kaT=kaT_, sc=sc, pT=pT, tables=tables)

            run(act, "scalar", handlers)

        @block.vector
        def _(v):
            TT, TS, STT = v.tensor_tensor, v.tensor_scalar, v.scalar_tensor_tensor

            def handlers(p):
                def half(*key):
                    return chain[half_of[(p.sec,) + key]]

                def flat(x):
                    return x.rearrange("p a n -> p (a n)")

                def newton(y, x, tmp):
                    TT(tmp, y, y, ALU.mult).then_inc(p.own, 1)
                    v.wait_ge(*p.last())
                    TT(tmp, tmp, x, ALU.mult).then_inc(p.own, 1)
                    v.wait_ge(*p.last())
                    TS(tmp, tmp, -0.5, 1.5, ALU.mult, ALU.add).then_inc(p.own, 1)
                    v.wait_ge(*p.last())
                    TT(y, y, tmp, ALU.mult).then_inc(p.own, 1)
                    v.wait_ge(*p.last())

                def split_T(c, r, hi, lo, k0, nk):
                    src = c[:, 0:nk * P].rearrange("p (k n) -> p k n", k=nk)
                    rr = slice(r * P, (r + 1) * P)
                    v.tensor_copy(hi[:, k0:k0 + nk, rr], src).then_inc(p.own, 1)
                    v.wait_ge(*p.last())
                    return TT(lo[:, k0:k0 + nk, rr], src, hi[:, k0:k0 + nk, rr].bitcast(F32), ALU.subtract)

                def low_T(c, r):
                    rr = slice(r * P, (r + 1) * P)
                    return TT(hT_lo[:, :, rr], c[:, :].rearrange("p (k n) -> p k n", k=KD),
                              hT_hi[:, :, rr].bitcast(F32), ALU.subtract)

                def memT(r):
                    v.wait_ge(*p.after("tensor", "memT", r))
                    split_T(half("memT", r), r, hT_hi, hT_lo, 0, KD).then_inc(p.done("memT"), 1)

                def tables_a():
                    v.wait_ge(const_in, 48)
                    pf = ang[:, 0, 0:4]
                    v.tensor_copy(pf, pos_i[:, :, :].rearrange("p a r -> p (a r)")).then_inc(p.own, 1)
                    v.wait_ge(*p.last())
                    for r in range(R):
                        TS(ang[:, 1, r * 40:r * 40 + 24], cst[:, K_FREQ:K_FREQ + 24], ang[:, 0, r:r + 1], None, ALU.mult)
                        TS(ang[:, 1, r * 40 + 24:r * 40 + 40], cst[:, K_FREQ + 24:K_FREQ + 40],
                                  ang[:, 0, 2 + r:3 + r], None, ALU.mult).then_inc(p.own, 1)
                        v.wait_ge(*p.last())
                    two_pi = 2 * np.pi
                    c1 = 6.28125
                    c2 = float(np.float32(np.round((two_pi - c1) * 2 ** 24) / 2 ** 24))
                    c3 = float(two_pi - c1 - c2)
                    magic = 1.5 * 2 ** 23
                    TS(ang[:, 2, :], ang[:, 1, :], float(1 / two_pi), magic, ALU.mult, ALU.add).then_inc(p.own, 1)
                    v.wait_ge(*p.last())
                    TS(ang[:, 2, :], ang[:, 2, :], -magic, None, ALU.add).then_inc(p.own, 1)
                    v.wait_ge(*p.last())
                    STT(ang[:, 3, :], ang[:, 2, :], -c1, ang[:, 1, :], ALU.mult, ALU.add).then_inc(p.own, 1)
                    v.wait_ge(*p.last())
                    STT(ang[:, 3, :], ang[:, 2, :], -c2, ang[:, 3, :], ALU.mult, ALU.add).then_inc(p.own, 1)
                    v.wait_ge(*p.last())
                    STT(ang[:, 3, :], ang[:, 2, :], -c3, ang[:, 3, :], ALU.mult, ALU.add).then_inc(p.own, 1)
                    v.wait_ge(*p.last())
                    pi_ = 3.1415925
                    TS(ang[:, 3, :], ang[:, 3, :], pi_, -pi_, ALU.min, ALU.max).then_inc(p.done("tables_a"), 1)

                def tables_c():
                    v.wait_ge(*p.after("scalar", "tables"))
                    TT(ang[:, 4, :], ang[:, 4, :], ang[:, 4, :], ALU.mult).then_inc(p.own, 1)
                    v.wait_ge(*p.last())
                    TS(cos_t[:, :, :].rearrange("p r n -> p (r n)"), ang[:, 4, :], -2.0, 1.0,
                                  ALU.mult, ALU.add).then_inc(p.done("tables_c"), 1)
                    v.wait_ge(*p.here("tables_c"))

                def cwT():
                    v.wait_ge(*p.after("tensor", "cwT"))
                    c = half("cwT")
                    v.tensor_copy(par1[:, :, 0:96], c[:, 0:2 * P].rearrange("p (l n) -> p l n", l=DEPTH)[:, :, 0:96]).then_inc(
                            p.done("cwT"), 1)
                    v.wait_ge(*p.here("cwT"))

                def params():
                    ins = v.tensor_copy(now1[:, :], par1[:, bass.ds(p.l, 1), :].rearrange("p a n -> p (a n)"))
                    ins.then_inc(p.done("params"), 1)
                    v.wait_ge(*p.here("params"))

                def norm_a():
                    v.wait_ge(x_in, 16)
                    for r in range(1 if p.sec == "one" else R):
                        ins = v.tensor_tensor_reduce(h_nat[:, r, :], xs[:, r, :], xs[:, r, :], 1.0, 0.0,
                                                     ALU.mult, ALU.add, nrm[:, 2, r:r + 1])
                    ins.then_inc(p.own, 1)
                    v.wait_ge(*p.last())
                    if p.sec == "one":
                        v.wait_ge(*p.after("scalar", "norm_a"))
                    TS(nrm[:, 0, :], nrm[:, 2, :], 1.0 / D, EPS, ALU.mult, ALU.add).then_inc(p.done("norm_a"), 1)

                def norm_c():
                    v.wait_ge(*p.after("scalar", "norm"))
                    newton(nrm[:, 1, :], nrm[:, 0, :], nrm[:, 3, :])
                    v.wait_ge(gain_in, 16 * (p.l + 1) if p.sec == "one" else 16 * (DEPTH + 1))
                    for r in range(R):
                        dst = h_nat if p.sec == "one" else xs
                        ins = STT(dst[:, r, :], xs[:, r, :], nrm[:, 1, r:r + 1], gain[:, :], ALU.mult, ALU.mult)
                        if r == 0:
                            ins.then_inc(p.own, 1)
                            v.wait_ge(*p.last())
                    ins.then_inc(p.done("norm_c"), 1)
                    v.wait_ge(*p.here("norm_c"))

                def hT(r):
                    v.wait_ge(*p.after("scalar", "hT", r))
                    low_T(half("hT", r), r).then_inc(p.done("hT"), 1)

                def tile_in(name):
                    names = [x for x, _ in TILES[p.sec]]
                    v.wait_ge(*p.after("tensor", "mm", max(u for u, x in enumerate(UNITS[p.sec]) if x[0] == name)))
                    return bulk[names.index(name) % 2]

                def rows(b, n):
                    return b[:, :].rearrange("p (r n) -> p r n", r=R)[:, :, 0:n]

                def drain(name):
                    b = tile_in(name)
                    if name in ("ba", "ki"):
                        v.tensor_copy(narrow[0:NARROW, :], b[0:NARROW, 0:S]).then_inc(p.done("drain_v"), 1)
                        return None
                    if p.sec == "one":
                        xv = xs[:, :, int(name[1]) * 512:int(name[1]) * 512 + 512]
                        TT(xv, xv, rows(b, 512), ALU.add).then_inc(p.done("drain_v"), 1)
                        v.wait_ge(*p.here("drain_v"))
                        return None
                    drain_two(name, b)

                def baT():
                    v.wait_ge(*p.after("tensor", "baT"))
                    v.tensor_copy(ba[:, :, :], half("baT")[:, 0:2 * P].rearrange("p (r n) -> p r n", r=R)[
                        :, :, NARROW - 16:NARROW]).then_inc(
                        p.done("baT"), 1)
                    v.wait_ge(*p.here("baT"))

                def kxT():
                    v.wait_ge(*p.after("tensor", "kxT"))
                    v.tensor_copy(pi[:, :, 512:584],
                                  half("kxT")[:, 0:2 * P].rearrange("p (r n) -> p r n", r=R)[:, :, 0:NARROW]).then_inc(
                        p.done("kxT"), 1)
                    v.wait_ge(*p.here("kxT"))

                def drain_two(name, b):
                    if name == "mr":
                        v.tensor_copy(sT_hi[:, 5, :], b[:, 0:S]).then_inc(p.own, 1)
                        v.wait_ge(*p.last())
                        TT(sT_lo[:, 5, :], b[:, 0:S], sT_hi[:, 5, :].bitcast(F32), ALU.subtract).then_inc(
                            p.done("drain_v"), 1)
                        return None
                    c = int(name[-1]) * 512
                    if name[0] == "o":
                        xv = xs[:, :, c:c + 512]
                        STT(xv, xv, ALPHA, rows(b, 512), ALU.mult, ALU.add).then_inc(p.done("drain_v"), 1)
                        v.wait_ge(*p.here("drain_v"))
                        return None
                    n = int(name[2])
                    m = mg[:, :, n * D + c:n * D + c + 512]
                    v.wait_ge(*p.after("scalar", "drain_s", f"mu{2 * n + c // 512}"))
                    if n == 1:
                        TT(merged[:, :, c:c + 512], m, rows(b, 512), ALU.mult).then_inc(p.done("drain_v"), 1)
                        v.wait_ge(*p.here("drain_v"))
                        return None
                    TT(m, m, rows(b, 512), ALU.mult).then_inc(p.own, 1)
                    v.wait_ge(*p.last())
                    TT(merged[:, :, c:c + 512], merged[:, :, c:c + 512], m, ALU.add).then_inc(p.done("drain_v"), 1)
                    v.wait_ge(*p.here("drain_v"))

                def gmul(name):
                    v.wait_ge(*p.after("scalar", "drain_s", name))
                    c = int(name[2]) * 512
                    gv = (g0 if name[1] == "0" else g1)[:, :, c:c + 512]
                    TT(gv, gv, gain2[:, :].rearrange("p (r n) -> p r n", r=R), ALU.mult).then_inc(p.done("gmul"), 1)
                    v.wait_ge(*p.here("gmul"))

                def tap(w, g):
                    v.wait_ge(*p.after("scalar", "tap", w, g))
                    b = tile_in(f"c{w}{g}")
                    for k in range(3):
                        back = 3 - k
                        for j in range(4):
                            c = k * 24 + w * 8 + g * 4 + j
                            ins = STT(cv[:, j, back:S], b[:, j * S:(j + 1) * S - back], taps[:, c:c + 1],
                                      cv[:, j, back:S], ALU.mult, ALU.add)
                            if k < 2 or j < 3:
                                ins.then_inc(p.own, 1)
                                v.wait_ge(*p.last())
                    ins.then_inc(p.done("tap"), 1)

                def ba_a():
                    y = ay[:, 0, :, :]
                    TT(y, ba[:, :, 8:16], over(dt_bias, R), ALU.add).then_inc(p.own, 1)
                    v.wait_ge(*p.last())
                    STT(ay[:, 1, :, :], y, -1.0, y, ALU.mult, ALU.max).then_inc(p.done("ba_a"), 1)

                def ba_c():
                    v.wait_ge(*p.after("scalar", "ba_b"))
                    TS(be[:, :, :], be[:, :, :], 1.0, None, ALU.add).then_inc(p.own, 1)
                    v.wait_ge(*p.last())
                    v.reciprocal(be[:, :, :], be[:, :, :]).then_inc(p.own, 1)
                    v.wait_ge(*p.last())
                    TS(ay[:, 0, :, :], ay[:, 0, :, :], 0.0, None, ALU.max).then_inc(p.own, 1)
                    v.wait_ge(*p.last())
                    TT(ay[:, 0, :, :], ay[:, 0, :, :], eb[:, :, :], ALU.add).then_inc(p.own, 1)
                    v.wait_ge(*p.last())
                    TS(ea, ea, -1.0, None, ALU.mult).then_inc(p.own, 1)
                    v.wait_ge(*p.last())
                    TT(gdec[:, :, :], ay[:, 0, :, :], over(ea, R), ALU.mult).then_inc(p.done("ba_c"), 1)
                    v.wait_ge(*p.here("ba_c"))

                def gc_():
                    v.wait_ge(*p.after("tensor", "gc"))
                    c = half("gc")
                    v.tensor_copy(gc[:, :, :].rearrange("p r n -> p (r n)"), c[:, 0:16]).then_inc(p.own, 1)
                    v.wait_ge(*p.last())
                    TT(wl[:, 1, :], c[:, 16:24], gc[:, 0, :], ALU.subtract).then_inc(p.done("gc"), 1)
                    v.wait_ge(*p.here("gc"))

                def stat(w, g):
                    v.wait_ge(*p.after("tensor", "stat", w, g))
                    TS(s2[:, w, :, :].rearrange("p r n -> p (r n)"), half("stat", w, g)[:, 0:8], EPS, None,
                                  ALU.add).then_inc(p.done("stat"), 1)
                    v.wait_ge(*p.here("stat"))

                def rn(g):
                    v.wait_ge(*p.after("scalar", "rn", g))
                    newton(f3(ss), f3(s2), f3(s3))
                    hs = slice(4 * g, 4 * g + 4)
                    TT(av[:, :, :], be[:, :, hs], ss[:, 1, :, :], ALU.mult).then_inc(p.own, 1)
                    v.wait_ge(*p.last())
                    TS(ss[:, 0, :, :], ss[:, 0, :, :], float(P) ** -0.5, None, ALU.mult).then_inc(p.own, 1)
                    v.wait_ge(*p.last())
                    v.wait_ge(*p.after("scalar", "gc_b"))
                    TT(bke, av[:, 1, :], egc[:, 1, hs], ALU.mult).then_inc(p.own, 1)
                    v.wait_ge(*p.last())
                    TT(wk, ss[:, 1, 0, :], wl[:, 0, hs], ALU.mult).then_inc(p.done("rn"), 1)
                    v.wait_ge(*p.here("rn"))

                def f3(x):
                    return x.rearrange("p a b c -> p (a b c)")

                def dec(g, r):
                    v.wait_ge(*p.after("tensor", "dec", g, r))
                    c = half("dec", g, r)
                    for j in range(4):
                        ins = TS(dt_[:, r, j, :], c[:, j * P:(j + 1) * P], gc[:, r, 4 * g + j:4 * g + j + 1], 0.0,
                                 ALU.subtract, ALU.min)
                    ins.then_inc(p.done("dec"), 1)

                def dec_c(g, r):
                    v.wait_ge(*p.after("scalar", "dec_b", g, r))
                    for j in range(4):
                        ins = STT(dt_[:, r, j, :], dt_[:, r, j, :], ss[:, 1, r, j:j + 1], triu, ALU.mult, ALU.mult)
                    ins.then_inc(p.own, 1)
                    v.wait_ge(*p.last())
                    TT(yy[:, r, :, :], dt_[:, r, :, :], heads(half("dec", g, r)[:, 512:1024]), ALU.mult).then_inc(
                            p.done("dec_c"), 1)
                    v.wait_ge(*p.here("dec_c"))

                def kk(g, r):
                    v.wait_ge(*p.after("tensor", "kk", g, r))
                    TT(lt[:, r, :, :], yy[:, r, :, :], heads(half("kk", g, r)[:, 0:512]), ALU.mult).then_inc(p.own, 1)
                    v.wait_ge(*p.last())
                    TT(xt[:, r, :, :], lt[:, r, :, :], over(cst[:, K_PAIR:K_PAIR + P], 4), ALU.mult).then_inc(p.own, 1)
                    v.wait_ge(*p.last())
                    TT(xt[:, r, :, :], over(ident, 4), xt[:, r, :, :], ALU.subtract).then_inc(p.done("kk"), 1)
                    v.wait_ge(*p.here("kk"))

                def kT(g):
                    v.wait_ge(*p.after("tensor", "kT", g))
                    TT(kd[:, :, :], heads(half("kT", g)[:, 0:512]), bc(wk, P), ALU.mult).then_inc(p.done("kT"), 1)
                    v.wait_ge(*p.here("kT"))

                def vT(g):
                    v.wait_ge(*p.after("tensor", "vT", g))
                    for r in range(R):
                        ins = TT(vb[:, r, :, :], heads(half("vT", g)[:, r * 512:(r + 1) * 512]),
                                 bc(be[:, r, 4 * g:4 * g + 4], P), ALU.mult)
                    ins.then_inc(p.done("vT"), 1)
                    v.wait_ge(*p.here("vT"))

                def invY(g, r, n):
                    v.wait_ge(*p.after("tensor", "invY", g, r, n))
                    m = cst[:, K_LEVEL + n * P:K_LEVEL + (n + 1) * P]
                    TT(yy[:, r, :, :], heads(half("invY", g, r, n)[:, 0:512]), over(m, 4), ALU.mult).then_inc(
                            p.done("invY"), 1)
                    v.wait_ge(*p.here("invY"))

                def invZ(g, r, n):
                    v.wait_ge(*p.after("tensor", "invZ", g, r, n))
                    c = half("invZ", g, r, n)
                    if n < len(LEVELS) - 1:
                        TT(xx[:, r, :, :], xx[:, r, :, :], heads(c[:, 0:512]), ALU.subtract).then_inc(p.own, 1)
                        v.wait_ge(*p.last())
                    TT(xt[:, r, :, :], xt[:, r, :, :], heads(c[:, 512:1024]), ALU.subtract).then_inc(p.done("invZ"), 1)
                    v.wait_ge(*p.here("invZ"))

                def kq(g, r):
                    v.wait_ge(*p.after("tensor", "kq", g, r))
                    TT(lt[:, r, :, :], dt_[:, r, :, :], heads(half("kq", g, r)[:, 0:512]), ALU.mult).then_inc(
                            p.done("kq"), 1)
                    v.wait_ge(*p.here("kq"))

                def ks(g):
                    v.wait_ge(*p.after("tensor", "ks", g))
                    TT(yy[:, 0, :, :], heads(half("ks", g)[:, 0:512]), bc(bke, P), ALU.mult).then_inc(p.own, 1)
                    v.wait_ge(*p.last())
                    TT(vb[:, 1, :, :], vb[:, 1, :, :], yy[:, 0, :, :], ALU.subtract).then_inc(p.done("ks"), 1)
                    v.wait_ge(*p.here("ks"))

                def o_(g, r):
                    v.wait_ge(*p.after("tensor", "o", g, r))
                    c = half("o", g, r)
                    dst = heads(od[:, r, g * 512:(g + 1) * 512])
                    hs = slice(4 * g, 4 * g + 4)
                    if r == 0:
                        TT(dst, heads(c[:, 0:512]), bc(ss[:, 0, 0, :], P), ALU.mult).then_inc(p.done("o"), 1)
                        v.wait_ge(*p.here("o"))
                        return None
                    TT(dst, heads(c[:, 512:1024]), bc(egc[:, 1, hs], P), ALU.mult).then_inc(p.own, 1)
                    v.wait_ge(*p.last())
                    TT(dst, dst, heads(c[:, 0:512]), ALU.add).then_inc(p.own, 1)
                    v.wait_ge(*p.last())
                    TT(dst, dst, bc(ss[:, 0, 1, :], P), ALU.mult).then_inc(p.done("o"), 1)
                    v.wait_ge(*p.here("o"))

                def onorm_a():
                    for r in range(R):
                        TT(od_sq, od[:, r, :], od[:, r, :], ALU.mult).then_inc(p.own, 1)
                        v.wait_ge(*p.last())
                        v.tensor_reduce(so[:, 2, r, :], heads(od_sq, 8), AX, ALU.add).then_inc(p.own, 1)
                        v.wait_ge(*p.last())
                    TS(so[:, 0, :, :], so[:, 2, :, :], 1.0 / P, EPS, ALU.mult, ALU.add).then_inc(p.done("onorm_a"), 1)
                    v.wait_ge(*p.here("onorm_a"))

                def onorm():
                    v.wait_ge(*p.after("scalar", "onorm"))
                    newton(so[:, 1, :, :], so[:, 0, :, :], so[:, 2, :, :])
                    for r in range(R):
                        o8 = heads(od[:, r, :], 8)
                        TT(o8, o8, bc(so[:, 1, r, :], P), ALU.mult).then_inc(p.own, 1)
                        v.wait_ge(*p.last())
                        ins = TT(o8, o8, over(gdn_gain, 8), ALU.mult)
                        if r == 0:
                            ins.then_inc(p.own, 1)
                            v.wait_ge(*p.last())
                    ins.then_inc(p.done("onorm_c"), 1)
                    v.wait_ge(*p.here("onorm_c"))

                def kinorm_a():
                    v.wait_ge(*p.after("scalar", "drain_s", "qi"))
                    for r in range(R):
                        ins = v.tensor_tensor_reduce(kk2[:, r, 0, :], pi[:, r, 512:576], pi[:, r, 512:576], 1.0, 0.0,
                                                     ALU.mult, ALU.add, kn[:, 2, r:r + 1])
                    ins.then_inc(p.own, 1)
                    v.wait_ge(*p.last())
                    TS(kn[:, 0, :], kn[:, 2, :], 1.0 / 64, EPS, ALU.mult, ALU.add).then_inc(p.done("kinorm_a"), 1)

                def rope(x, cos, sin, into=rope_tmp):
                    _, nr, nh, two = x.shape
                    hf = two // 2
                    a, b = x[:, :, :, 0:hf], x[:, :, :, hf:two]

                    def tmp(i):
                        return into[:, i, 0:nr * nh * hf].rearrange("p (r h n) -> p r h n", r=nr, h=nh)

                    def tab(x_):
                        return x_.unsqueeze(2).broadcast_to([P, nr, nh, hf])
                    for i, (m, n) in enumerate(((a, cos), (b, sin), (b, cos), (a, sin))):
                        ins = TT(tmp(i), m, tab(n), ALU.mult)
                    ins.then_inc(p.own, 1)
                    v.wait_ge(*p.last())
                    TT(a, tmp(0), tmp(1), ALU.subtract)
                    return TT(b, tmp(2), tmp(3), ALU.add)

                def rope_i():
                    v.wait_ge(*p.after("scalar", "kinorm"))
                    newton(kn[:, 1, :], kn[:, 0, :], kn[:, 3, :])
                    for r in range(R):
                        ins = STT(pi[:, r, 512:576], pi[:, r, 512:576], kn[:, 1, r:r + 1], idx_gain, ALU.mult, ALU.mult)
                    ins.then_inc(p.own, 1)
                    v.wait_ge(*p.last())
                    x = pi[:, :, 0:576].rearrange("p r (h n) -> p r h n", h=9)[:, :, :, 0:16]
                    rope(x, cos_t[:, :, 16:24], sin_t[:, :, 16:24]).then_inc(p.own, 1)
                    v.wait_ge(*p.last())
                    TS(wi[:, :, :], pi[:, :, 576:584], 8 ** -0.5 * 64 ** -0.5, None, ALU.mult)
                    v.sem_clear(topk_step)
                    for c in range(2):
                        ins = v.tensor_copy(kk2[:, :, c, :], pi[:, :, 512:576])
                    ins.then_inc(p.done("rope_i"), 1)
                    v.wait_ge(*p.here("rope_i"))

                def raw_(qb, part):
                    v.wait_ge(*p.after("scalar", "raw", qb, part))
                    nk = P * (qb + 1)
                    per = 1024 // nk
                    for i in range(per):
                        h = part * per + bank_order(i, per)
                        x = rl[:, i * nk:(i + 1) * nk]
                        if h == 0:
                            ins = TS(isc[qb], x, wi[:, qb, 0:1], None, ALU.mult)
                        else:
                            ins = STT(isc[qb], x, wi[:, qb, h:h + 1], isc[qb], ALU.mult, ALU.add)
                        if i < per - 1:
                            ins.then_inc(p.own, 1)
                            v.wait_ge(*p.last())
                    ins.then_inc(p.done("raw"), 1)
                    v.wait_ge(*p.here("raw"))

                def topk(qb):
                    nk = P * (qb + 1)
                    neg = cst[:, K_NEG + P - P * qb:K_NEG + 2 * P]
                    n = qb * (1 + TOPK // 4)
                    TT(isc[qb], isc[qb], neg, ALU.add).then_inc(topk_step, 1)
                    for _ in range(TOPK // 8):
                        v.wait_ge(topk_step, n + 1)
                        v.max(top, isc[qb]).then_inc(topk_step, 1)
                        v.wait_ge(topk_step, n + 2)
                        v.match_replace(isc[qb], top, isc[qb], TAKEN).then_inc(topk_step, 1)
                        n += 2
                    v.wait_ge(topk_step, n + 1)
                    TS(mb[qb], isc[qb], TAKEN, NEG, ALU.not_equal, ALU.mult).then_inc(p.own, 1)
                    v.wait_ge(*p.last())
                    TT(mb[qb], mb[qb], neg, ALU.add).then_inc(p.done("topk"), 1)
                    v.wait_ge(*p.here("topk"))

                def rope_a():
                    for name in ("kv", "qa0", "qa1"):
                        v.wait_ge(*p.after("scalar", "drain_s", name))
                    x = pq[:, :, 0:1280].rearrange("p r (h n) -> p r h n", h=10)[:, :, :, 0:32]
                    rope(x, cos_t[:, :, 0:16], sin_t[:, :, 0:16]).then_inc(p.done("rope_a"), 1)
                    v.wait_ge(*p.here("rope_a"))

                def sc(kv, qb):
                    v.wait_ge(*p.after("tensor", "sc", kv, qb))
                    if kv:
                        v.wait_ge(*p.after("tensor", "pT", 0, qb))
                    nk = P * (qb + 1)
                    x = heads(pr[qb][:, 0:4 * nk])
                    STT(x, heads(half("sc", kv, qb)[:, 0:4 * nk]), float(P) ** -0.5, over(mb[qb], 4),
                               ALU.mult, ALU.add).then_inc(p.own, 1)
                    v.wait_ge(*p.last())
                    v.tensor_reduce(mx[qb], x, AX, ALU.max).then_inc(p.own, 1)
                    v.wait_ge(*p.last())
                    TS(mx[qb], mx[qb], -1.0, None, ALU.mult).then_inc(p.done("sc"), 1)
                    v.wait_ge(*p.here("sc"))

                def pv(kv, qb):
                    v.wait_ge(*p.after("tensor", "pv", kv, qb))
                    v.wait_ge(*p.after("scalar", "sc", kv, qb))
                    v.reciprocal(rs[qb], rs[qb]).then_inc(p.own, 1)
                    v.wait_ge(*p.last())
                    dst = heads(pq[:, qb, kv * 512:(kv + 1) * 512])
                    TT(dst, heads(half("pv", kv, qb)[:, 0:512]), bc(rs[qb], P), ALU.mult).then_inc(p.done("pv"), 1)
                    v.wait_ge(*p.here("pv"))

                def mix_b(r):
                    TT(g1[:, r, :], g1[:, r, :], od[:, r, :], ALU.mult).then_inc(p.done("mix_b"), 1)
                    v.wait_ge(*p.here("mix_b"))

                def mix(r):
                    TT(g0[:, r, :], g0[:, r, :], pq[:, r, 0:D], ALU.mult).then_inc(p.own, 1)
                    v.wait_ge(*p.last())
                    TT(g0[:, r, :], g0[:, r, :], g1[:, r, :], ALU.add).then_inc(p.done("mix"), 1)
                    v.wait_ge(*p.here("mix"))

                def mT(r):
                    v.wait_ge(*p.after("scalar", "mT", r))
                    low_T(half("mT", r), r).then_inc(p.done("mT"), 1)

                def params2():
                    v.tensor_copy(now2[:, :], par2[:, bass.ds(p.l, 1), :].rearrange("p a n -> p (a n)")).then_inc(
                            p.own, 1)
                    v.wait_ge(*p.last())
                    v.tensor_copy(gain2[:, :], mkv[:, bass.ds(p.l, 1), :, :].rearrange("p a r n -> p (a r n)")).then_inc(
                            p.done("params2"), 1)
                    v.wait_ge(*p.here("params2"))

                def xT(r):
                    v.wait_ge(*p.after("scalar", "xT", r))
                    low_T(half("xT", r), r).then_inc(p.done("xT"), 1)

                def lat_a():
                    v.wait_ge(*p.after("scalar", "drain_s", "h1"))
                    for i, (c, n) in enumerate(((0, 384), (384, 256))):
                        for r in range(R):
                            ins = v.tensor_tensor_reduce(reg_a[:, (2 * i + r) * 512:(2 * i + r) * 512 + n],
                                                         h2[:, r, c:c + n], h2[:, r, c:c + n],
                                                         1.0, 0.0, ALU.mult, ALU.add, lat[:, 2, i, r:r + 1])
                    ins.then_inc(p.own, 1)
                    v.wait_ge(*p.last())
                    TS(lat[:, 0, 0, :], lat[:, 2, 0, :], 1.0 / 384, EPS, ALU.mult, ALU.add)
                    TS(lat[:, 0, 1, :], lat[:, 2, 1, :], 1.0 / 256, EPS, ALU.mult, ALU.add).then_inc(p.done("lat_a"), 1)

                def lat_c():
                    v.wait_ge(*p.after("scalar", "lat"))
                    newton(lat[:, 1, :, :], lat[:, 0, :, :], lat[:, 3, :, :])
                    for i, (c, n, gn) in enumerate(((0, 384, q_gain), (384, 256, kv_gain))):
                        for r in range(R):
                            ins = STT(h2[:, r, c:c + n], h2[:, r, c:c + n], lat[:, 1, i, r:r + 1], gn, ALU.mult, ALU.mult)
                    ins.then_inc(p.done("lat_c"), 1)
                    v.wait_ge(*p.here("lat_c"))

                def ckT(r):
                    v.wait_ge(*p.after("tensor", "ckT", r))
                    split_T(half("ckT", r), r, sT_hi, sT_lo, 0, 5).then_inc(p.done("ckT"), 1)

                def sbz(k):
                    v.wait_ge(*p.after("tensor", "sbz", k))
                    n = S - k * P
                    z, a = heads(pr2[1 - k]), heads(pt2[1 - k])
                    STT(z, places(half("sbz", k)[:, :], n), 64 ** -0.5, over(cst[:, K_NSTR:K_NSTR + n], 4),
                               ALU.mult, ALU.add).then_inc(p.own, 1)
                    v.wait_ge(*p.last())
                    STT(a, z, -1.0, z, ALU.mult, ALU.max).then_inc(p.done("sbz"), 1)

                def sbm(k):
                    v.wait_ge(*p.after("scalar", "sbl", k))
                    STT(pt2[1 - k], pr2[1 - k], 0.0, pt2[1 - k], ALU.max, ALU.add).then_inc(p.done("sbm"), 1)
                    v.wait_ge(*p.here("sbm"))

                def sbi(k):
                    v.wait_ge(*p.after("tensor", "sbi", k))
                    n = 4 * (S - k * P)
                    TT(pr2[1 - k], pr2[1 - k], half("sbi", k)[:, 0:n], ALU.subtract).then_inc(p.done("sbi"), 1)
                    v.wait_ge(*p.here("sbi"))

                def sbo(qb):
                    v.wait_ge(*p.after("tensor", "sbo", qb))
                    v.tensor_copy(branch_y(1, qb), half("sbo", qb)[:, 0:S]).then_inc(p.done("sbo"), 1)
                    v.wait_ge(*p.here("sbo"))

                def ff_a():
                    v.wait_ge(*p.after("scalar", "drain_s", "h4"))
                    y = fy[:, 0, :, :]
                    TT(y, h2[:, :, B_FF:B_FF + 4], over(fox_bias, R), ALU.add).then_inc(p.own, 1)
                    v.wait_ge(*p.last())
                    STT(fy[:, 1, :, :], y, -1.0, y, ALU.mult, ALU.max).then_inc(p.done("ff_a"), 1)

                def ff_c():
                    v.wait_ge(*p.after("scalar", "ff"))
                    TS(fy[:, 0, :, :], fy[:, 0, :, :], 0.0, None, ALU.min).then_inc(p.own, 1)
                    v.wait_ge(*p.last())
                    TT(fy[:, 2, :, :], fy[:, 0, :, :], fy[:, 1, :, :], ALU.subtract).then_inc(p.done("ff_c"), 1)
                    v.wait_ge(*p.here("ff_c"))

                def fc():
                    v.wait_ge(*p.after("tensor", "fc"))
                    v.tensor_copy(cf[:, :, :].rearrange("p r n -> p (r n)"), half("fc")[:, 0:8]).then_inc(
                            p.done("fc"), 1)
                    v.wait_ge(*p.here("fc"))

                def fb():
                    v.wait_ge(*p.after("tensor", "fb"))
                    v.wait_ge(*p.after("tensor", "sbi", 1))
                    c = half("fb")
                    for qb in range(2):
                        nk = P * (qb + 1)
                        for q in range(4):
                            h = head_of(FOX, q)
                            ins = STT(pt2[qb][:, q * nk:(q + 1) * nk], c[:, q * S:q * S + nk], cf[:, qb, h:h + 1],
                                      cst[:, K_NEG + P - P * qb:K_NEG + 2 * P], ALU.subtract, ALU.subtract)
                    ins.then_inc(p.done("fb"), 1)
                    v.wait_ge(*p.here("fb"))

                def sc2(n, qb):
                    v.wait_ge(*p.after("tensor", "sc2", n, qb))
                    nk, b = keys_of(n, qb), buf_of(n, qb)
                    prev = user_before(n, qb)
                    if prev:
                        v.wait_ge(*p.after("tensor", "p2T", *prev))
                    x, src = heads(pr2[b][:, 0:4 * nk]), places(half("sc2", n, qb)[:, :], nk)
                    scale = (96 if n == MLA else 64) ** -0.5
                    if n == MLA:
                        neg = cst[:, K_NEG + P - P * qb:K_NEG + 2 * P]
                        ins = STT(x, src, scale, over(neg, 4), ALU.mult, ALU.add)
                    elif n == FOX:
                        ins = STT(x, src, scale, heads(pt2[b][:, 0:4 * nk]), ALU.mult, ALU.subtract)
                    else:
                        ins = TS(x, src, scale, None, ALU.mult)
                    ins.then_inc(p.own, 1)
                    v.wait_ge(*p.last())
                    v.tensor_reduce(mx2[qb], x, AX, ALU.max).then_inc(p.own, 1)
                    v.wait_ge(*p.last())
                    TS(mx2[qb], mx2[qb], -1.0, None, ALU.mult).then_inc(p.done("sc2"), 1)
                    v.wait_ge(*p.here("sc2"))

                def pv2(n, qb):
                    v.wait_ge(*p.after("tensor", "pv2", n, qb))
                    b = buf_of(n, qb)
                    v.reciprocal(rs2[qb], rs2[qb]).then_inc(p.own, 1)
                    v.wait_ge(*p.last())
                    TT(heads(branch_y(n, qb)), heads(half("pv2", n, qb)[:, 0:S]), bc(rs2[qb], 64), ALU.mult).then_inc(
                            p.done("pv2"), 1)
                    v.wait_ge(*p.here("pv2"))

                def rope_2():
                    v.wait_ge(*p.after("scalar", "drain_s", "kvb"))
                    def parts(x, nh, w, c):
                        return x.rearrange("p r (h n) -> p r h n", h=nh)[:, :, :, c:c + 32]
                    cos, sin = cos_t[:, :, 24:40], sin_t[:, :, 24:40]
                    rope(parts(q2[:, :, :], 4, 96, 64), cos, sin, tmp2).then_inc(p.own, 1)
                    v.wait_ge(*p.last())
                    rope(parts(h2[:, :, B_KR:B_KR + 32], 1, 32, 0), cos, sin, tmp2).then_inc(p.own, 1)
                    v.wait_ge(*p.last())
                    kh = kc[:, :, :].rearrange("p r (h n) -> p r h n", h=4)
                    v.tensor_copy(kh[:, :, :, 0:64], kv2[:, :, :].rearrange("p r (h n) -> p r h n", h=4)[:, :, :, 0:64])
                    v.tensor_copy(kh[:, :, :, 64:96],
                                             h2[:, :, B_KR:B_KR + 32].unsqueeze(2).broadcast_to([P, R, 4, 32])).then_inc(
                                                     p.done("rope_2"), 1)
                    v.wait_ge(*p.here("rope_2"))

                def gy(n):
                    v.wait_ge(*p.after("scalar", "drain_s", "gz1"))
                    gz = h2[:, :, B_GATE + n * S:B_GATE + (n + 1) * S]
                    y = q2[:, :, 0:S] if n == MLA else h2[:, :, Q_OF[n]:Q_OF[n] + S]
                    TT(gz, gz, y, ALU.mult).then_inc(p.done("gy"), 1)
                    v.wait_ge(*p.here("gy"))

                def yT(n):
                    v.wait_ge(*p.after("tensor", "mm", max(u for u, x in enumerate(UNITS["two"]) if x[0] == "gz1")))
                    v.wait_ge(*p.after("tensor", "yT", n))
                    src = half("yT", n)[:, 0:512].rearrange("p (r k n) -> p k r n", r=R, k=2)
                    hi = hT_hi[:, 2 * n:2 * n + 2, :].rearrange("p k (r n) -> p k r n", r=R)
                    lo = hT_lo[:, 2 * n:2 * n + 2, :].rearrange("p k (r n) -> p k r n", r=R)
                    v.tensor_copy(hi, src).then_inc(p.own, 1)
                    v.wait_ge(*p.last())
                    TT(lo, src, hi.bitcast(F32), ALU.subtract).then_inc(p.done("yT"), 1)

                def gT(r):
                    v.wait_ge(*p.after("scalar", "gT", r))
                    low_T(half("gT", r), r).then_inc(p.done("gT"), 1)

                def ln_a():
                    x, m = xs[:, 0, :], lnm[:, 0, 0:1]
                    v.tensor_reduce(m, x, AX, ALU.add).then_inc(p.own, 1)
                    v.wait_ge(*p.last())
                    TS(m, m, -1.0 / D, None, ALU.mult).then_inc(p.own, 1)
                    v.wait_ge(*p.last())
                    TS(x, x, m, None, ALU.add).then_inc(p.own, 1)
                    v.wait_ge(*p.last())
                    v.tensor_tensor_reduce(h2[:, 0, 0:D], x, x, 1.0, 0.0,
                                           ALU.mult, ALU.add, lnm[:, 1, 0:1]).then_inc(p.own, 1)
                    v.wait_ge(*p.last())
                    v.wait_ge(*p.after("scalar", "ln_a"))
                    TS(lnm[:, 2, :], lnm[:, 1, :], 1.0 / D, LN_EPS, ALU.mult, ALU.add).then_inc(p.done("ln_a"), 1)

                def ln():
                    v.wait_ge(*p.after("scalar", "ln_s"))
                    newton(lnm[:, 3, :], lnm[:, 2, :], lnm[:, 4, :])
                    v.wait_ge(ln_in, 32 * (p.l + 1))
                    for r in range(R):
                        STT(xs[:, r, :], xs[:, r, :], lnm[:, 3, r:r + 1], gain[:, :], ALU.mult, ALU.mult).then_inc(
                                p.own, 1)
                        v.wait_ge(*p.last())
                        ins = TT(xs[:, r, :], xs[:, r, :], gain2[:, :], ALU.add)
                        if r == 0:
                            ins.then_inc(p.own, 1)
                            v.wait_ge(*p.last())
                    ins.then_inc(p.done("ln"), 1)
                    v.wait_ge(*p.here("ln"))

                return dict(params2=params2, xT=xT, lat_a=lat_a, lat_c=lat_c, ckT=ckT, baT=baT, kxT=kxT, sbz=sbz, sbm=sbm,
                            sbi=sbi, sbo=sbo, ff_a=ff_a, ff_c=ff_c, fc=fc, fb=fb, sc2=sc2, pv2=pv2, rope_2=rope_2,
                            gy=gy, yT=yT, gT=gT, ln_a=ln_a, ln=ln,
                            memT=memT, tables_a=tables_a, tables_c=tables_c, cwT=cwT, params=params, norm_a=norm_a,
                            norm_c=norm_c, hT=hT, drain_v=drain, gmul=gmul, tap=tap, ba_a=ba_a, ba_c=ba_c, gc=gc_, stat=stat, rn=rn,
                            dec=dec, dec_c=dec_c, kk=kk, kT=kT, vT=vT, invY=invY, invZ=invZ, kq=kq, ks=ks, o=o_,
                            onorm_a=onorm_a, onorm_c=onorm, kinorm_a=kinorm_a, rope_i=rope_i, raw=raw_, topk=topk,
                            rope_a=rope_a, sc=sc, pv=pv, mix=mix, mix_b=mix_b, mT=mT)

            run(v, "vector", handlers)


WEIGHTS = {"w_in": "w_in", "w_out": "w_out", "w_in_2": "w_in_2", "mla_w_qb_2": "mla_w_qb", "mla_w_kvb_2": "mla_w_kvb",
           "w_mem_kv_2": "w_mem_kv", "w_merge_up_2": "w_merge_up", "w_branch_2": "w_branch", "w_out_2": "w_out_2"}
PLAIN = ["x", "positions", "conv_w", "a_log", "dt_bias", "gdn_norm_gain", "idx_k_gain", "mem_2", "positions_2",
         "mla_q_norm_2", "mla_kv_norm_2", "fox_forget_bias_2"]


def kernel(**inputs):
    import concourse.bacc as bacc
    from concourse.bass_utils import run_bass_kernel_spmd

    arrays = laid_out(inputs)
    nc = bacc.Bacc("TRN2", target_bir_lowering=False, num_devices=1, dynamic_dma_scratch_size=8192)
    t = {name: nc.dram_tensor(f"in_{name}_dram", a.shape, mybir.dt.from_np(a.dtype), kind="ExternalInput").ap()
         for name, a in arrays.items()}
    out = nc.dram_tensor("out_0_dram", (1, S, D), F32, kind="ExternalOutput").ap()
    build(nc, t, out)
    r = run_bass_kernel_spmd(nc, [{f"in_{k}_dram": a for k, a in arrays.items()}], core_ids=[0])
    return r.results[0]["out_0_dram"]


def laid_out(inputs):
    arrays = {name: np.ascontiguousarray(inputs[name]) for name in PLAIN}
    for name, short in WEIGHTS.items():
        arrays[short] = np.ascontiguousarray(inputs[name])
    arrays["gains"] = np.concatenate([np.asarray(inputs["norm_gain"]), np.asarray(inputs["final_gain"])[None]])
    arrays["ln_rows"] = np.concatenate([np.stack([np.asarray(inputs["ln_gain_2"])[l], np.asarray(inputs["ln_bias_2"])[l]])
                                        for l in range(DEPTH)])
    arrays["shape_constants"] = shape_constants()
    return arrays
```
